# Optimizing a Trainium2 kernel written in Bass

```python
import math
import jax, jax.numpy as jnp
from jax import lax
import numpy as np

D_MODEL = 1024
BATCH = 1
SEQ = 256
DEPTH = 2

CHUNK = 64
N_MIXERS = 2
DA_HEADS = 8
DA_HEAD_DIM = 64
DA_V_DIM = 2 * DA_HEAD_DIM
DA_PROJ = 3 * DA_HEADS * 2 * DA_HEAD_DIM
Q_BLOCK = 128
GLA_HEADS = 4
GLA_KEY_WIDTH = D_MODEL // 2
GLA_VAL_WIDTH = D_MODEL
GLA_DK = GLA_KEY_WIDTH // GLA_HEADS
GLA_DV = GLA_VAL_WIDTH // GLA_HEADS
GLA_PROJ = 2 * GLA_KEY_WIDTH + 2 * GLA_VAL_WIDTH
GLA_GATE_RANK = 16
GLA_TAU = 16.0
FFN_DIM = 2816
N_EXPERTS = 8
TOP_K = 2
EXPERT_DIM = 3584
EXPERT_BLOCK = 256
NORM_EPS = 1e-6

kernel_name = "hybrid_diffattn_gla_moe_adaln_encoder"

def rms_norm(x, g):
    xf = x.astype(jnp.float32)
    y = xf * lax.rsqrt(jnp.mean(xf * xf, axis=-1, keepdims=True) + NORM_EPS)
    return (y * g.astype(jnp.float32)).astype(x.dtype)

def alibi_slopes(n_heads):
    return 2.0 ** (-8.0 * jnp.arange(1, n_heads + 1, dtype=jnp.float32) / n_heads)

def swiglu(x, w1, w3, w2):
    return (jax.nn.silu(x @ w1) * (x @ w3)) @ w2

def diff_attention(h, w_in, q_gain, k_gain, lam_q1, lam_k1, lam_q2, lam_k2, subln_g, w_out, lambda_init):
    B, S, _ = h.shape
    H, Dh = DA_HEADS, DA_HEAD_DIM
    q, k, v = jnp.split(h @ w_in, 3, axis=-1)
    q = rms_norm(q.reshape(B, S, H, 2, Dh), q_gain)
    k = rms_norm(k.reshape(B, S, H, 2, Dh), k_gain)
    v = v.reshape(B, S, H, DA_V_DIM)
    f32 = jnp.float32
    lam = (jnp.exp(jnp.sum(lam_q1.astype(f32) * lam_k1.astype(f32)))
           - jnp.exp(jnp.sum(lam_q2.astype(f32) * lam_k2.astype(f32))) + lambda_init)
    slopes = alibi_slopes(H)
    key_pos = jnp.arange(S, dtype=jnp.int32)
    n_qb = S // Q_BLOCK
    q_blocks = jnp.moveaxis(q.reshape(B, n_qb, Q_BLOCK, H, 2, Dh), 1, 0)
    scale = Dh ** -0.5

    def attend_block(args):
        q_blk, start = args
        q_pos = start + jnp.arange(Q_BLOCK, dtype=jnp.int32)
        visible = (key_pos // CHUNK)[None, :] <= (q_pos // CHUNK)[:, None]
        dist = jnp.abs(q_pos[:, None] - key_pos[None, :]).astype(f32)
        bias = -slopes[:, None, None] * dist
        scores = jnp.einsum('bqhmd,bshmd->bhmqs', q_blk, k).astype(f32) * scale + bias[None, :, None]
        scores = jnp.where(visible, scores, -jnp.inf)
        p = jax.nn.softmax(scores, axis=-1)
        p_diff = (p[:, :, 0] - lam * p[:, :, 1]).astype(v.dtype)
        return jnp.einsum('bhqs,bshe->bqhe', p_diff, v)

    starts = jnp.arange(n_qb, dtype=jnp.int32) * Q_BLOCK
    o = lax.map(attend_block, (q_blocks, starts))
    o = jnp.moveaxis(o, 0, 1).reshape(B, S, H, DA_V_DIM)
    o = rms_norm(o, subln_g) * (1.0 - lambda_init)
    return o.reshape(B, S, H * DA_V_DIM) @ w_out

def gla_mixer(h, w_in, w_a1, w_a2, b_a, out_g, w_out):
    B, S, _ = h.shape
    H, dk, dv = GLA_HEADS, GLA_DK, GLA_DV
    n = S // CHUNK
    f32 = jnp.float32
    q, k, v, r = jnp.split(h @ w_in, [GLA_KEY_WIDTH, 2 * GLA_KEY_WIDTH, 2 * GLA_KEY_WIDTH + GLA_VAL_WIDTH], axis=-1)
    log_a = jax.nn.log_sigmoid(((h @ w_a1) @ w_a2 + b_a).astype(f32)) / GLA_TAU

    def chunked(t, d):
        return t.astype(f32).reshape(B, n, CHUNK, H, d)

    q = chunked(q, dk) * dk ** -0.5
    k = chunked(k, dk)
    v = chunked(v, dv)
    b = jnp.cumsum(chunked(log_a, dk), axis=2)
    b_last = b[:, :, -1]
    q_dec = q * jnp.exp(b)
    k_inv = k * jnp.exp(-b)
    k_dec = k * jnp.exp(b_last[:, :, None] - b)
    causal = jnp.tril(jnp.ones((CHUNK, CHUNK), dtype=bool))
    attn = jnp.where(causal, jnp.einsum('bnthk,bnshk->bnhts', q_dec, k_inv), 0.0)
    o_intra = jnp.einsum('bnhts,bnshv->bnthv', attn, v)

    def step(state, xs):
        q_c, k_c, v_c, decay = xs
        o_c = jnp.einsum('bthk,bhkv->bthv', q_c, state)
        state = decay[..., None] * state + jnp.einsum('bshk,bshv->bhkv', k_c, v_c)
        return state, o_c

    xs = (jnp.moveaxis(q_dec, 1, 0), jnp.moveaxis(k_dec, 1, 0), jnp.moveaxis(v, 1, 0),
          jnp.moveaxis(jnp.exp(b_last), 1, 0))
    _, o_inter = lax.scan(step, jnp.zeros((B, H, dk, dv), f32), xs)
    o = o_intra + jnp.moveaxis(o_inter, 0, 1)
    o = rms_norm(o.reshape(B, S, H, dv), out_g).astype(h.dtype)
    o = o * jax.nn.silu(r).reshape(B, S, H, dv)
    return o.reshape(B, S, GLA_VAL_WIDTH) @ w_out

def moe_swiglu(h, router_w, w1, w3, w2):
    B, S, D = h.shape
    N = B * S
    A = N * TOP_K
    xf = h.reshape(N, D)
    logits = (xf @ router_w).astype(jnp.float32)
    top_val, top_idx = lax.top_k(logits, TOP_K)
    gates = jax.nn.softmax(top_val, axis=-1)
    e_flat = top_idx.reshape(A).astype(jnp.int32)
    tok_flat = jnp.repeat(jnp.arange(N, dtype=jnp.int32), TOP_K)
    g_flat = gates.reshape(A)
    e_s, tok_s, g_s = lax.sort((e_flat, tok_flat, g_flat), num_keys=1)
    counts = jax.ops.segment_sum(jnp.ones((A,), jnp.int32), e_flat, num_segments=N_EXPERTS)
    padded = (counts + EXPERT_BLOCK - 1) // EXPERT_BLOCK * EXPERT_BLOCK
    pend = jnp.cumsum(padded)
    pstart = pend - padded
    ustart = jnp.cumsum(counts) - counts
    dest = pstart[e_s] + (jnp.arange(A, dtype=jnp.int32) - ustart[e_s])
    P = A + N_EXPERTS * EXPERT_BLOCK
    buf_tok = jnp.full((P,), N, jnp.int32).at[dest].set(tok_s)
    buf_g = jnp.zeros((P,), jnp.float32).at[dest].set(g_s)
    n_blocks = P // EXPERT_BLOCK
    block_starts = jnp.arange(n_blocks, dtype=jnp.int32) * EXPERT_BLOCK
    block_exp = jnp.clip(jnp.searchsorted(pend, block_starts, side='right'), 0, N_EXPERTS - 1)
    x_pad = jnp.concatenate([xf, jnp.zeros((1, D), xf.dtype)], axis=0)

    def expert_block(args):
        tok_b, e = args
        return swiglu(x_pad[tok_b], w1[e], w3[e], w2[e])

    y = lax.map(expert_block, (buf_tok.reshape(n_blocks, EXPERT_BLOCK), block_exp))
    y = y.reshape(P, D) * buf_g[:, None].astype(y.dtype)
    out = jax.ops.segment_sum(y, buf_tok, num_segments=N + 1)[:N]
    return out.reshape(B, S, D)

def setup_inputs(seed: int = 0) -> dict:
    key = jax.random.key(seed)
    ks = iter(jax.random.split(key, 40))
    n_a = (DEPTH + 1) // 2
    n_b = DEPTH // 2
    D = D_MODEL

    def nrm(shape, scale):
        return jax.random.normal(next(ks), shape, jnp.float32) * scale

    def gain(shape):
        return 1.0 + nrm(shape, 0.05)

    return {
        "x": nrm((BATCH, SEQ, D), 1.0),
        "c": nrm((BATCH, D), 1.0),
        "ada_w": nrm((DEPTH, D, 6 * D), D ** -0.5),
        "ada_b": nrm((DEPTH, 6 * D), 0.02),
        "norm1_g": gain((DEPTH, D)),
        "norm2_g": gain((DEPTH, D)),
        "da_w_in": nrm((n_a, D, DA_PROJ), D ** -0.5),
        "da_q_gain": gain((n_a, 2, DA_HEAD_DIM)),
        "da_k_gain": gain((n_a, 2, DA_HEAD_DIM)),
        "da_lam_q1": nrm((n_a, DA_HEAD_DIM), 0.1),
        "da_lam_k1": nrm((n_a, DA_HEAD_DIM), 0.1),
        "da_lam_q2": nrm((n_a, DA_HEAD_DIM), 0.1),
        "da_lam_k2": nrm((n_a, DA_HEAD_DIM), 0.1),
        "da_subln_g": gain((n_a, DA_V_DIM)),
        "da_w_out": nrm((n_a, DA_HEADS * DA_V_DIM, D), (DA_HEADS * DA_V_DIM) ** -0.5),
        "gla_w_in": nrm((n_b, D, GLA_PROJ), D ** -0.5),
        "gla_w_a1": nrm((n_b, D, GLA_GATE_RANK), D ** -0.5),
        "gla_w_a2": nrm((n_b, GLA_GATE_RANK, GLA_KEY_WIDTH), GLA_GATE_RANK ** -0.5),
        "gla_b_a": nrm((n_b, GLA_KEY_WIDTH), 0.1),
        "gla_out_g": gain((n_b, GLA_DV)),
        "gla_w_out": nrm((n_b, GLA_VAL_WIDTH, D), GLA_VAL_WIDTH ** -0.5),
        "ffn_w1": nrm((n_a, D, FFN_DIM), D ** -0.5),
        "ffn_w3": nrm((n_a, D, FFN_DIM), D ** -0.5),
        "ffn_w2": nrm((n_a, FFN_DIM, D), FFN_DIM ** -0.5),
        "moe_router": nrm((n_b, D, N_EXPERTS), D ** -0.5),
        "moe_w1": nrm((n_b, N_EXPERTS, D, EXPERT_DIM), D ** -0.5),
        "moe_w3": nrm((n_b, N_EXPERTS, D, EXPERT_DIM), D ** -0.5),
        "moe_w2": nrm((n_b, N_EXPERTS, EXPERT_DIM, D), EXPERT_DIM ** -0.5),
    }

def reference(x, c, ada_w, ada_b, norm1_g, norm2_g,
              da_w_in, da_q_gain, da_k_gain, da_lam_q1, da_lam_k1, da_lam_q2, da_lam_k2, da_subln_g, da_w_out,
              gla_w_in, gla_w_a1, gla_w_a2, gla_b_a, gla_out_g, gla_w_out,
              ffn_w1, ffn_w3, ffn_w2,
              moe_router, moe_w1, moe_w3, moe_w2):
    c_act = jax.nn.silu(c)
    for i in range(DEPTH):
        j = i // N_MIXERS
        mod = c_act @ ada_w[i] + ada_b[i]
        shift1, scale1, gate1, shift2, scale2, gate2 = jnp.split(mod[:, None, :], 6, axis=-1)
        h = rms_norm(x, norm1_g[i]) * (1.0 + scale1) + shift1
        if i % N_MIXERS == 0:
            lambda_init = 0.8 - 0.6 * math.exp(-0.3 * i)
            y = diff_attention(h, da_w_in[j], da_q_gain[j], da_k_gain[j], da_lam_q1[j], da_lam_k1[j],
                               da_lam_q2[j], da_lam_k2[j], da_subln_g[j], da_w_out[j], lambda_init)
        else:
            y = gla_mixer(h, gla_w_in[j], gla_w_a1[j], gla_w_a2[j], gla_b_a[j], gla_out_g[j], gla_w_out[j])
        x = x + gate1 * y
        h = rms_norm(x, norm2_g[i]) * (1.0 + scale2) + shift2
        if i % 2 == 0:
            y = swiglu(h, ffn_w1[j], ffn_w3[j], ffn_w2[j])
        else:
            y = moe_swiglu(h, moe_router[j], moe_w1[j], moe_w3[j], moe_w2[j])
        x = x + gate2 * y
    return x


_drawn_inputs = setup_inputs


def setup_inputs(seed=0):
    import zlib

    import numpy as np

    out = dict(_drawn_inputs(seed))
    spreads = {}
    factors = {'da_k_gain': 3.006, 'da_lam_q1': 6.995, 'da_lam_k1': 8.0}
    for name, (base, spread) in spreads.items():
        noise = np.random.default_rng([zlib.crc32(name.encode()), seed]).standard_normal(out[name].shape)
        drawn = base * np.exp(spread * noise) if base else spread * noise
        out[name] = __import__('jax').numpy.asarray(drawn.astype(out[name].dtype))
    for name, factor in factors.items():
        out[name] = (out[name] * factor).astype(out[name].dtype)
    return out
```

```python
import math
from contextlib import ExitStack

import concourse.bass as bass
from concourse import mybir

ALU = mybir.AluOpType
ACT = mybir.ActivationFunctionType
AX_X = mybir.AxisListType.X
F32 = mybir.dt.float32
I32 = mybir.dt.int32

P = 128
D = 1024
S = 256
TT = S // P
KT = D // P
CHUNK = 64
EPS = 1e-6
H = 8
DH = 64
LAMBDA_INIT = 0.8 - 0.6 * math.exp(-0.3 * 0)
GH = 4
DV = D // GH
NC = S // CHUNK
GLA_RANK = 16
GLA_TAU = 16.0
FFN = 2816
FT = FFN // P
NE = 8
EF = 3584
FW = 512
FPC = FW // P
ECH = EF // FW
NCH = (FFN + FW - 1) // FW
HIDDEN = -1e30

SLOTS = 7
SLOT = KT * FW


def stream_before_experts():
    order = [("ada0", i) for i in range(4)] + [("in0", i) for i in range(6)]
    order += [("ada0", i) for i in (4, 5)] + [("out0", i) for i in range(2)]
    order += [("ada0", i) for i in range(6, 12)]
    for f in range(NCH):
        order += [("w1", f), ("w3", f), ("w2", f), ("ada1", 2 * f), ("ada1", 2 * f + 1)]
    order += [("in1", i) for i in range(6)] + [("out1", i) for i in range(2)]
    return order


def build(nc, t):
    order = stream_before_experts()
    index = {key: i for i, key in enumerate(order)}
    PRE = len(order)
    PER = 3 * ECH
    assert PER % SLOTS == 0
    proj_rank = {k: i + 1 for i, k in enumerate([k for k in order if k[0][:-1] in ("in", "out")])}
    ada_rank = {k: i + 1 for i, k in enumerate([k for k in order if k[0].startswith("ada")])}

    ROOT = {"norm0": 0, "qk": 1, "sub": 9, "norm1": 13, "norm2": 14, "gla": 15, "norm3": 19}

    with ExitStack() as ctx:
        def sb(name, shape, dt=F32):
            return ctx.enter_context(nc.sbuf_tensor(name, shape, dt))

        def sem(name):
            return ctx.enter_context(nc.semaphore(name))

        ring = sb("ring", [P, SLOTS, SLOT])
        ident = sb("ident", [P, P])
        ones = sb("ones", [P, P])
        halves = sb("halves", [P, P])
        tri = sb("tri", [P, P])
        before = sb("before", [P, P])
        dist = sb("dist", [P, S])
        slot_no = sb("slot_no", [P, S])
        lower_e = sb("lower_e", [P, NE, NE])
        NPAR = 8 + 16 + 16 + 96 + 5
        par = sb("par", [P, NPAR])
        C0, N1, N2, AB, QG = 0, 8, 24, 40, 136
        c_act = sb("c_act", [P, KT])
        lam = sb("lam", [P, 4])
        router = sb("router", [P, KT, NE])
        mod = sb("mod", [P, 2, 48])
        ada_acc = sb("ada_acc", [P, 2, 1024])
        cols = sb("cols", [P, 4, KT])
        eps = sb("eps", [P, 4])
        gq = sb("gq", [P, 8])
        xT = sb("xT", [P, KT, S])
        hT = sb("hT", [P, KT, S])
        sq = sb("sq", [P, KT, S])
        rstd = sb("rstd", [P, KT, S])
        bufA = sb("bufA", [P, KT, S])
        bufB = sb("bufB", [P, KT, S])
        V = sb("V", [P, TT, D])
        oT = sb("oT", [P, KT, S])
        work = sb("work", [P, 2, 2048])
        small = sb("small", [P, 2, 16])
        nbk = sb("nbk", [P, NE], I32)

        psum = [ctx.enter_context(nc.psum_tensor(f"bank{i}", [P, 512], F32)) for i in range(8)]

        s_small = sem("s_small")
        s_late = sem("s_late")
        landed = [sem(f"landed{i}") for i in range(SLOTS)]
        ada_used = sem("ada_used")
        s_const = sem("s_const")
        s_constv = sem("s_constv")
        s_tp = sem("s_tp")
        s_par = sem("s_par")
        s_cact = sem("s_cact")
        s_xt = sem("s_xt")
        s_x = sem("s_x")
        s_modp = sem("s_modp")
        s_mod = sem("s_mod")
        s_sq = sem("s_sq")
        s_ssq = sem("s_ssq")
        s_root = sem("s_root")
        s_hp = sem("s_hp")
        s_h = sem("s_h")
        s_fill = sem("s_fill")
        s_evac = sem("s_evac")
        s_qsq = sem("s_qsq")
        s_qss = sem("s_qss")
        s_qn = sem("s_qn")
        s_lam = sem("s_lam")
        s_lame = sem("s_lame")
        s_sc = sem("s_sc")
        s_mx = sem("s_mx")
        s_ex = sem("s_ex")
        s_pd = sem("s_pd")
        s_pt = sem("s_pt")
        s_pte = sem("s_pte")
        s_o = sem("s_o")
        s_oe = sem("s_oe")
        s_oss = sem("s_oss")
        s_on = sem("s_on")
        s_h13 = sem("s_h13")
        s_silu = sem("s_silu")
        s_hid = sem("s_hid")
        s_hidu = sem("s_hidu")
        s_a1 = sem("s_a1")
        s_a1e = sem("s_a1e")
        s_z = sem("s_z")
        s_zb = sem("s_zb")
        s_ln = sem("s_ln")
        s_la = sem("s_la")
        s_b = sem("s_b")
        s_be = sem("s_be")
        s_dd = sem("s_dd")
        s_ed = sem("s_ed")
        s_qd = sem("s_qd")
        s_kdt = sem("s_kdt")
        s_kde = sem("s_kde")
        s_am = sem("s_am")
        s_ame = sem("s_ame")
        s_kv = sem("s_kv")
        s_st = sem("s_st")
        s_go = sem("s_go")
        s_goe = sem("s_goe")
        s_gss = sem("s_gss")
        s_gn = sem("s_gn")
        s_lg = sem("s_lg")
        s_sel = sem("s_sel")
        s_pos = sem("s_pos")
        s_rt = sem("s_rt")
        s_ht = sem("s_ht")
        s_hte = sem("s_hte")
        s_dg = sem("s_dg")
        s_g2 = sem("s_g2")
        s_g2e = sem("s_g2e")
        w2_used = sem("w2_used")
        w2f_used = sem("w2f_used")
        s_lgm = sem("s_lgm")
        s_rexp = sem("s_rexp")
        s_P = sem("s_P")
        s_gt = sem("s_gt")
        s_gte = sem("s_gte")
        s_gg = sem("s_gg")
        s_gge = sem("s_gge")
        s_e1 = sem("s_e1")
        s_e3 = sem("s_e3")
        s_esl = sem("s_esl")
        s_ea = sem("s_ea")
        s_et = sem("s_et")
        s_ete = sem("s_ete")
        s_eye = sem("s_eye")
        s_sct = sem("s_sct")
        s_add = sem("s_add")
        s_out = sem("s_out")
        s_chain = sem("s_chain")
        s_achain = sem("s_achain")
        s_gchain = sem("s_gchain")

        dist_i = sq[:, 0, :].bitcast(I32)
        slot_i = sq[:, 1, :].bitcast(I32)
        row_a, row_b = sq[:, 2, 0:P], sq[:, 3, 0:P]
        lam_in = sq[:, 4, :].rearrange("p (j d) -> p j d", j=4)
        lam_pr = sq[:, 5, 0:2 * DH].rearrange("p (j d) -> p j d", j=2)
        ba_row = bufB[:, 0:2, :].rearrange("p a s -> p (a s)")
        wa2 = bufB[0:GLA_RANK, 2:4, :].rearrange("p a s -> p (a s)")
        wa1 = bufB[:, 4, 0:KT * GLA_RANK].rearrange("p (k n) -> p k n", k=KT)
        x_rows = work[:, :, 0:D]
        def att(h):
            w = work[:, h % 2, :]
            return {"t1": w[:, 0:512].rearrange("p (m s) -> p m s", m=2),
                    "t0": w[:, 512:768].rearrange("p (m s) -> p m s", m=2),
                    "d1": w[:, 768:1024], "d0": w[:, 1024:1152], "pt": w[:, 1152:1536]}
        hid = work
        silu_f = rstd
        la = work[:, 0, 0:1024].rearrange("p (t c) -> p t c", t=TT)
        lz = work[:, 1, 0:1024].rearrange("p (t c) -> p t c", t=TT)
        le = work[:, 1, 1024:2048].rearrange("p (t c) -> p t c", t=TT)
        a1T = work[0:GLA_RANK, 0, 1024:1280]
        gq_t, gk_t = bufA[:, 0:GH, :], bufA[:, GH:2 * GH, :]
        bT = hT[:, 0:GH, :]
        dd = hT[:, GH:2 * GH, :]
        eb = rstd[:, 0:GH, :]
        ei = rstd[:, GH:2 * GH, :]
        qd = sq[:, 0:GH, :]
        ki = sq[:, GH:2 * GH, :]
        kd = oT[:, 0:GH, :]
        kdt = work[:, 0, 0:1024].rearrange("p (g c) -> p g c", g=8)
        am = work[:, 1, 0:1024].rearrange("p (g c) -> p g c", g=8)
        state = [w.rearrange("p (g v) -> p g v", g=GH)
                 for w in (ada_acc[:, 0, :], ada_acc[:, 1, :], work[:, 1, 1024:2048])]
        x_acc = oT[:, :, :].rearrange("p (t k) s -> p t (k s)", t=TT)
        h_tok = bufA[:, :, :].rearrange("p (t k) s -> p t (k s)", t=TT)
        hgT = bufB
        g2bc = work[:, 0, 0:1024]
        silu_e = work[:, 0, 1024:1536]
        hid_e = work[:, 0, 1536:2048]
        hidT = work[:, 1, 0:512]
        diag = work[:, 1, 512:1536].rearrange("p (k c) -> p k c", k=KT)
        Pm = work[:, 1, 512:1024].rearrange("p (t s) -> p t s", t=TT)
        Pg = work[:, 1, 1024:1536].rearrange("p (t s) -> p t s", t=TT)
        PgT = work[:, 1, 1536:2048].rearrange("p (b s) -> p b s", b=2)
        y_sb = V
        rt = sb("rt", [P, 9, TT * NE])
        cmp_a = ada_acc[:, 0, 0:128].rearrange("p (t e o) -> p t e o", t=TT, e=NE)
        cmp_b = ada_acc[:, 0, 128:256].rearrange("p (t e o) -> p t e o", t=TT, e=NE)

        def slot(i, n=SLOT):
            return ring[:, i % SLOTS, 0:n]

        def chunk_in(w, c0, n):
            return w[:, c0:c0 + n].rearrange("(k p) n -> p k n", p=P)

        def ffn_width(f):
            return min(FW, FFN - f * FW)

        def source(key):
            kind, i = key
            if kind.startswith("ada"):
                return chunk_in(t["ada_w"][int(kind[3])], i * FW, FW), KT, FW
            if kind == "in0":
                return chunk_in(t["da_w_in"][0], i * FW, FW), KT, FW
            if kind == "in1":
                return chunk_in(t["gla_w_in"][0], i * FW, FW), KT, FW
            if kind == "out0":
                return chunk_in(t["da_w_out"][0], i * FW, FW), KT, FW
            if kind == "out1":
                return chunk_in(t["gla_w_out"][0], i * FW, FW), KT, FW
            n = ffn_width(i)
            if kind == "w2":
                return t["ffn_w2"][0][i * FW:i * FW + n, :].rearrange("(k p) n -> p k n", p=P), n // P, D
            return chunk_in(t["ffn_" + kind][0], i * FW, n), KT, n

        def slot_view(i, k, n):
            return ring[:, i % SLOTS, 0:k * n].rearrange("p (k n) -> p k n", k=k)

        def expert_source(e, i):
            c, what = divmod(i, 3)
            if what == 2:
                w = t["moe_w2"].rearrange("e (c k p) n -> e c p k n", p=P, k=FPC)
                return w[bass.ds(e, 1), c, :, :, :].rearrange("o p k n -> p (o k) n"), FPC, D
            w = t["moe_w1" if what == 0 else "moe_w3"].rearrange("e (k p) n -> e p k n", p=P)
            return w[bass.ds(e, 1), :, :, c * FW:(c + 1) * FW].rearrange("o p k n -> p (o k) n"), KT, FW

        def wait_landed(eng, i, e=0):
            if isinstance(e, int):
                eng.wait_ge(landed[i % SLOTS], 16 * (i // SLOTS + 1 + e * (PER // SLOTS)))
            else:
                eng.wait_ge(landed[i % SLOTS], e * (16 * PER // SLOTS) + 16 * (i // SLOTS + 1))

        block = ctx.enter_context(nc.Block())

        @block.sync
        def _(sp):
            sp.dma_start(x_rows, t["x"][0].rearrange("(t p) d -> p t d", p=P)).then_inc(s_small, 16)

            def rows(dst, r0, src, n):
                sp.dma_start(dst[r0:r0 + n, :], src).then_inc(s_small, 16)

            rows(row_a, 0, t["c"].rearrange("o (k p) -> (o k) p", p=P), 8)
            rows(row_a, 8, t["norm1_g"].rearrange("l (k p) -> (l k) p", p=P), 16)
            rows(row_a, 24, t["norm2_g"].rearrange("l (k p) -> (l k) p", p=P), 16)
            rows(row_a, 40, t["ada_b"][0:1].rearrange("l (k p) -> (l k) p", p=P), 48)
            rows(row_a, 88, t["da_q_gain"].rearrange("o m d -> o (m d)"), 1)
            rows(row_a, 89, t["da_k_gain"].rearrange("o m d -> o (m d)"), 1)
            rows(row_a, 90, t["da_subln_g"], 1)
            rows(row_a, 91, t["gla_out_g"].rearrange("o (k p) -> (o k) p", p=P), 2)
            rows(row_b, 0, t["ada_b"][1:2].rearrange("l (k p) -> (l k) p", p=P), 48)
            for j, name in enumerate(("da_lam_q1", "da_lam_k1", "da_lam_q2", "da_lam_k2")):
                sp.dma_start(lam_in[:, j, :], t[name][0:1, :].to_broadcast([P, DH])).then_inc(s_small, 16)

            def wait_used(key):
                kind, f = key
                if kind.startswith("ada"):
                    sp.wait_ge(ada_used, ada_rank[key])
                elif kind == "w2":
                    sp.wait_ge(w2f_used, f + 1)
                elif kind in ("w1", "w3"):
                    sp.wait_ge(s_h13, min((f + 1) * FPC, FT))
                else:
                    sp.wait_ge(s_fill, 2 * proj_rank[key])

            def load(i, key):
                if i >= SLOTS:
                    wait_used(order[i - SLOTS])
                src, k, n = source(key)
                sp.dma_start(slot_view(i, k, n), src).then_inc(landed[i % SLOTS], 16)

            for i, key in enumerate(order):
                load(i, key)
                if key == ("w1", 0):
                    sp.wait_ge(s_pt, H)
                    sp.dma_start(ba_row[:, :], t["gla_b_a"][0:1, :].to_broadcast([P, 512])).then_inc(s_late, 16)
                    sp.dma_start(wa1[:, :, :], t["gla_w_a1"][0].rearrange("(k p) n -> p k n", p=P)).then_inc(s_late, 16)
                    sp.dma_start(wa2[:, :], t["gla_w_a2"][0]).then_inc(s_late, 16)
                    sp.dma_start(router[:, :, :], t["moe_router"][0].rearrange("(k p) n -> p k n", p=P)).then_inc(s_late, 16)

            def load_expert(e, i, first=False):
                j = i - SLOTS
                if first:
                    wait_used(order[PRE + j])
                else:
                    back, j = (0, j) if j >= 0 else (-1, j + PER)
                    c, what = divmod(j, 3)
                    if what == 2:
                        sp.wait_ge(w2_used, (e + back) * ECH + (c + 1))
                    else:
                        sp.wait_ge((s_e1, s_e3)[what], (e + back) * (2 * ECH) + 2 * (c + 1))
                src, k, n = expert_source(e, i)
                sp.dma_start(slot_view(PRE + i, k, n), src).then_inc(landed[(PRE + i) % SLOTS], 16)

            for i in range(SLOTS):
                load_expert(0, i, first=True)
            with sp.Fori(0, NE - 1) as e:
                for i in range(SLOTS, PER):
                    load_expert(e, i)
                for i in range(SLOTS):
                    load_expert(e + 1, i)
            for i in range(SLOTS, PER):
                load_expert(NE - 1, i)
            sp.wait_ge(s_add, 4 * NE)
            sp.dma_start(t["out"][0].rearrange("(t p) d -> p t d", p=P), x_acc).then_inc(s_out, 16)
            sp.wait_ge(s_out, 16)

        @block.gpsimd
        def _(pool):
            n = [0]

            def link(ins):
                n[0] += 1
                ins.then_inc(s_gchain, 1)
                pool.wait_ge(s_gchain, n[0])

            nc.gpsimd.memset(ident[:], 0.0).then_inc(s_gchain, 1)
            nc.gpsimd.memset(ones[:], 1.0).then_inc(s_gchain, 1)
            nc.gpsimd.memset(halves[:], 0.0).then_inc(s_gchain, 1)
            nc.gpsimd.memset(lower_e[:], 1.0).then_inc(s_gchain, 1)
            n[0] = 4
            pool.wait_ge(s_gchain, 4)
            link(nc.gpsimd.affine_select(out=ident[:], in_=ident[:], compare_op=ALU.not_equal, fill=1.0, base=0,
                                         pattern=[[-1, P]], channel_multiplier=1))
            link(nc.gpsimd.memset(halves[0:64, 0:64], 1.0))
            link(nc.gpsimd.memset(halves[64:128, 64:128], 1.0))
            link(nc.gpsimd.affine_select(out=tri[:], in_=halves[:], compare_op=ALU.is_ge, fill=0.0, base=0,
                                         pattern=[[1, P]], channel_multiplier=-1))
            link(nc.gpsimd.affine_select(out=before[:], in_=ones[:], compare_op=ALU.is_gt, fill=0.0, base=0,
                                         pattern=[[1, P]], channel_multiplier=-1))
            link(nc.gpsimd.affine_select(out=lower_e[:], in_=lower_e[:], compare_op=ALU.is_gt, fill=0.0, base=0,
                                         pattern=[[1, NE], [-1, NE]], channel_multiplier=0))
            link(nc.gpsimd.iota(dist_i, pattern=[[-1, S]], base=P, channel_multiplier=1))
            link(nc.gpsimd.iota(slot_i, pattern=[[1, S]], base=0, channel_multiplier=0))
            for j, width in enumerate((D, DH, P, DV)):
                last = nc.gpsimd.memset(eps[:, j:j + 1], width * EPS)
            last.then_inc(s_const, 1)

        @block.tensor
        def _(pe):
            mm = nc.tensor.matmul
            fill = [0]
            pe.wait_ge(s_const, 1)

            pe.wait_ge(s_small, 16 * 14)
            nc.tensor.transpose(psum[7][:, 0:93], row_a[0:93, :], ident[0:93, 0:93])
            nc.tensor.transpose(psum[7][:, 128:176], row_b[0:48, :], ident[0:48, 0:48]).then_inc(s_tp, 1)
            for b in range(4):
                for j in range(2):
                    for i in range(TT):
                        last = nc.tensor.transpose(psum[b][:, j * S + i * P:j * S + (i + 1) * P],
                                                   x_rows[:, i, (2 * b + j) * P:(2 * b + j + 1) * P], ident[:])
                last.then_inc(s_xt, 1)

            def mod_columns(l, third):
                n = 6 * l + third
                pe.wait_ge(ada_used, 2 * n + 2)
                if n:
                    pe.wait_ge(s_mod, n)
                for j in range(8):
                    last = mm(psum[7][:, 256 + 48 * l + 8 * third + j:257 + 48 * l + 8 * third + j],
                              ada_acc[:, n % 2, j * P:(j + 1) * P], ones[:, 0:1], start=True, stop=True)
                last.then_inc(s_modp, 1)

            def norm_sums(n):
                pe.wait_ge(s_sq, n + 1)
                for k in range(KT):
                    last = mm(psum[6][:, 0:S], ones[:], sq[:, k, :], start=(k == 0), stop=(k == KT - 1))
                last.then_inc(s_ssq, 1)

            def project(key, n, token_major):
                i = index[key]
                w = slot_view(i, KT, FW)
                wait_landed(pe, i)
                src, have = (hT, 8 * (n + 1)) if n is not None else (oT, None)
                for g in range(2):
                    f = fill[0]
                    if f >= 4:
                        pe.wait_ge(s_evac, f - 3)
                    if token_major:
                        for k in range(KT):
                            if have:
                                pe.wait_ge(s_h, have - KT + k + 1)
                            last = mm(psum[f % 4][:, :], src[:, k, g * P:(g + 1) * P], w[:, k, :],
                                      start=(k == 0), stop=(k == KT - 1))
                    else:
                        for j in range(2):
                            for k in range(KT):
                                if have:
                                    pe.wait_ge(s_h, have - KT + k + 1)
                                m = 2 * g + j
                                last = mm(psum[f % 4][:, j * S:(j + 1) * S], w[:, k, m * P:(m + 1) * P], src[:, k, :],
                                          start=(k == 0), stop=(k == KT - 1))
                    last.then_inc(s_fill, 1)
                    fill[0] += 1

            def qk_sums(f):
                pe.wait_ge(s_qsq, f + 1)
                if f >= 2:
                    pe.wait_ge(s_root, ROOT["qk"] + f - 1)
                mm(psum[4 + f % 2][:, :], halves[:], sq[:, 2 * (f % 4):2 * (f % 4) + 2, :],
                   start=True, stop=True).then_inc(s_qss, 1)

            pe.wait_ge(s_par, 1)
            mod_columns(0, 0)
            mod_columns(0, 1)
            norm_sums(0)
            for i in range(6):
                project(("in0", i), 0, token_major=(i >= 4))
                if 1 <= i <= 4:
                    qk_sums(2 * (i - 1))
                    qk_sums(2 * (i - 1) + 1)
            mod_columns(0, 2)

            def scores(h):
                if h >= 2:
                    pe.wait_ge(s_mx, h - 1)
                for m in range(2):
                    q = bufA[m * DH:(m + 1) * DH, h, :]
                    k = bufB[m * DH:(m + 1) * DH, h, :]
                    mm(psum[2 * (h % 2) + m][:, 0:S], q[:, P:S], k, start=True, stop=True)
                    last = mm(psum[2 * (h % 2) + m][:, S:S + P], q[:, 0:P], k[:, 0:P], start=True, stop=True)
                last.then_inc(s_sc, 1)

            def attend(h):
                a = att(h)
                pe.wait_ge(s_pd, h + 1)
                if h >= 1:
                    pe.wait_ge(s_pte, h)
                nc.tensor.transpose(psum[4][:, 0:P], a["d0"], ident[:])
                nc.tensor.transpose(psum[4][:, P:2 * P], a["d1"][:, 0:P], ident[:])
                nc.tensor.transpose(psum[4][:, 2 * P:3 * P], a["d1"][:, P:S], ident[:]).then_inc(s_pt, 1)
                pe.wait_ge(s_pte, h + 1)
                if h >= 1:
                    pe.wait_ge(s_oe, h)
                mm(psum[5][:, 0:S], V[:, 0, h * P:(h + 1) * P], a["pt"][:, 0:S], start=True, stop=False)
                mm(psum[5][:, P:S], V[:, 1, h * P:(h + 1) * P], a["pt"][:, S:S + P], start=False,
                   stop=True).then_inc(s_o, 1)

            pe.wait_ge(s_qn, 8)
            pe.wait_ge(s_evac, 12)
            scores(0)
            for h in range(H):
                if h + 1 < H:
                    scores(h + 1)
                attend(h)
            pe.wait_ge(s_mx, H)
            for g in range(4):
                pe.wait_ge(s_oe, 2 * g + 2)
                mm(psum[g][:, :], ones[:], sq[:, 2 * g:2 * g + 2, :], start=True, stop=True).then_inc(s_oss, 1)
            pe.wait_ge(s_on, H)
            for i in range(2):
                project(("out0", i), None, False)
            for third in (3, 4, 5):
                mod_columns(0, third)

            norm_sums(1)
            pe.wait_ge(s_evac, 16)

            def hidden(f, what, j):
                i = index[(what, f)]
                w = slot_view(i, KT, ffn_width(f))
                wait_landed(pe, i)
                o = 0 if what == "w1" else S
                g = f * FPC + j
                if o == 0 and g >= 2:
                    pe.wait_ge(s_hid, g - 1)
                for k in range(KT):
                    pe.wait_ge(s_h, 8 + k + 1)
                    last = mm(psum[4 + g % 2][:, o:o + S], w[:, k, j * P:(j + 1) * P], hT[:, k, :],
                              start=(k == 0), stop=(k == KT - 1))
                return last

            def ffn_out(f):
                n = ffn_width(f) // P
                i = index[("w2", f)]
                w = slot_view(i, n, D)
                wait_landed(pe, i)
                pe.wait_ge(s_hid, f * FPC + n)
                for j in range(n):
                    for m in range(KT):
                        last = mm(psum[m // 2][:, (m % 2) * S:(m % 2 + 1) * S], w[:, j, m * P:(m + 1) * P],
                                  hid[:, f % 2, j * S:(j + 1) * S], start=(f == 0 and j == 0 and m % 2 == 0),
                                  stop=(f == NCH - 1 and j == n - 1), skip_group_check=True)
                last.then_inc(w2f_used, 1)

            for f in range(NCH):
                n = ffn_width(f) // P
                for j in range(n):
                    a = hidden(f, "w1", j)
                    b = hidden(f, "w3", j)
                    b.then_inc(s_h13, 1)
                if f:
                    ffn_out(f - 1)
                mod_columns(1, f)
            ffn_out(NCH - 1)

            norm_sums(2)
            pe.wait_ge(s_late, 64)
            for k in range(KT):
                pe.wait_ge(s_h, 16 + k + 1)
                last = mm(psum[4][0:GLA_RANK, 0:S], wa1[:, k, :], hT[:, k, :], start=(k == 0), stop=(k == KT - 1))
            last.then_inc(s_a1, 1)
            for i in range(6):
                project(("in1", i), 2, token_major=(i in (2, 3)))
                if i == 0:
                    pe.wait_ge(s_a1e, 1)
                    for tt in range(TT):
                        mm(psum[4 + tt][:, :], a1T[:, tt * P:(tt + 1) * P], wa2[:, :], start=True,
                           stop=True).then_inc(s_z, 1)
            pe.wait_ge(s_la, 1)
            for g in range(GH):
                for tt in range(TT):
                    o = (g % 2) * S + tt * P
                    last = mm(psum[4 + g // 2][:, o:o + P], la[:, tt, g * P:(g + 1) * P], tri[:],
                              start=True, stop=True)
            last.then_inc(s_b, 1)
            pe.wait_ge(s_qd, 3)
            pe.wait_ge(s_evac, 28)
            for g in range(GH):
                for tt in range(TT):
                    n = g * TT + tt
                    last = nc.tensor.transpose(psum[n // 4][:, (n % 4) * P:(n % 4 + 1) * P],
                                               kd[:, g, tt * P:(tt + 1) * P], ident[:])
            last.then_inc(s_kdt, 1)
            for g in range(GH):
                for tt in range(TT):
                    n = g * TT + tt
                    last = mm(psum[2 + n // 4][:, (n % 4) * P:(n % 4 + 1) * P], ki[:, g, tt * P:(tt + 1) * P],
                              qd[:, g, tt * P:(tt + 1) * P], start=True, stop=True)
            last.then_inc(s_am, 1)
            pe.wait_ge(s_kde, 1)
            for c in range(NC - 1):
                r0, tt = (c % 2) * CHUNK, c // 2
                if c:
                    pe.wait_ge(s_st, c)
                for g in range(GH):
                    last = mm(psum[4 + g // 2][:, (g % 2) * DV:(g % 2 + 1) * DV], kdt[r0:r0 + CHUNK, g * TT + tt, :],
                              V[r0:r0 + CHUNK, tt, g * DV:(g + 1) * DV], start=True, stop=True)
                last.then_inc(s_kv, 1)
            pe.wait_ge(s_ame, 1)
            pe.wait_ge(s_st, NC - 1)
            for g in range(GH):
                for v in range(2):
                    for tt in range(TT):
                        o = v * S + tt * P
                        mm(psum[g][:, o:o + P], V[:, tt, g * DV + v * P:g * DV + (v + 1) * P], am[:, g * TT + tt, :],
                           start=(v == 0 and tt == 0), stop=False, skip_group_check=True)
                    for c in range(1, NC):
                        o = v * S + c * CHUNK
                        last = mm(psum[g][:, o:o + CHUNK], state[c - 1][:, g, v * P:(v + 1) * P],
                                  qd[:, g, c * CHUNK:(c + 1) * CHUNK], start=False, stop=True, skip_group_check=True)
                last.then_inc(s_go, 1)
            pe.wait_ge(s_mod, 12)
            for g in range(GH):
                pe.wait_ge(s_goe, g + 1)
                for v in range(2):
                    last = mm(psum[4 + g][:, 0:S], ones[:], rstd[:, 2 * g + v, :],
                              start=(v == 0), stop=(v == 1))
                last.then_inc(s_gss, 1)
            pe.wait_ge(s_gn, GH * 2)
            for i in range(2):
                project(("out1", i), None, False)

            norm_sums(3)
            for tt in range(TT):
                for k in range(KT):
                    pe.wait_ge(s_h, 24 + k + 1)
                    last = mm(psum[4][:, tt * NE:(tt + 1) * NE], hT[:, k, tt * P:(tt + 1) * P], router[:, k, :],
                              start=(k == 0), stop=(k == KT - 1))
            last.then_inc(s_lg, 1)
            pe.wait_ge(s_evac, 32)
            for n, src in enumerate((hT, xT)):
                for b in range(4):
                    if n:
                        pe.wait_ge(s_hte, b + 1)
                    tt, half = divmod(b, 2)
                    for k in range(4):
                        last = nc.tensor.transpose(psum[b][:, k * P:(k + 1) * P],
                                                   src[:, half * 4 + k, tt * P:(tt + 1) * P], ident[:])
                    last.then_inc(s_ht, 1)
            pe.wait_ge(s_dg, 1)
            for k in range(KT):
                last = mm(psum[5 + k // 4][:, (k % 4) * P:(k % 4 + 1) * P], ones[:], diag[:, k, :], start=True, stop=True)
            last.then_inc(s_g2, 1)
            pe.wait_ge(s_sel, 1)
            selT = rt[:, 0, :].rearrange("p (t e) -> p t e", t=TT)
            mm(psum[7][:, 0:NE], before[:], selT[:, 0, :], start=True, stop=True)
            mm(psum[7][:, NE:2 * NE], before[:], selT[:, 1, :], start=True, stop=False)
            mm(psum[7][:, NE:2 * NE], ones[:], selT[:, 0, :], start=False, stop=True)
            mm(psum[7][:, 2 * NE:3 * NE], ones[:], selT[:, 0, :], start=True, stop=False)
            mm(psum[7][:, 2 * NE:3 * NE], ones[:], selT[:, 1, :], start=False, stop=True).then_inc(s_pos, 1)
            pe.wait_ge(s_rt, 1)
            pe.wait_ge(s_hte, 8)
            pe.wait_ge(s_g2e, 2)

            def expert(e, nb):
                inc = 2 // nb

                def first(u):
                    c, b = divmod(u, nb)
                    for what in range(2):
                        i = PRE + 3 * c + what
                        if b == 0:
                            wait_landed(pe, i, e)
                        if u:
                            pe.wait_ge((s_esl, s_ea)[what], e * (2 * ECH) + u * inc)
                        w = slot_view(i, KT, FW)
                        for k in range(KT):
                            last = mm(psum[what][:, :], hgT[:, k, b * P:(b + 1) * P], w[:, k, :],
                                      start=(k == 0), stop=(k == KT - 1))
                        last.then_inc((s_e1, s_e3)[what], inc)

                def second(u):
                    c, b = divmod(u, nb)
                    i = PRE + 3 * c + 2
                    if b == 0:
                        wait_landed(pe, i, e)
                    pe.wait_ge(s_ete, e * (2 * ECH) + (u + 1) * inc)
                    w = slot_view(i, FPC, D)
                    for j in range(FPC):
                        for half in range(2):
                            last = mm(psum[2 + 2 * b + half][:, :], hidT[:, j * P:(j + 1) * P],
                                      w[:, j, half * 512:(half + 1) * 512], start=(c == 0 and j == 0),
                                      stop=(c == ECH - 1 and j == FPC - 1))
                    return last

                def turn(u):
                    pe.wait_ge(s_ea, e * (2 * ECH) + (u + 1) * inc)
                    for j in range(FPC):
                        last = nc.tensor.transpose(psum[6][:, j * P:(j + 1) * P], hid_e[:, j * P:(j + 1) * P], ident[:])
                    last.then_inc(s_et, inc)

                for half in range(4):
                    if half:
                        pe.wait_ge(s_gte, e * 4 + half)
                    for k in range(2):
                        kk = half * 2 + k
                        for tt in range(TT):
                            last = mm(psum[7][:, k * S:k * S + nb * P], h_tok[:, tt, kk * P:(kk + 1) * P],
                                      Pm[:, tt, 0:nb * P], start=(tt == 0), stop=(tt == TT - 1))
                    last.then_inc(s_gt, 1)
                pe.wait_ge(s_gte, e * 4 + 4)
                for b in range(nb):
                    for tt in range(TT):
                        last = nc.tensor.transpose(psum[7][:, b * S + tt * P:b * S + (tt + 1) * P],
                                                   Pg[:, tt, b * P:(b + 1) * P], ident[:])
                last.then_inc(s_gg, 1)
                units = ECH * nb
                for u in range(units):
                    c, b = divmod(u, nb)
                    first(u)
                    if u:
                        last = second(u - 1)
                        if (u - 1) % nb == nb - 1:
                            last.then_inc(w2_used, 1)
                    turn(u)
                last = second(units - 1)
                last.then_inc(w2_used, 1)
                pe.wait_ge(s_gge, e + 1)
                pe.wait_ge(s_eye, e * 2 + 2)
                n = 0
                for tt in range(TT):
                    for half in range(2):
                        if n >= 2:
                            pe.wait_ge(s_add, e * 4 + n - 1)
                        for b in range(nb):
                            last = mm(psum[6 + n % 2][:, :], PgT[:, b, tt * P:(tt + 1) * P],
                                      y_sb[:, b, half * 512:(half + 1) * 512], start=(b == 0), stop=(b == nb - 1))
                        last.then_inc(s_sct, 1)
                        n += 1
                pe.wait_ge(s_add, e * 4 + 4)

            with pe.Fori(0, NE) as e:
                pe.wait_ge(s_P, e + 1)
                nb = pe.value_load(nbk[0:1, bass.ds(e, 1)], min_val=1, max_val=2)
                for n in (1, 2):
                    with pe.If(nb == n):
                        expert(e, n)

        @block.scalar
        def _(act):
            A = nc.scalar.activation
            n_link = [0]

            def link(ins):
                n_link[0] += 1
                ins.then_inc(s_achain, 1)
                act.wait_ge(s_achain, n_link[0])

            act.wait_ge(s_par, 1)
            A(c_act[:], par[:, C0:C0 + KT], ACT.Silu).then_inc(s_cact, 1)
            act.wait_ge(s_lam, 1)
            A(lam[:, 2:4], lam[:, 0:2], ACT.Exp).then_inc(s_lame, 1)

            def squares(n):
                act.wait_ge(s_x, 8 * (n + 1))
                if n == 0:
                    act.wait_ge(s_constv, 1)
                A(sq[:], xT[:], ACT.Square).then_inc(s_sq, 1)

            def shift(n):
                l, second = divmod(n, 2)
                c = 24 if second else 0
                act.wait_ge(s_mod, 6 * l + (4 if second else 1))
                for k in range(KT):
                    act.wait_ge(s_hp, 8 * n + k + 1)
                    A(hT[:, k, :], hT[:, k, :], ACT.Identity, bias=mod[:, l, c + k:c + k + 1]).then_inc(s_h, 1)

            def evac(f, dst, func=ACT.Copy):
                act.wait_ge(s_fill, f + 1)
                A(dst, psum[f % 4][:, :], func).then_inc(s_evac, 1)

            def root(dst, src, kind):
                A(dst, src, ACT.Sqrt, bias=eps[:, kind:kind + 1]).then_inc(s_root, 1)

            def norm_root(n):
                act.wait_ge(s_ssq, n + 1)
                root(rstd[:, 0, :], psum[6][:, 0:S], 0)

            def qk_root(f):
                act.wait_ge(s_qss, f + 1)
                if f >= 2:
                    act.wait_ge(s_qn, f - 1)
                root(rstd[:, 2 * (f % 2) + 2:2 * (f % 2) + 4, :], psum[4 + f % 2][:, :], 1)

            act.wait_ge(s_const, 1)
            squares(0)
            norm_root(0)
            shift(0)
            for f in range(8):
                act.wait_ge(s_fill, f + 1)
                if f < 4:
                    act.wait_ge(s_ssq, 1)
                else:
                    act.wait_ge(s_qss, f - 3)
                A(sq[:, 2 * (f % 4):2 * (f % 4) + 2, :], psum[f % 4][:, :], ACT.Square).then_inc(s_qsq, 1)
                evac(f, (bufA if f < 4 else bufB)[:, 2 * (f % 4):2 * (f % 4) + 2, :])
                if f >= 4:
                    qk_root(f - 4)
            for f in range(8, 12):
                evac(f, V[:, f % 2, ((f - 8) // 2) * 512:((f - 8) // 2 + 1) * 512])
                qk_root(f - 4)
            for h in range(H):
                a = att(h)
                act.wait_ge(s_mx, h + 1)
                nm = small[:, h % 2, :]
                for m in range(2):
                    A(a["t1"][:, m, :], a["t1"][:, m, :], ACT.Exp, bias=nm[:, m:m + 1], accum_out=nm[:, 4 + m:5 + m])
                    last = A(a["t0"][:, m, :], a["t0"][:, m, :], ACT.Exp, bias=nm[:, 2 + m:3 + m],
                             accum_out=nm[:, 6 + m:7 + m])
                last.then_inc(s_ex, 1)

                def tail(h):
                    a = att(h)
                    act.wait_ge(s_pt, h + 1)
                    A(a["pt"], psum[4][:, 0:3 * P], ACT.Copy).then_inc(s_pte, 1)
                    act.wait_ge(s_o, h + 1)
                    if h == 0:
                        act.wait_ge(s_qss, 8)
                    A(sq[:, h, :], psum[5][:, 0:S], ACT.Square)
                    A(oT[:, h, :], psum[5][:, 0:S], ACT.Copy).then_inc(s_oe, 1)

                if h:
                    tail(h - 1)
            tail(H - 1)
            for g in range(4):
                act.wait_ge(s_oss, g + 1)
                root(rstd[:, 2 * g:2 * g + 2, :], psum[g][:, :], 2)
            squares(1)
            norm_root(1)
            shift(1)
            for g in range(FT):
                act.wait_ge(s_h13, g + 1)
                if g >= 8:
                    act.wait_ge(s_hid, g - 7)
                else:
                    act.wait_ge(s_hp, 16)
                A(silu_f[:, g % 8, :], psum[4 + g % 2][:, 0:S], ACT.Silu).then_inc(s_silu, 1)
            squares(2)
            norm_root(2)
            shift(2)
            act.wait_ge(s_a1, 1)
            A(a1T, psum[4][0:GLA_RANK, 0:S], ACT.Copy).then_inc(s_a1e, 1)
            for f in range(16, 20):
                evac(f, bufA[:, 2 * (f - 16):2 * (f - 16) + 2, :])
            act.wait_ge(s_zb, 2)
            A(le, le, ACT.Exp, scale=-1.0).then_inc(s_achain, 1)
            act.wait_ge(s_achain, 1)
            A(le, le, ACT.Ln, bias=ones[:, 0:1]).then_inc(s_ln, 1)
            for f in range(20, 24):
                evac(f, V[:, f % 2, ((f - 20) // 2) * 512:((f - 20) // 2 + 1) * 512])
            for f in range(24, 28):
                evac(f, bufB[:, 2 * (f - 24):2 * (f - 24) + 2, :], ACT.Silu)
            act.wait_ge(s_b, 1)
            for g in range(2):
                A(bT[:, 2 * g:2 * g + 2, :], psum[4 + g][:, :], ACT.Copy)
                A(eb[:, 2 * g:2 * g + 2, :], psum[4 + g][:, :], ACT.Exp)
                A(ei[:, 2 * g:2 * g + 2, :], psum[4 + g][:, :], ACT.Exp, scale=-1.0).then_inc(s_be, 1)
            act.wait_ge(s_dd, 1)
            A(dd, dd, ACT.Exp).then_inc(s_ed, 1)
            act.wait_ge(s_kdt, 1)
            A(kdt[:, 0:4, :], psum[0][:, :], ACT.Copy)
            A(kdt[:, 4:8, :], psum[1][:, :], ACT.Copy).then_inc(s_kde, 1)
            act.wait_ge(s_qd, 3)
            act.wait_ge(s_st, NC - 1)
            for g in range(GH):
                act.wait_ge(s_go, g + 1)
                A(rstd[:, 2 * g:2 * g + 2, :], psum[g][:, :], ACT.Square)
                A(oT[:, 2 * g:2 * g + 2, :], psum[g][:, :], ACT.Copy).then_inc(s_goe, 1)
            for g in range(GH):
                act.wait_ge(s_gss, g + 1)
                root(bufA[:, g, :], psum[4 + g][:, 0:S], 3)
            act.wait_ge(s_gn, 8)
            squares(3)
            norm_root(3)
            shift(3)
            for n in range(8):
                act.wait_ge(s_ht, n + 1)
                dst = h_tok if n < 4 else x_acc
                tt, half = divmod(n % 4, 2)
                A(dst[:, tt, half * 512:(half + 1) * 512], psum[n % 4][:, :], ACT.Copy).then_inc(s_hte, 1)
            act.wait_ge(s_lgm, 1)
            A(rt[:, 4, :], rt[:, 3, :], ACT.Exp).then_inc(s_rexp, 1)
            act.wait_ge(s_g2, 1)
            for g in range(2):
                A(g2bc[:, g * 512:(g + 1) * 512], psum[5 + g][:, :], ACT.Copy).then_inc(s_g2e, 1)
            act.wait_ge(s_rt, 1)

            def expert(e, nb):
                inc = 2 // nb
                for half in range(4):
                    act.wait_ge(s_gt, e * 4 + half + 1)
                    A(hgT[:, 2 * half:2 * half + 2, 0:nb * P],
                      psum[7][:, :].rearrange("p (k s) -> p k s", k=2)[:, :, 0:nb * P], ACT.Copy).then_inc(s_gte, 1)
                act.wait_ge(s_gg, e + 1)
                A(PgT[:, 0:nb, :], psum[7][:, 0:nb * S].rearrange("p (b s) -> p b s", b=nb), ACT.Copy).then_inc(s_gge, 1)
                for u in range(ECH * nb):
                    act.wait_ge(s_e1, e * (2 * ECH) + (u + 1) * inc)
                    if u:
                        act.wait_ge(s_ea, e * (2 * ECH) + u * inc)
                    A(silu_e, psum[0][:, :], ACT.Silu).then_inc(s_esl, inc)
                    act.wait_ge(s_et, e * (2 * ECH) + (u + 1) * inc)
                    A(hidT, psum[6][:, :], ACT.Copy).then_inc(s_ete, inc)

            with act.Fori(0, NE) as e:
                nb = act.value_load(nbk[0:1, bass.ds(e, 1)], min_val=1, max_val=2)
                for n in (1, 2):
                    with act.If(nb == n):
                        expert(e, n)

        @block.vector
        def _(dve):
            v = nc.vector
            n_link = [0]

            def link(ins):
                n_link[0] += 1
                ins.then_inc(s_chain, 1)
                dve.wait_ge(s_chain, n_link[0])

            dve.wait_ge(s_tp, 1)
            v.tensor_copy(par[:, 0:88], psum[7][:, 0:88])
            v.tensor_copy(par[:, 136:141], psum[7][:, 88:93])
            link(v.tensor_copy(par[:, 88:136], psum[7][:, 128:176]))
            v.tensor_scalar(gq[:, 0:1], par[:, QG:QG + 1], 1.0, None, ALU.mult)
            v.tensor_scalar(gq[:, 1:2], par[:, QG + 1:QG + 2], math.sqrt(DH), None, ALU.mult)
            v.tensor_scalar(gq[:, 2:3], par[:, QG + 2:QG + 3], (1.0 - LAMBDA_INIT) * math.sqrt(P), None, ALU.mult)
            link(v.tensor_scalar(gq[:, 3:5], par[:, QG + 3:QG + 5], math.sqrt(DV), None, ALU.mult))
            v.memset(rt[:, 8, :], 0.0).then_inc(s_par, 1)
            for b in range(4):
                dve.wait_ge(s_xt, b + 1)
                v.tensor_copy(xT[:, 2 * b:2 * b + 2, :], psum[b][:, :]).then_inc(s_x, 2)
            dve.wait_ge(s_const, 1)
            v.tensor_copy(slot_no[:], slot_i)
            link(v.tensor_copy(dist[:], dist_i))
            link(v.tensor_scalar(tri[:], tri[:], 1.0 / GLA_TAU, None, ALU.mult))
            link(v.scalar_tensor_tensor(dist[:], dist[:], -1.0, dist[:], ALU.mult, ALU.min))
            link(v.memset(dist[0:64, 192:256], HIDDEN))
            dve.wait_ge(s_small, 16 * 14)
            v.tensor_tensor(lam_pr[:, 0, :], lam_in[:, 0, :], lam_in[:, 1, :], ALU.mult)
            link(v.tensor_tensor(lam_pr[:, 1, :], lam_in[:, 2, :], lam_in[:, 3, :], ALU.mult))
            v.tensor_reduce(lam[:, 0:2], lam_pr, AX_X, ALU.add).then_inc(s_lam, 1)
            dve.wait_ge(s_lam, 1)
            dve.sem_inc(s_constv, 1)
            dve.wait_ge(s_lame, 1)
            link(v.tensor_tensor(lam[:, 0:1], lam[:, 3:4], lam[:, 2:3], ALU.subtract))
            link(v.tensor_scalar(lam[:, 0:1], lam[:, 0:1], -LAMBDA_INIT, None, ALU.add))

            dve.wait_ge(s_cact, 1)

            def ada_chunk(l, c):
                key = (f"ada{l}", c)
                i = index[key]
                n = 6 * l + c // 2
                w = slot_view(i, KT, FW)
                acc = ada_acc[:, n % 2, (c % 2) * FW:(c % 2 + 1) * FW]
                wait_landed(dve, i)
                if n >= 2:
                    dve.wait_ge(s_modp, n - 1)
                link(v.tensor_scalar(acc, w[:, 0, :], c_act[:, 0:1], None, ALU.mult))
                for k in range(1, KT):
                    last = v.scalar_tensor_tensor(acc, w[:, k, :], c_act[:, k:k + 1], acc, ALU.mult, ALU.add)
                    if k < KT - 1:
                        link(last)
                last.then_inc(ada_used, 1)

            def mod_third(l, third):
                dve.wait_ge(s_modp, 6 * l + third + 1)
                o = 256 + 48 * l + 8 * third
                v.tensor_tensor(mod[:, l, 8 * third:8 * third + 8], psum[7][:, o:o + 8],
                                par[:, AB + 48 * l + 8 * third:AB + 48 * l + 8 * third + 8], ALU.add).then_inc(s_mod, 1)

            def gains(n):
                l, second = divmod(n, 2)
                dve.wait_ge(s_mod, 6 * l + (5 if second else 2))
                c = 32 if second else 8
                g = (N2 if second else N1) + 8 * l
                link(v.scalar_tensor_tensor(cols[:, n, :], mod[:, l, c:c + 8], 1.0, par[:, g:g + 8], ALU.add, ALU.mult))
                link(v.tensor_scalar(cols[:, n, :], cols[:, n, :], math.sqrt(D), None, ALU.mult))

            def normalise(n):
                r = rstd[:, 0, :]
                dve.wait_ge(s_root, ROOT[f"norm{n}"] + 1)
                link(v.reciprocal(r, r))
                if n == 1 or n == 3:
                    dve.wait_ge(s_fill, 8 * (n + 1))
                if n == 2:
                    dve.wait_ge(w2f_used, NCH)
                for k in range(KT):
                    v.scalar_tensor_tensor(hT[:, k, :], xT[:, k, :], cols[:, n, k:k + 1], r, ALU.mult,
                                           ALU.mult).then_inc(s_hp, 1)

            for c in range(4):
                ada_chunk(0, c)
            mod_third(0, 0)
            mod_third(0, 1)
            gains(0)
            normalise(0)
            for f in range(8):
                dve.wait_ge(s_root, ROOT["qk"] + f + 1)
                dve.wait_ge(s_evac, f + 1)
                dst = (bufA if f < 4 else bufB)[:, 2 * (f % 4):2 * (f % 4) + 2, :]
                r = rstd[:, 2 * (f % 2) + 2:2 * (f % 2) + 4, :]
                link(v.reciprocal(r, r))
                v.scalar_tensor_tensor(dst, dst, gq[:, f // 4:f // 4 + 1], r, ALU.mult, ALU.mult).then_inc(s_qn, 1)
            ada_chunk(0, 4)
            ada_chunk(0, 5)
            mod_third(0, 2)

            def biased(h):
                a = att(h)
                slope = 2.0 ** (-8.0 * (h + 1) / H)
                nm = small[:, h % 2, :]
                dve.wait_ge(s_sc, h + 1)
                if h >= 2:
                    dve.wait_ge(s_pd, h - 1)
                    dve.wait_ge(s_pt, h - 1)
                for m in range(2):
                    v.scalar_tensor_tensor(a["t1"][:, m, :], dist[:, :], slope,
                                           psum[2 * (h % 2) + m][:, 0:S], ALU.mult, ALU.add)
                    last = v.scalar_tensor_tensor(a["t0"][:, m, :], dist[:, P:S], slope,
                                                  psum[2 * (h % 2) + m][:, S:S + P], ALU.mult, ALU.add)
                link(last)
                v.tensor_reduce(nm[:, 0:2], a["t1"], AX_X, ALU.max, negate=True)
                v.tensor_reduce(nm[:, 2:4], a["t0"], AX_X, ALU.max, negate=True).then_inc(s_mx, 1)

            def differ(h):
                a = att(h)
                nm = small[:, h % 2, :]
                dve.wait_ge(s_ex, h + 1)
                link(v.reciprocal(nm[:, 8:12], nm[:, 4:8]))
                v.tensor_scalar(nm[:, 12:13], nm[:, 9:10], lam[:, 0:1], None, ALU.mult)
                v.tensor_scalar(nm[:, 13:14], nm[:, 11:12], lam[:, 0:1], None, ALU.mult)
                v.tensor_scalar(a["d1"], a["t1"][:, 0, :], nm[:, 8:9], None, ALU.mult)
                link(v.tensor_scalar(a["d0"], a["t0"][:, 0, :], nm[:, 10:11], None, ALU.mult))
                link(v.scalar_tensor_tensor(a["d1"], a["t1"][:, 1, :], nm[:, 12:13], a["d1"], ALU.mult, ALU.add))
                v.scalar_tensor_tensor(a["d0"], a["t0"][:, 1, :], nm[:, 13:14], a["d0"], ALU.mult,
                                       ALU.add).then_inc(s_pd, 1)

            biased(0)
            for h in range(H):
                if h + 1 < H:
                    biased(h + 1)
                differ(h)
            for g in range(4):
                dve.wait_ge(s_root, ROOT["sub"] + g + 1)
                r = rstd[:, 2 * g:2 * g + 2, :]
                link(v.reciprocal(r, r))
                v.scalar_tensor_tensor(oT[:, 2 * g:2 * g + 2, :], oT[:, 2 * g:2 * g + 2, :], gq[:, 2:3], r,
                                       ALU.mult, ALU.mult).then_inc(s_on, 2)

            def residual(l, f0):
                dve.wait_ge(s_mod, 6 * l + 3)
                for g in range(4):
                    f = f0 + g
                    dve.wait_ge(s_fill, f + 1)
                    for j in range(2):
                        m = 2 * g + j
                        last = v.scalar_tensor_tensor(xT[:, m, :], psum[f % 4][:, j * S:(j + 1) * S],
                                                      mod[:, l, 16 + m:17 + m], xT[:, m, :], ALU.mult, ALU.add)
                        if j == 0:
                            last.then_inc(s_x, 1)
                    last.then_inc(s_evac, 1)
                    dve.wait_ge(s_evac, f + 1)
                    dve.sem_inc(s_x, 1)

            residual(0, 12)
            for third in (3, 4, 5):
                ada_chunk(0, 2 * third)
                ada_chunk(0, 2 * third + 1)
                mod_third(0, third)
            gains(1)
            normalise(1)
            for f in range(NCH):
                n = ffn_width(f) // P
                for j in range(n):
                    g = f * FPC + j
                    dve.wait_ge(s_silu, g + 1)
                    if f >= 2:
                        dve.wait_ge(w2f_used, f - 1)
                    v.tensor_tensor(hid[:, f % 2, j * S:(j + 1) * S], silu_f[:, g % 8, :],
                                    psum[4 + g % 2][:, S:2 * S], ALU.mult).then_inc(s_hid, 1)
                ada_chunk(1, 2 * f)
                ada_chunk(1, 2 * f + 1)
                mod_third(1, f)
            dve.wait_ge(w2f_used, NCH)
            for m in range(KT):
                v.scalar_tensor_tensor(xT[:, m, :], psum[m // 2][:, (m % 2) * S:(m % 2 + 1) * S],
                                       mod[:, 0, 40 + m:41 + m], xT[:, m, :], ALU.mult, ALU.add).then_inc(s_x, 1)
            gains(2)
            normalise(2)

            dve.wait_ge(s_late, 64)
            for tt in range(TT):
                dve.wait_ge(s_z, tt + 1)
                link(v.tensor_tensor(lz[:, tt, :], psum[4 + tt][:, :], ba_row[:, :], ALU.add))
                v.scalar_tensor_tensor(le[:, tt, :], lz[:, tt, :], -1.0, lz[:, tt, :], ALU.mult, ALU.max).then_inc(s_zb, 1)
            dve.wait_ge(s_ln, 1)
            v.scalar_tensor_tensor(la, lz, 0.0, le, ALU.min, ALU.subtract).then_inc(s_la, 1)
            dve.wait_ge(s_be, 2)
            b16 = bT.rearrange("p g (c s) -> p (g c) s", c=NC)
            d16 = dd.rearrange("p g (c s) -> p (g c) s", c=NC)
            v.tensor_tensor(d16, b16[:, :, CHUNK - 1:CHUNK].to_broadcast([P, GH * NC, CHUNK]), b16,
                            ALU.subtract).then_inc(s_dd, 1)
            dve.wait_ge(s_evac, 20)
            v.scalar_tensor_tensor(qd, gq_t, float(P) ** -0.5, eb, ALU.mult, ALU.mult).then_inc(s_qd, 1)
            v.tensor_tensor(ki, gk_t, ei, ALU.mult).then_inc(s_qd, 1)
            dve.wait_ge(s_ed, 1)
            v.tensor_tensor(kd, gk_t, dd, ALU.mult).then_inc(s_qd, 1)
            dve.wait_ge(s_la, 1)
            link(v.memset(am[:, :, :], 0.0))
            dve.wait_ge(s_am, 1)
            for g in range(2):
                last = v.copy_predicated(am[:, 4 * g:4 * g + 4, :],
                                         tri[:, :].bitcast(I32).rearrange("p (o c) -> p o c", o=1).to_broadcast([P, 4, P]),
                                         psum[2 + g][:, :].rearrange("p (o c) -> p o c", o=4))
            last.then_inc(s_ame, 1)
            for c in range(NC - 1):
                dve.wait_ge(s_kv, c + 1)
                for g in range(GH):
                    kv = psum[4 + g // 2][:, (g % 2) * DV:(g % 2 + 1) * DV]
                    if c == 0:
                        last = v.tensor_copy(state[0][:, g, :], kv)
                    else:
                        last = v.scalar_tensor_tensor(state[c][:, g, :], state[c - 1][:, g, :],
                                                      eb[:, g, (c + 1) * CHUNK - 1:(c + 1) * CHUNK], kv,
                                                      ALU.mult, ALU.add)
                last.then_inc(s_st, 1)
                dve.wait_ge(s_st, c + 1)
            for g in range(GH):
                r = bufA[:, g, :]
                dve.wait_ge(s_root, ROOT["gla"] + g + 1)
                link(v.reciprocal(r, r))
                for w in range(2):
                    o = oT[:, 2 * g + w, :]
                    link(v.scalar_tensor_tensor(o, o, gq[:, 3 + w:4 + w], r, ALU.mult, ALU.mult))
                    dve.wait_ge(s_evac, 28)
                    v.tensor_tensor(o, o, bufB[:, 2 * g + w, :], ALU.mult).then_inc(s_gn, 1)
            residual(1, 28)
            gains(3)
            normalise(3)

            for k in range(KT):
                last = v.tensor_scalar(diag[:, k, :], ident[:], mod[:, 1, 40 + k:41 + k], None, ALU.mult)
            last.then_inc(s_dg, 1)
            r3 = [rt[:, j, :].rearrange("p (t e) -> p t e", t=TT) for j in range(9)]
            sel, gate, posm, tmp, ex, lg = r3[0], r3[1], r3[2], r3[3], r3[4], r3[5]
            mx = rt[:, 6, :]
            dve.wait_ge(s_lg, 1)
            link(v.tensor_copy(lg, psum[4][:, 0:TT * NE].rearrange("p (t e) -> p t e", t=TT)))
            for tt in range(TT):
                mine = rt[:, 5, tt * NE:(tt + 1) * NE].rearrange("p (e o) -> p e o", o=1).to_broadcast([P, NE, NE])
                other = rt[:, 5, tt * NE:(tt + 1) * NE].rearrange("p (o e) -> p o e", o=1).to_broadcast([P, NE, NE])
                link(v.tensor_tensor(cmp_a[:, tt], other, mine, ALU.is_gt))
                link(v.tensor_tensor(cmp_b[:, tt], other, mine, ALU.is_equal))
                link(v.tensor_tensor(cmp_b[:, tt], cmp_b[:, tt], lower_e[:, :, :], ALU.mult))
                link(v.tensor_tensor(cmp_a[:, tt], cmp_a[:, tt], cmp_b[:, tt], ALU.add))
                link(v.tensor_reduce(tmp[:, tt, :], cmp_a[:, tt], AX_X, ALU.add))
                link(v.tensor_reduce(mx[:, tt:tt + 1], lg[:, tt, :], AX_X, ALU.max, negate=True))
            link(v.tensor_scalar(sel, tmp, 1.5, None, ALU.is_lt))
            dve.sem_inc(s_sel, 1)
            for tt in range(TT):
                link(v.tensor_scalar(tmp[:, tt, :], lg[:, tt, :], mx[:, tt:tt + 1], None, ALU.add))
            dve.sem_inc(s_lgm, 1)
            dve.wait_ge(s_rexp, 1)
            link(v.tensor_tensor(ex, ex, sel, ALU.mult))
            link(v.tensor_reduce(mx[:, 2:4], ex, AX_X, ALU.add))
            link(v.reciprocal(mx[:, 4:6], mx[:, 2:4]))
            for tt in range(TT):
                link(v.tensor_scalar(gate[:, tt, :], ex[:, tt, :], mx[:, 4 + tt:5 + tt], None, ALU.mult))
            dve.wait_ge(s_pos, 1)
            pos = psum[7][:, 0:TT * NE].rearrange("p (t e) -> p t e", t=TT)
            link(v.scalar_tensor_tensor(tmp, pos, 1.0, sel, ALU.add, ALU.mult))
            link(v.tensor_scalar(posm, tmp, -1.0, None, ALU.add))
            link(v.tensor_scalar(rt[:, 7, 0:NE], psum[7][:, 2 * NE:3 * NE], P + 0.5, 1.0, ALU.is_gt, ALU.add))
            link(v.tensor_copy(nbk[:, :], rt[:, 7, 0:NE]))
            dve.wait_ge(s_g2, 1)
            dve.sem_inc(s_rt, 1)

            def expert(e, nb):
                inc = 2 // nb
                for u in range(ECH * nb):
                    dve.wait_ge(s_esl, e * (2 * ECH) + (u + 1) * inc)
                    dve.wait_ge(s_e3, e * (2 * ECH) + (u + 1) * inc)
                    if u:
                        dve.wait_ge(s_et, e * (2 * ECH) + u * inc)
                    v.tensor_tensor(hid_e, silu_e, psum[1][:, :], ALU.mult).then_inc(s_ea, inc)
                dve.wait_ge(w2_used, (e + 1) * ECH)
                for b in range(nb):
                    for half in range(2):
                        last = v.tensor_tensor(y_sb[:, b, half * 512:(half + 1) * 512], psum[2 + 2 * b + half][:, :],
                                               g2bc[:, half * 512:(half + 1) * 512], ALU.mult)
                        if half == 1:
                            last.then_inc(s_eye, inc)
                for n in range(4):
                    tt, half = divmod(n, 2)
                    dve.wait_ge(s_sct, e * 4 + n + 1)
                    dst = x_acc[:, tt, half * 512:(half + 1) * 512]
                    v.tensor_tensor(dst, dst, psum[6 + n % 2][:, :], ALU.add).then_inc(s_add, 1)

            with dve.Fori(0, NE) as e:
                for tt in range(TT):
                    v.tensor_scalar(Pm[:, tt, :], slot_no[:], posm[:, tt, bass.ds(e, 1)], None, ALU.is_equal)
                    last = v.tensor_scalar(Pg[:, tt, :], slot_no[:], posm[:, tt, bass.ds(e, 1)],
                                           gate[:, tt, bass.ds(e, 1)], ALU.is_equal, ALU.mult)
                last.then_inc(s_P, 1)
                nb = dve.value_load(nbk[0:1, bass.ds(e, 1)], min_val=1, max_val=2)
                for n in (1, 2):
                    with dve.If(nb == n):
                        expert(e, n)
                dve.wait_ge(s_add, e * 4 + 4)


INPUTS = ["x", "c", "ada_w", "ada_b", "norm1_g", "norm2_g", "da_w_in", "da_q_gain", "da_k_gain", "da_lam_q1",
          "da_lam_k1", "da_lam_q2", "da_lam_k2", "da_subln_g", "da_w_out", "gla_w_in", "gla_w_a1", "gla_w_a2",
          "gla_b_a", "gla_out_g", "gla_w_out", "ffn_w1", "ffn_w3", "ffn_w2", "moe_router", "moe_w1", "moe_w3",
          "moe_w2"]


def kernel(**inputs):
    import numpy as np
    import concourse.bacc as bacc
    from concourse.bass_utils import run_bass_kernel_spmd

    nc = bacc.Bacc("TRN2", target_bir_lowering=False, num_devices=1)
    arrays, t = {}, {}
    for name in INPUTS:
        a = np.ascontiguousarray(inputs[name])
        if name in ("moe_w1", "moe_w3", "moe_w2"):
            a = a[0]
        arrays[f"in_{name}"] = a
        t[name] = nc.dram_tensor(f"in_{name}", a.shape, mybir.dt.from_np(a.dtype), kind="ExternalInput").ap()
    t["out"] = nc.dram_tensor("out_x", (1, S, D), F32, kind="ExternalOutput").ap()
    build(nc, t)
    r = run_bass_kernel_spmd(nc, [arrays], core_ids=[0])
    return r.results[0]["out_x"]
```

```python
import math
from contextlib import ExitStack

import concourse.bass as bass
from concourse import mybir

ALU = mybir.AluOpType
ACT = mybir.ActivationFunctionType
AX_X = mybir.AxisListType.X
F32 = mybir.dt.float32
F32R = mybir.dt.float32r
I32 = mybir.dt.int32

P = 128
D = 1024
S = 256
TT = S // P
KT = D // P
CHUNK = 64
EPS = 1e-6
H = 8
DH = 64
LAMBDA_INIT = 0.8 - 0.6 * math.exp(-0.3 * 0)
GH = 4
DV = D // GH
NC = S // CHUNK
GLA_RANK = 16
GLA_TAU = 16.0
FFN = 2816
FT = FFN // P
NE = 8
EF = 3584
FW = 512
FPC = FW // P
ECH = EF // FW
NCH = (FFN + FW - 1) // FW
HIDDEN = -1e30

SLOTS = 7
SLOT = KT * FW
SUB = 1024
PPC = SLOT // SUB
PIECES = 3
AHEAD = PIECES - 1


def stream_before_experts():
    ada = iter([("ada0", i) for i in range(12)] + [("ada1", i) for i in range(12)])
    order = [next(ada) for _ in range(4)]
    for i in range(6):
        order += [("in0", i), next(ada)]
    order += [("out0", i) for i in range(2)]
    for f in range(NCH):
        order += [("w1", f), next(ada), ("w3", f), next(ada)]
        if f:
            order += [("w2", f - 1)]
    order += [("w2", NCH - 1)]
    for i in range(6):
        order += [("in1", i)]
        if i < 2:
            order += [next(ada)]
    return order + [("out1", i) for i in range(2)]


def stream_of_expert():
    order = []
    for c in range(ECH):
        order += [("w1", c), ("w3", c)]
        if c:
            order += [("w2", c - 1)]
    return order + [("w2", ECH - 1)]


def build(nc, t):
    order = stream_before_experts()
    index = {key: i for i, key in enumerate(order)}
    PRE = len(order)
    eorder = stream_of_expert()
    PER = len(eorder)
    EQ = PER * PPC
    assert PER % SLOTS == 0 and EQ % PIECES == 0
    last_piece = {key: PPC * i + PPC - 1 for i, key in enumerate(eorder)}
    turn_at = {last_piece["w3", c] + 2: c for c in range(ECH)}
    proj_rank = {k: i + 1 for i, k in enumerate([k for k in order if k[0][:-1] in ("in", "out")])}
    ada_rank = {k: i + 1 for i, k in enumerate([k for k in order if k[0].startswith("ada")])}

    ROOT = {"norm0": 0, "qk": 1, "sub": 9, "norm1": 13, "norm2": 14, "gla": 15, "norm3": 19}

    with ExitStack() as ctx:
        def sb(name, shape, dt=F32):
            return ctx.enter_context(nc.sbuf_tensor(name, shape, dt))

        def sem(name):
            return ctx.enter_context(nc.semaphore(name))

        with ExitStack() as ahead_of_experts:
            def sb_ahead(name, shape):
                return ahead_of_experts.enter_context(nc.sbuf_tensor(name, shape, F32))

            xT = sb_ahead("xT", [P, KT, S])
            hT = sb_ahead("hT", [P, KT, S])
            sq = sb_ahead("sq", [P, KT, S])
            rstd = sb_ahead("rstd", [P, KT, S])
            V = sb_ahead("V", [P, TT, D])
            halves = sb_ahead("halves", [P, P])
            tri = sb_ahead("tri", [P, P])
            dist = sb_ahead("dist", [P, S])
            bT = sb_ahead("bT", [P, GH, S])
            dd = sb_ahead("dd", [P, GH, S])
        w_hi = sb("w_hi", [P, PIECES, SUB], F32R)
        w_lo = sb("w_lo", [P, PIECES, SUB], F32R)
        hg_hi = sb("hg_hi", [P, KT, S], F32R)
        hg_lo = sb("hg_lo", [P, KT, S], F32R)
        hid_hi = sb("hid_hi", [P, 2, 2, FW], F32R)
        hid_lo = sb("hid_lo", [P, 2, 2, FW], F32R)
        ring = sb("ring", [P, SLOTS, SLOT])
        ident = sb("ident", [P, P])
        ones = sb("ones", [P, P])
        before = sb("before", [P, P])
        slot_no = sb("slot_no", [P, S])
        lower_e = sb("lower_e", [P, NE, NE])
        NPAR = 8 + 16 + 16 + 96 + 5
        par = sb("par", [P, NPAR])
        C0, N1, N2, AB, QG = 0, 8, 24, 40, 136
        c_act = sb("c_act", [P, KT])
        lam = sb("lam", [P, 4])
        router = sb("router", [P, KT, NE])
        mod = sb("mod", [P, 2, 48])
        ada_acc = sb("ada_acc", [P, 2, 1024])
        cols = sb("cols", [P, 4, KT])
        eps = sb("eps", [P, 4])
        gq = sb("gq", [P, 8])
        bufA = sb("bufA", [P, KT, S])
        bufB = sb("bufB", [P, KT, S])
        oT = sb("oT", [P, KT, S])
        work = sb("work", [P, 2, 2048])
        small = sb("small", [P, 2, 16])
        nbk = sb("nbk", [P, NE], I32)
        nbp = sb("nbp", [P, NE], I32)
        gate = sb("gate", [P, TT, NE + 1])
        posx = sb("posx", [P, TT, NE + 1])

        psum = [ctx.enter_context(nc.psum_tensor(f"bank{i}", [P, 512], F32)) for i in range(8)]

        s_small = sem("s_small")
        s_late = sem("s_late")
        landed = [sem(f"landed{i}") for i in range(SLOTS)]
        s_ada = sem("s_ada")
        ada_used = sem("ada_used")
        s_const = sem("s_const")
        s_constv = sem("s_constv")
        s_tp = sem("s_tp")
        s_par = sem("s_par")
        s_cact = sem("s_cact")
        s_xt = sem("s_xt")
        s_x = sem("s_x")
        s_modp = sem("s_modp")
        s_mod = sem("s_mod")
        s_sq = sem("s_sq")
        s_ssq = sem("s_ssq")
        s_root = sem("s_root")
        s_hp = sem("s_hp")
        s_h = sem("s_h")
        s_fill = sem("s_fill")
        s_evac = sem("s_evac")
        s_qsq = sem("s_qsq")
        s_qss = sem("s_qss")
        s_qn = sem("s_qn")
        s_lam = sem("s_lam")
        s_lame = sem("s_lame")
        s_sc = sem("s_sc")
        s_mx = sem("s_mx")
        s_ex = sem("s_ex")
        s_pd = sem("s_pd")
        s_pt = sem("s_pt")
        s_pte = sem("s_pte")
        s_o = sem("s_o")
        s_oe = sem("s_oe")
        s_oss = sem("s_oss")
        s_on = sem("s_on")
        s_h13 = sem("s_h13")
        s_silu = sem("s_silu")
        s_hid = sem("s_hid")
        s_hidu = sem("s_hidu")
        s_a1 = sem("s_a1")
        s_a1e = sem("s_a1e")
        s_z = sem("s_z")
        s_zb = sem("s_zb")
        s_ln = sem("s_ln")
        s_la = sem("s_la")
        s_b = sem("s_b")
        s_be = sem("s_be")
        s_dd = sem("s_dd")
        s_ed = sem("s_ed")
        s_qd = sem("s_qd")
        s_kdt = sem("s_kdt")
        s_kde = sem("s_kde")
        s_am = sem("s_am")
        s_ame = sem("s_ame")
        s_kv = sem("s_kv")
        s_st = sem("s_st")
        s_go = sem("s_go")
        s_goe = sem("s_goe")
        s_gss = sem("s_gss")
        s_gn = sem("s_gn")
        s_lg = sem("s_lg")
        s_sel = sem("s_sel")
        s_pos = sem("s_pos")
        s_rt = sem("s_rt")
        s_ht = sem("s_ht")
        s_hte = sem("s_hte")
        s_dg = sem("s_dg")
        s_g2 = sem("s_g2")
        s_g2e = sem("s_g2e")
        s_y = sem("s_y")
        w2f_used = sem("w2f_used")
        s_lgm = sem("s_lgm")
        s_rexp = sem("s_rexp")
        hi_done = sem("hi_done")
        lo_done = sem("lo_done")
        w_free = sem("w_free")
        s_P = sem("s_P")
        s_gt = sem("s_gt")
        s_gh = sem("s_gh")
        s_gl = sem("s_gl")
        s_gg = sem("s_gg")
        s_gge = sem("s_gge")
        s_esl = sem("s_esl")
        s_ea = sem("s_ea")
        s_et = sem("s_et")
        s_hdh = sem("s_hdh")
        s_hdl = sem("s_hdl")
        s_eye = sem("s_eye")
        s_sct = sem("s_sct")
        s_add = sem("s_add")
        s_out = sem("s_out")
        s_chain = sem("s_chain")
        s_achain = sem("s_achain")
        s_gchain = sem("s_gchain")

        dist_i = sq[:, 0, :].bitcast(I32)
        slot_i = sq[:, 1, :].bitcast(I32)
        row_a, row_b = sq[:, 2, 0:P], sq[:, 3, 0:P]
        lam_in = sq[:, 4, :].rearrange("p (j d) -> p j d", j=4)
        lam_pr = sq[:, 5, 0:2 * DH].rearrange("p (j d) -> p j d", j=2)
        ba_row = bufB[:, 0:2, :].rearrange("p a s -> p (a s)")
        wa2 = bufB[0:GLA_RANK, 2:4, :].rearrange("p a s -> p (a s)")
        wa1 = bufB[:, 4, 0:KT * GLA_RANK].rearrange("p (k n) -> p k n", k=KT)
        x_rows = work[:, :, 0:D]
        def att(h):
            w = work[:, h % 2, :]
            return {"t1": w[:, 0:512].rearrange("p (m s) -> p m s", m=2),
                    "t0": w[:, 512:768].rearrange("p (m s) -> p m s", m=2),
                    "d1": w[:, 768:1024], "d0": w[:, 1024:1152], "pt": w[:, 1152:1536]}
        hid = work
        silu_f = rstd
        la = work[:, 0, 0:1024].rearrange("p (t c) -> p t c", t=TT)
        lz = work[:, 1, 0:1024].rearrange("p (t c) -> p t c", t=TT)
        le = work[:, 1, 1024:2048].rearrange("p (t c) -> p t c", t=TT)
        a1T = work[0:GLA_RANK, 0, 1024:1280]
        gq_t, gk_t = bufA[:, 0:GH, :], bufA[:, GH:2 * GH, :]
        eb = rstd[:, 0:GH, :]
        ei = rstd[:, GH:2 * GH, :]
        qd = sq[:, 0:GH, :]
        ki = sq[:, GH:2 * GH, :]
        kd = oT[:, 0:GH, :]
        kdt = work[:, 0, 0:1024].rearrange("p (g c) -> p g c", g=8)
        am = work[:, 1, 0:1024].rearrange("p (g c) -> p g c", g=8)
        state = [w.rearrange("p (g v) -> p g v", g=GH)
                 for w in (ada_acc[:, 0, :], ada_acc[:, 1, :], work[:, 1, 1024:2048])]
        x_acc = oT[:, :, :].rearrange("p (t k) s -> p t (k s)", t=TT)
        h_tok = bufA[:, :, :].rearrange("p (t k) s -> p t (k s)", t=TT)
        y_sb = bufB[:, :, :].rearrange("p (t k) s -> p t (k s)", t=TT)
        g2bc = work[:, 0, 0:1024]
        silu_e = work[:, 0, 1024:2048].rearrange("p (b n) -> p b n", b=2)
        hid_e = ada_acc[:, 0, :].rearrange("p (b n) -> p b n", b=2)
        diag = work[:, 1, 512:1536].rearrange("p (k c) -> p k c", k=KT)
        Pm = work[:, 1, 512:1024].rearrange("p (t s) -> p t s", t=TT)
        Pg = work[:, 1, 1024:1536].rearrange("p (t s) -> p t s", t=TT)
        PgT = work[:, 1, 1536:2048].rearrange("p (b s) -> p b s", b=2)
        rt = sb("rt", [P, 9, TT * NE])
        cmp_a = ada_acc[:, 0, 0:128].rearrange("p (t e o) -> p t e o", t=TT, e=NE)
        cmp_b = ada_acc[:, 0, 128:256].rearrange("p (t e o) -> p t e o", t=TT, e=NE)

        def slot(i, n=SLOT):
            return ring[:, i % SLOTS, 0:n]

        def chunk_in(w, c0, n):
            return w[:, c0:c0 + n].rearrange("(k p) n -> p k n", p=P)

        def ffn_width(f):
            return min(FW, FFN - f * FW)

        def source(key):
            kind, i = key
            if kind.startswith("ada"):
                return chunk_in(t["ada_w"][int(kind[3])], i * FW, FW), KT, FW
            if kind == "in0":
                return chunk_in(t["da_w_in"][0], i * FW, FW), KT, FW
            if kind == "in1":
                return chunk_in(t["gla_w_in"][0], i * FW, FW), KT, FW
            if kind == "out0":
                return chunk_in(t["da_w_out"][0], i * FW, FW), KT, FW
            if kind == "out1":
                return chunk_in(t["gla_w_out"][0], i * FW, FW), KT, FW
            n = ffn_width(i)
            if kind == "w2":
                return t["ffn_w2"][0][i * FW:i * FW + n, :].rearrange("(k p) n -> p k n", p=P), n // P, D
            return chunk_in(t["ffn_" + kind][0], i * FW, n), KT, n

        def slot_view(i, k, n):
            return ring[:, i % SLOTS, 0:k * n].rearrange("p (k n) -> p k n", k=k)

        def expert_source(e, i):
            what, c = eorder[i]
            if what == "w2":
                w = t["moe_w2"].rearrange("e (c k p) n -> e c p k n", p=P, k=FPC)
                return w[bass.ds(e, 1), c, :, :, :].rearrange("o p k n -> p (o k) n"), FPC, D
            w = t["moe_" + what].rearrange("e (k p) n -> e p k n", p=P)
            return w[bass.ds(e, 1), :, :, c * FW:(c + 1) * FW].rearrange("o p k n -> p (o k) n"), KT, FW

        def raw_piece(q):
            i, p = divmod(q, PPC)
            return ring[:, (PRE + i) % SLOTS, p * SUB:(p + 1) * SUB]

        def wait_landed(eng, i, e=0):
            if isinstance(e, int):
                eng.wait_ge(landed[i % SLOTS], 16 * (i // SLOTS + 1 + e * (PER // SLOTS)))
            else:
                eng.wait_ge(landed[i % SLOTS], e * (16 * PER // SLOTS) + 16 * (i // SLOTS + 1))

        block = ctx.enter_context(nc.Block())

        @block.sync
        def _(sp):
            sp.dma_start(x_rows, t["x"][0].rearrange("(t p) d -> p t d", p=P)).then_inc(s_small, 16)

            def rows(dst, r0, src, n):
                sp.dma_start(dst[r0:r0 + n, :], src).then_inc(s_small, 16)

            rows(row_a, 0, t["c"].rearrange("o (k p) -> (o k) p", p=P), 8)
            rows(row_a, 8, t["norm1_g"].rearrange("l (k p) -> (l k) p", p=P), 16)
            rows(row_a, 24, t["norm2_g"].rearrange("l (k p) -> (l k) p", p=P), 16)
            rows(row_a, 40, t["ada_b"][0:1].rearrange("l (k p) -> (l k) p", p=P), 48)
            rows(row_a, 88, t["da_q_gain"].rearrange("o m d -> o (m d)"), 1)
            rows(row_a, 89, t["da_k_gain"].rearrange("o m d -> o (m d)"), 1)
            rows(row_a, 90, t["da_subln_g"], 1)
            rows(row_a, 91, t["gla_out_g"].rearrange("o (k p) -> (o k) p", p=P), 2)
            rows(row_b, 0, t["ada_b"][1:2].rearrange("l (k p) -> (l k) p", p=P), 48)
            for j, name in enumerate(("da_lam_q1", "da_lam_k1", "da_lam_q2", "da_lam_k2")):
                sp.dma_start(lam_in[:, j, :], t[name][0:1, :].to_broadcast([P, DH])).then_inc(s_small, 16)

            def wait_used(key):
                kind, f = key
                if kind.startswith("ada"):
                    sp.wait_ge(ada_used, ada_rank[key])
                elif kind == "w2":
                    sp.wait_ge(w2f_used, f + 1)
                elif kind in ("w1", "w3"):
                    sp.wait_ge(s_h13, min((f + 1) * FPC, FT))
                else:
                    sp.wait_ge(s_fill, 2 * proj_rank[key])

            def load(i, key):
                if i >= SLOTS:
                    wait_used(order[i - SLOTS])
                src, k, n = source(key)
                sp.dma_start(slot_view(i, k, n), src).then_inc(landed[i % SLOTS], 16)

            for i, key in enumerate(order):
                load(i, key)
                if key == ("w1", 1):
                    sp.wait_ge(s_pt, H)
                    sp.dma_start(ba_row[:, :], t["gla_b_a"][0:1, :].to_broadcast([P, 512])).then_inc(s_late, 16)
                    sp.dma_start(wa1[:, :, :], t["gla_w_a1"][0].rearrange("(k p) n -> p k n", p=P)).then_inc(s_late, 16)
                    sp.dma_start(wa2[:, :], t["gla_w_a2"][0]).then_inc(s_late, 16)
                    sp.dma_start(router[:, :, :], t["moe_router"][0].rearrange("(k p) n -> p k n", p=P)).then_inc(s_late, 16)

            def load_expert(e, i, first=False):
                j = i - SLOTS
                if first:
                    wait_used(order[PRE + j])
                else:
                    back, j = (0, j) if j >= 0 else (-1, j + PER)
                    sp.wait_ge(lo_done, (e + back) * EQ + (j + 1) * PPC)
                src, k, n = expert_source(e, i)
                sp.dma_start(slot_view(PRE + i, k, n), src).then_inc(landed[(PRE + i) % SLOTS], 16)

            for i in range(SLOTS):
                load_expert(0, i, first=True)
            with sp.Fori(0, NE - 1) as e:
                for i in range(SLOTS, PER):
                    load_expert(e, i)
                for i in range(SLOTS):
                    load_expert(e + 1, i)
            for i in range(SLOTS, PER):
                load_expert(NE - 1, i)
            sp.wait_ge(s_add, 4 * (NE + 1))
            sp.dma_start(t["out"][0].rearrange("(t p) d -> p t d", p=P), x_acc).then_inc(s_out, 16)
            sp.wait_ge(s_out, 16)

        @block.gpsimd
        def _(pool):
            n = [0]

            def link(ins):
                n[0] += 1
                ins.then_inc(s_gchain, 1)
                pool.wait_ge(s_gchain, n[0])

            nc.gpsimd.memset(ident[:], 0.0).then_inc(s_gchain, 1)
            nc.gpsimd.memset(ones[:], 1.0).then_inc(s_gchain, 1)
            nc.gpsimd.memset(halves[:], 0.0).then_inc(s_gchain, 1)
            nc.gpsimd.memset(lower_e[:], 1.0).then_inc(s_gchain, 1)
            n[0] = 4
            pool.wait_ge(s_gchain, 4)
            link(nc.gpsimd.affine_select(out=ident[:], in_=ident[:], compare_op=ALU.not_equal, fill=1.0, base=0,
                                         pattern=[[-1, P]], channel_multiplier=1))
            link(nc.gpsimd.memset(halves[0:64, 0:64], 1.0))
            link(nc.gpsimd.memset(halves[64:128, 64:128], 1.0))
            link(nc.gpsimd.affine_select(out=tri[:], in_=halves[:], compare_op=ALU.is_ge, fill=0.0, base=0,
                                         pattern=[[1, P]], channel_multiplier=-1))
            link(nc.gpsimd.affine_select(out=before[:], in_=ones[:], compare_op=ALU.is_gt, fill=0.0, base=0,
                                         pattern=[[1, P]], channel_multiplier=-1))
            link(nc.gpsimd.affine_select(out=lower_e[:], in_=lower_e[:], compare_op=ALU.is_gt, fill=0.0, base=0,
                                         pattern=[[1, NE], [-1, NE]], channel_multiplier=0))
            link(nc.gpsimd.iota(dist_i, pattern=[[-1, S]], base=P, channel_multiplier=1))
            link(nc.gpsimd.iota(slot_i, pattern=[[1, S]], base=0, channel_multiplier=0))
            for j, width in enumerate((D, DH, P, DV)):
                last = nc.gpsimd.memset(eps[:, j:j + 1], width * EPS)
            last.then_inc(s_const, 1)

        @block.tensor
        def _(pe):
            mm = nc.tensor.matmul
            fill = [0]
            pe.wait_ge(s_const, 1)

            pe.wait_ge(s_small, 16 * 14)
            nc.tensor.transpose(psum[7][:, 0:93], row_a[0:93, :], ident[0:93, 0:93])
            nc.tensor.transpose(psum[7][:, 128:176], row_b[0:48, :], ident[0:48, 0:48]).then_inc(s_tp, 1)
            for b in range(4):
                for j in range(2):
                    for i in range(TT):
                        last = nc.tensor.transpose(psum[b][:, j * S + i * P:j * S + (i + 1) * P],
                                                   x_rows[:, i, (2 * b + j) * P:(2 * b + j + 1) * P], ident[:])
                last.then_inc(s_xt, 1)

            def mod_columns(l, third):
                n = 6 * l + third
                pe.wait_ge(ada_used, 2 * n + 2)
                if n:
                    pe.wait_ge(s_mod, n)
                for j in range(8):
                    last = mm(psum[7][:, 256 + 48 * l + 8 * third + j:257 + 48 * l + 8 * third + j],
                              ada_acc[:, n % 2, j * P:(j + 1) * P], ones[:, 0:1], start=True, stop=True)
                last.then_inc(s_modp, 1)

            def norm_sums(n):
                for k in range(KT):
                    pe.wait_ge(s_sq, 8 * n + k + 1)
                    last = mm(psum[6][:, 0:S], ones[:], sq[:, k, :], start=(k == 0), stop=(k == KT - 1))
                last.then_inc(s_ssq, 1)

            def half_project(key, ready, token_major, g):
                i = index[key]
                w = slot_view(i, KT, FW)
                wait_landed(pe, i)
                src, signal, base = ready
                f = fill[0]
                if f >= 4:
                    pe.wait_ge(s_evac, f - 3)
                if token_major:
                    for k in range(KT):
                        pe.wait_ge(signal, base + k + 1)
                        last = mm(psum[f % 4][:, :], src[:, k, g * P:(g + 1) * P], w[:, k, :],
                                  start=(k == 0), stop=(k == KT - 1))
                else:
                    for j in range(2):
                        for k in range(KT):
                            pe.wait_ge(signal, base + k + 1)
                            m = 2 * g + j
                            last = mm(psum[f % 4][:, j * S:(j + 1) * S], w[:, k, m * P:(m + 1) * P], src[:, k, :],
                                      start=(k == 0), stop=(k == KT - 1))
                last.then_inc(s_fill, 1)
                fill[0] += 1

            def project(key, ready, token_major):
                for g in range(2):
                    half_project(key, ready, token_major, g)

            def qk_sums(f):
                pe.wait_ge(s_qsq, f + 1)
                if f >= 2:
                    pe.wait_ge(s_root, ROOT["qk"] + f - 1)
                mm(psum[4 + f % 2][:, :], halves[:], sq[:, 2 * (f % 4):2 * (f % 4) + 2, :],
                   start=True, stop=True).then_inc(s_qss, 1)

            pe.wait_ge(s_par, 1)
            mod_columns(0, 0)
            mod_columns(0, 1)
            norm_sums(0)
            for i in range(6):
                project(("in0", i), (hT, s_h, 0), token_major=(i >= 4))
                if 1 <= i <= 4:
                    qk_sums(2 * (i - 1))
                    qk_sums(2 * (i - 1) + 1)
                if i in (2, 4):
                    mod_columns(0, 1 + i // 2)
            mod_columns(0, 4)

            def scores(h):
                if h >= 2:
                    pe.wait_ge(s_mx, h - 1)
                for m in range(2):
                    q = bufA[m * DH:(m + 1) * DH, h, :]
                    k = bufB[m * DH:(m + 1) * DH, h, :]
                    mm(psum[2 * (h % 2) + m][:, 0:S], q[:, P:S], k, start=True, stop=True)
                    last = mm(psum[2 * (h % 2) + m][:, S:S + P], q[:, 0:P], k[:, 0:P], start=True, stop=True)
                last.then_inc(s_sc, 1)

            def turn_map(h):
                a = att(h)
                pe.wait_ge(s_pd, h + 1)
                if h >= 1:
                    pe.wait_ge(s_pte, h)
                nc.tensor.transpose(psum[4][:, 0:P], a["d0"], ident[:])
                nc.tensor.transpose(psum[4][:, P:2 * P], a["d1"][:, 0:P], ident[:])
                nc.tensor.transpose(psum[4][:, 2 * P:3 * P], a["d1"][:, P:S], ident[:]).then_inc(s_pt, 1)

            def attend(h):
                a = att(h)
                pe.wait_ge(s_pte, h + 1)
                if h >= 1:
                    pe.wait_ge(s_oe, h)
                mm(psum[5][:, 0:S], V[:, 0, h * P:(h + 1) * P], a["pt"][:, 0:S], start=True, stop=False)
                mm(psum[5][:, P:S], V[:, 1, h * P:(h + 1) * P], a["pt"][:, S:S + P], start=False,
                   stop=True).then_inc(s_o, 1)

            def head_sums(g):
                pe.wait_ge(s_oe, 2 * g + 2)
                if g:
                    pe.wait_ge(s_root, ROOT["sub"] + g)
                mm(psum[6][:, :], ones[:], sq[:, 2 * g:2 * g + 2, :], start=True, stop=True).then_inc(s_oss, 1)

            pe.wait_ge(s_qn, 8)
            pe.wait_ge(s_evac, 12)
            scores(0)
            scores(1)
            for h in range(H):
                if h + 2 < H:
                    scores(h + 2)
                turn_map(h)
                if h >= 3 and h % 2 == 1:
                    head_sums((h - 3) // 2)
                attend(h)
            head_sums(3)
            pe.wait_ge(s_mx, H)
            for i in range(2):
                project(("out0", i), (oT, s_on, 0), False)

            norm_sums(1)
            pe.wait_ge(s_evac, 16)

            def hidden(f, what, j):
                i = index[(what, f)]
                w = slot_view(i, KT, ffn_width(f))
                wait_landed(pe, i)
                o = 0 if what == "w1" else S
                g = f * FPC + j
                if o == 0 and g >= 2:
                    pe.wait_ge(s_hid, g - 1)
                for k in range(KT):
                    pe.wait_ge(s_h, 8 + k + 1)
                    last = mm(psum[4 + g % 2][:, o:o + S], w[:, k, j * P:(j + 1) * P], hT[:, k, :],
                              start=(k == 0), stop=(k == KT - 1))
                return last

            def ffn_out(f):
                n = ffn_width(f) // P
                i = index[("w2", f)]
                w = slot_view(i, n, D)
                wait_landed(pe, i)
                pe.wait_ge(s_hid, f * FPC + n)
                for j in range(n):
                    for m in range(KT):
                        last = mm(psum[m // 2][:, (m % 2) * S:(m % 2 + 1) * S], w[:, j, m * P:(m + 1) * P],
                                  hid[:, f % 2, j * S:(j + 1) * S], start=(f == 0 and j == 0 and m % 2 == 0),
                                  stop=(f == NCH - 1 and j == n - 1), skip_group_check=True)
                        if f == NCH - 1 and j == n - 1 and m in (1, 3, 5):
                            last.then_inc(s_y, 1)
                last.then_inc(w2f_used, 1)

            for f in range(NCH):
                n = ffn_width(f) // P
                for j in range(n):
                    a = hidden(f, "w1", j)
                    b = hidden(f, "w3", j)
                    b.then_inc(s_h13, 1)
                if f:
                    ffn_out(f - 1)
                    mod_columns(*((0, 5) if f == 1 else (1, f - 2)))
            ffn_out(NCH - 1)
            mod_columns(1, 4)

            norm_sums(2)
            pe.wait_ge(s_late, 64)
            for k in range(KT):
                pe.wait_ge(s_h, 16 + k + 1)
                last = mm(psum[4][0:GLA_RANK, 0:S], wa1[:, k, :], hT[:, k, :], start=(k == 0), stop=(k == KT - 1))
            last.then_inc(s_a1, 1)
            h2 = (hT, s_h, 16)
            project(("in1", 0), h2, False)
            pe.wait_ge(s_a1e, 1)
            for tt in range(TT):
                mm(psum[4 + tt][:, :], a1T[:, tt * P:(tt + 1) * P], wa2[:, :], start=True,
                   stop=True).then_inc(s_z, 1)
            project(("in1", 1), h2, False)
            pe.wait_ge(s_la, 1)
            for g in range(GH):
                for tt in range(TT):
                    o = (g % 2) * S + tt * P
                    last = mm(psum[4 + g // 2][:, o:o + P], la[:, tt, g * P:(g + 1) * P], tri[:],
                              start=True, stop=True)
            last.then_inc(s_b, 1)
            project(("in1", 2), h2, True)
            mod_columns(1, 5)
            pe.wait_ge(s_qd, 3)
            for g in range(GH):
                for tt in range(TT):
                    n = g * TT + tt
                    last = nc.tensor.transpose(psum[4 + n // 4][:, (n % 4) * P:(n % 4 + 1) * P],
                                               kd[:, g, tt * P:(tt + 1) * P], ident[:])
            last.then_inc(s_kdt, 1)
            project(("in1", 3), h2, True)
            pe.wait_ge(s_kde, 1)
            for g in range(GH):
                for tt in range(TT):
                    n = g * TT + tt
                    last = mm(psum[4 + n // 4][:, (n % 4) * P:(n % 4 + 1) * P], ki[:, g, tt * P:(tt + 1) * P],
                              qd[:, g, tt * P:(tt + 1) * P], start=True, stop=True)
            last.then_inc(s_am, 1)

            def chunk_state(c):
                r0, tt = (c % 2) * CHUNK, c // 2
                if c:
                    pe.wait_ge(s_st, c)
                else:
                    pe.wait_ge(s_ame, 1)
                for g in range(GH):
                    last = mm(psum[4 + g // 2][:, (g % 2) * DV:(g % 2 + 1) * DV], kdt[r0:r0 + CHUNK, g * TT + tt, :],
                              V[r0:r0 + CHUNK, tt, g * DV:(g + 1) * DV], start=True, stop=True)
                last.then_inc(s_kv, 1)

            project(("in1", 4), h2, False)
            pe.wait_ge(s_evac, 24)
            chunk_state(0)
            half_project(("in1", 5), h2, False, 0)
            chunk_state(1)
            half_project(("in1", 5), h2, False, 1)
            chunk_state(2)

            def head_out_sums(g):
                pe.wait_ge(s_goe, g + 1)
                if g == 3:
                    pe.wait_ge(s_mod, 12)
                for v in range(2):
                    last = mm(psum[4 + g][:, 0:S], ones[:], rstd[:, 2 * g + v, :],
                              start=(v == 0), stop=(v == 1))
                last.then_inc(s_gss, 1)

            for g in range(GH):
                pe.wait_ge(s_evac, 25 + g)
                for v in range(2):
                    for tt in range(TT):
                        o = v * S + tt * P
                        mm(psum[g][:, o:o + P], V[:, tt, g * DV + v * P:g * DV + (v + 1) * P], am[:, g * TT + tt, :],
                           start=(v == 0 and tt == 0), stop=False, skip_group_check=True)
                if g == 0:
                    pe.wait_ge(s_st, NC - 1)
                for v in range(2):
                    for c in range(1, NC):
                        o = v * S + c * CHUNK
                        last = mm(psum[g][:, o:o + CHUNK], state[c - 1][:, g, v * P:(v + 1) * P],
                                  qd[:, g, c * CHUNK:(c + 1) * CHUNK], start=False, stop=True, skip_group_check=True)
                last.then_inc(s_go, 1)
                if g:
                    head_out_sums(g - 1)
            head_out_sums(GH - 1)
            for i in range(2):
                project(("out1", i), (oT, s_gn, 0), False)

            norm_sums(3)
            for tt in range(TT):
                for k in range(KT):
                    pe.wait_ge(s_h, 24 + k + 1)
                    last = mm(psum[4][:, tt * NE:(tt + 1) * NE], hT[:, k, tt * P:(tt + 1) * P], router[:, k, :],
                              start=(k == 0), stop=(k == KT - 1))
            last.then_inc(s_lg, 1)
            pe.wait_ge(s_evac, 32)
            for n, src in enumerate((hT, xT)):
                for b in range(4):
                    if n:
                        pe.wait_ge(s_hte, b + 1)
                    tt, half = divmod(b, 2)
                    for k in range(4):
                        last = nc.tensor.transpose(psum[b][:, k * P:(k + 1) * P],
                                                   src[:, half * 4 + k, tt * P:(tt + 1) * P], ident[:])
                    last.then_inc(s_ht, 1)
            pe.wait_ge(s_dg, 1)
            for k in range(KT):
                last = mm(psum[5 + k // 4][:, (k % 4) * P:(k % 4 + 1) * P], ones[:], diag[:, k, :], start=True, stop=True)
            last.then_inc(s_g2, 1)
            pe.wait_ge(s_sel, 1)
            selT = rt[:, 0, :].rearrange("p (t e) -> p t e", t=TT)
            mm(psum[7][:, 0:NE], before[:], selT[:, 0, :], start=True, stop=True)
            mm(psum[7][:, NE:2 * NE], before[:], selT[:, 1, :], start=True, stop=False)
            mm(psum[7][:, NE:2 * NE], ones[:], selT[:, 0, :], start=False, stop=True)
            mm(psum[7][:, 2 * NE:3 * NE], ones[:], selT[:, 0, :], start=True, stop=False)
            mm(psum[7][:, 2 * NE:3 * NE], ones[:], selT[:, 1, :], start=False, stop=True).then_inc(s_pos, 1)
            pe.wait_ge(s_rt, 1)
            pe.wait_ge(s_hte, 8)
            pe.wait_ge(s_g2e, 2)

            pe.sem_inc(w_free, PIECES)

            def gather(e, nb):
                for g, bank in enumerate((0, 1, 6, 7)):
                    for k in range(2):
                        kk = 2 * g + k
                        for tt in range(TT):
                            last = mm(psum[bank][:, k * S:k * S + nb * P], h_tok[:, tt, kk * P:(kk + 1) * P],
                                      Pm[:, tt, 0:nb * P], start=(tt == 0), stop=(tt == TT - 1))
                    last.then_inc(s_gt, 1)

            def scatter(e, nb):
                pe.wait_ge(s_eye, e + 1)
                for n in range(4):
                    tt, half = divmod(n, 2)
                    for b in range(nb):
                        last = mm(psum[2 + n][:, :], PgT[:, b, tt * P:(tt + 1) * P],
                                  y_sb[:, b, half * 512:(half + 1) * 512], start=(b == 0), stop=(b == nb - 1))
                    last.then_inc(s_sct, 1)

            def gates_turned(e, nb):
                pe.wait_ge(s_gl, e * 4 + 4)
                for b in range(nb):
                    for tt in range(TT):
                        last = nc.tensor.transpose(psum[7][:, b * S + tt * P:b * S + (tt + 1) * P],
                                                   Pg[:, tt, b * P:(b + 1) * P], ident[:])
                last.then_inc(s_gg, 1)

            def expert(e, nb):
                for q in range(EQ):
                    i, p = divmod(q, PPC)
                    what, c = eorder[i]
                    pe.wait_ge(lo_done, e * EQ + q + 1)
                    if what == "w1":
                        if c == 0:
                            pe.wait_ge(s_gl, e * 4 + 4)
                        elif p == 0:
                            pe.wait_ge(s_esl, e * ECH + c)
                    elif what == "w3" and p == 0:
                        if c == 0:
                            pe.wait_ge(s_gge, e + 1)
                        else:
                            pe.wait_ge(s_hdl, e * ECH + c)
                    elif what == "w2" and p == 0:
                        if c == 0:
                            pe.wait_ge(s_add, e * 4 + 4)
                        pe.wait_ge(s_hdl, e * ECH + c + 1)
                    whi, wlo = w_hi[:, q % PIECES, :], w_lo[:, q % PIECES, :]
                    for b in range(nb):
                        for j in range(SUB // 512):
                            if what == "w2":
                                xs = slice(p * P, (p + 1) * P)
                                xhi, xlo = hid_hi[:, c % 2, b, xs], hid_lo[:, c % 2, b, xs]
                                out = psum[2 + 2 * b + j]
                                first, end = c == 0 and p == 0, c == ECH - 1 and p == PPC - 1
                            else:
                                k = 2 * p + j
                                xhi, xlo = hg_hi[:, k, b * P:(b + 1) * P], hg_lo[:, k, b * P:(b + 1) * P]
                                out = psum[(0 if what == "w1" else 6) + b]
                                first, end = k == 0, k == KT - 1
                            cs = slice(j * 512, (j + 1) * 512)
                            mm(out[:, :], xhi, whi[:, cs], start=first, stop=False)
                            mm(out[:, :], xhi, wlo[:, cs], start=False, stop=False)
                            last = mm(out[:, :], xlo, whi[:, cs], start=False, stop=end)
                    last.then_inc(w_free, 1)
                    if q in turn_at:
                        c = turn_at[q]
                        pe.wait_ge(s_ea, e * ECH + c + 1)
                        for b in range(nb):
                            for j in range(FPC):
                                last = nc.tensor.transpose(psum[6 + b][:, j * P:(j + 1) * P],
                                                           hid_e[:, b, j * P:(j + 1) * P], ident[:])
                        last.then_inc(s_et, 1)

            with pe.Fori(0, NE) as e:
                pe.wait_ge(s_P, e + 1)
                nb = pe.value_load(nbk[0:1, bass.ds(e, 1)], min_val=1, max_val=2)
                nb_before = pe.value_load(nbp[0:1, bass.ds(e, 1)], min_val=1, max_val=2)
                for n in (1, 2):
                    with pe.If(nb == n):
                        gather(e, n)
                for n in (1, 2):
                    with pe.If(nb_before == n):
                        scatter(e, n)
                for n in (1, 2):
                    with pe.If(nb == n):
                        gates_turned(e, n)
                        expert(e, n)
            nb_last = pe.value_load(nbk[0:1, NE - 1:NE], min_val=1, max_val=2)
            for n in (1, 2):
                with pe.If(nb_last == n):
                    scatter(NE, n)

        @block.scalar
        def _(act):
            A = nc.scalar.activation
            n_link = [0]

            def link(ins):
                n_link[0] += 1
                ins.then_inc(s_achain, 1)
                act.wait_ge(s_achain, n_link[0])

            act.wait_ge(s_par, 1)
            A(c_act[:], par[:, C0:C0 + KT], ACT.Silu).then_inc(s_cact, 1)
            act.wait_ge(s_lam, 1)
            A(lam[:, 2:4], lam[:, 0:2], ACT.Exp).then_inc(s_lame, 1)

            def squares(n):
                if n == 0:
                    act.wait_ge(s_constv, 1)
                for k in range(KT):
                    act.wait_ge(s_x, 8 * n + k + 1)
                    A(sq[:, k, :], xT[:, k, :], ACT.Square).then_inc(s_sq, 1)

            def shift(n):
                l, second = divmod(n, 2)
                c = 24 if second else 0
                act.wait_ge(s_mod, 6 * l + (4 if second else 1))
                for k in range(KT):
                    act.wait_ge(s_hp, 8 * n + k + 1)
                    A(hT[:, k, :], hT[:, k, :], ACT.Identity, bias=mod[:, l, c + k:c + k + 1]).then_inc(s_h, 1)

            def evac(f, dst, func=ACT.Copy):
                act.wait_ge(s_fill, f + 1)
                A(dst, psum[f % 4][:, :], func).then_inc(s_evac, 1)

            def root(dst, src, kind):
                A(dst, src, ACT.Sqrt, bias=eps[:, kind:kind + 1]).then_inc(s_root, 1)

            def norm_root(n):
                act.wait_ge(s_ssq, n + 1)
                root(rstd[:, 0, :], psum[6][:, 0:S], 0)

            def qk_root(f):
                act.wait_ge(s_qss, f + 1)
                if f >= 2:
                    act.wait_ge(s_qn, f - 1)
                root(rstd[:, 2 * (f % 2) + 2:2 * (f % 2) + 4, :], psum[4 + f % 2][:, :], 1)

            act.wait_ge(s_const, 1)
            squares(0)
            norm_root(0)
            shift(0)
            for f in range(8):
                act.wait_ge(s_fill, f + 1)
                if f < 4:
                    act.wait_ge(s_ssq, 1)
                else:
                    act.wait_ge(s_qss, f - 3)
                A(sq[:, 2 * (f % 4):2 * (f % 4) + 2, :], psum[f % 4][:, :], ACT.Square).then_inc(s_qsq, 1)
                evac(f, (bufA if f < 4 else bufB)[:, 2 * (f % 4):2 * (f % 4) + 2, :])
                if f >= 4:
                    qk_root(f - 4)
            for f in range(8, 12):
                evac(f, V[:, f % 2, ((f - 8) // 2) * 512:((f - 8) // 2 + 1) * 512])
                qk_root(f - 4)
            def exponentials(h):
                a = att(h)
                act.wait_ge(s_mx, h + 1)
                nm = small[:, h % 2, :]
                for m in range(2):
                    A(a["t1"][:, m, :], a["t1"][:, m, :], ACT.Exp, bias=nm[:, m:m + 1], accum_out=nm[:, 4 + m:5 + m])
                    last = A(a["t0"][:, m, :], a["t0"][:, m, :], ACT.Exp, bias=nm[:, 2 + m:3 + m],
                             accum_out=nm[:, 6 + m:7 + m])
                last.then_inc(s_ex, 1)

            def head_root(g):
                act.wait_ge(s_oss, g + 1)
                root(rstd[:, 2 * g:2 * g + 2, :], psum[6][:, :], 2)

            exponentials(0)
            for h in range(H):
                a = att(h)
                if h + 1 < H:
                    exponentials(h + 1)
                act.wait_ge(s_pt, h + 1)
                A(a["pt"], psum[4][:, 0:3 * P], ACT.Copy).then_inc(s_pte, 1)
                act.wait_ge(s_o, h + 1)
                if h == 0:
                    act.wait_ge(s_qss, 8)
                A(sq[:, h, :], psum[5][:, 0:S], ACT.Square)
                A(oT[:, h, :], psum[5][:, 0:S], ACT.Copy).then_inc(s_oe, 1)
                if h >= 3 and h % 2 == 1:
                    head_root((h - 3) // 2)
            head_root(3)
            squares(1)
            norm_root(1)
            shift(1)
            for g in range(FT):
                act.wait_ge(s_h13, g + 1)
                if g >= 8:
                    act.wait_ge(s_hid, g - 7)
                else:
                    act.wait_ge(s_hp, 16)
                A(silu_f[:, g % 8, :], psum[4 + g % 2][:, 0:S], ACT.Silu).then_inc(s_silu, 1)
            squares(2)
            norm_root(2)
            shift(2)
            act.wait_ge(s_a1, 1)
            A(a1T, psum[4][0:GLA_RANK, 0:S], ACT.Copy).then_inc(s_a1e, 1)
            for f in range(16, 20):
                evac(f, bufA[:, 2 * (f - 16):2 * (f - 16) + 2, :])
            act.wait_ge(s_zb, 2)
            A(le, le, ACT.Exp, scale=-1.0).then_inc(s_achain, 1)
            act.wait_ge(s_achain, 1)
            A(le, le, ACT.Ln, bias=ones[:, 0:1]).then_inc(s_ln, 1)
            act.wait_ge(s_b, 1)
            for g in range(2):
                A(bT[:, 2 * g:2 * g + 2, :], psum[4 + g][:, :], ACT.Copy)
                A(eb[:, 2 * g:2 * g + 2, :], psum[4 + g][:, :], ACT.Exp)
                A(ei[:, 2 * g:2 * g + 2, :], psum[4 + g][:, :], ACT.Exp, scale=-1.0).then_inc(s_be, 1)
            act.wait_ge(s_dd, 1)
            A(dd[:, :, :], dd[:, :, :], ACT.Exp).then_inc(s_ed, 1)
            for f in (20, 21):
                evac(f, V[:, f % 2, 0:512])
            act.wait_ge(s_kdt, 1)
            A(kdt[:, 0:4, :], psum[4][:, :], ACT.Copy)
            A(kdt[:, 4:8, :], psum[5][:, :], ACT.Copy).then_inc(s_kde, 1)
            for f in (22, 23):
                evac(f, V[:, f % 2, 512:1024])
            for f in range(24, 28):
                evac(f, bufB[:, 2 * (f - 24):2 * (f - 24) + 2, :], ACT.Silu)
            act.wait_ge(s_qd, 3)
            act.wait_ge(s_st, NC - 1)

            def head_out_root(g):
                act.wait_ge(s_gss, g + 1)
                root(bufA[:, g, :], psum[4 + g][:, 0:S], 3)

            for g in range(GH):
                act.wait_ge(s_go, g + 1)
                A(rstd[:, 2 * g:2 * g + 2, :], psum[g][:, :], ACT.Square)
                A(oT[:, 2 * g:2 * g + 2, :], psum[g][:, :], ACT.Copy).then_inc(s_goe, 1)
                if g:
                    head_out_root(g - 1)
            head_out_root(GH - 1)
            act.wait_ge(s_gn, 8)
            squares(3)
            norm_root(3)
            shift(3)
            for n in range(8):
                act.wait_ge(s_ht, n + 1)
                dst = h_tok if n < 4 else x_acc
                tt, half = divmod(n % 4, 2)
                A(dst[:, tt, half * 512:(half + 1) * 512], psum[n % 4][:, :], ACT.Copy).then_inc(s_hte, 1)
            act.wait_ge(s_lgm, 1)
            A(rt[:, 4, :], rt[:, 3, :], ACT.Exp).then_inc(s_rexp, 1)
            act.wait_ge(s_g2, 1)
            for g in range(2):
                A(g2bc[:, g * 512:(g + 1) * 512], psum[5 + g][:, :], ACT.Copy).then_inc(s_g2e, 1)
            act.wait_ge(s_rt, 1)

            def expert(e, nb):
                done = [0]

                def split_up_to(q_end):
                    while done[0] <= min(q_end, EQ - 1):
                        q = done[0]
                        if q % PPC == 0:
                            wait_landed(act, PRE + q // PPC, e)
                        act.wait_ge(w_free, e * EQ + q + 1)
                        A(w_hi[:, q % PIECES, :], raw_piece(q), ACT.Copy).then_inc(hi_done, 1)
                        done[0] += 1

                for g, bank in enumerate((0, 1, 6, 7)):
                    split_up_to(g if g < AHEAD else AHEAD)
                    act.wait_ge(s_gt, e * 4 + g + 1)
                    A(hg_hi[:, 2 * g:2 * g + 2, 0:nb * P],
                      psum[bank][:, :].rearrange("p (k s) -> p k s", k=2)[:, :, 0:nb * P], ACT.Copy).then_inc(s_gh, 1)
                act.wait_ge(s_gg, e + 1)
                A(PgT[:, 0:nb, :], psum[7][:, 0:nb * S].rearrange("p (b s) -> p b s", b=nb), ACT.Copy).then_inc(s_gge, 1)
                for q in range(EQ):
                    split_up_to(q + AHEAD)
                    i, p = divmod(q, PPC)
                    what, c = eorder[i]
                    if what == "w1" and p == PPC - 1:
                        act.wait_ge(w_free, e * EQ + PIECES + q + 1)
                        if c:
                            act.wait_ge(s_ea, e * ECH + c)
                        for b in range(nb):
                            last = A(silu_e[:, b, :], psum[b][:, :], ACT.Silu)
                        last.then_inc(s_esl, 1)
                    if q in turn_at:
                        c = turn_at[q]
                        act.wait_ge(s_et, e * ECH + c + 1)
                        for b in range(nb):
                            last = A(hid_hi[:, c % 2, b, :], psum[6 + b][:, :], ACT.Copy)
                        last.then_inc(s_hdh, 1)

            with act.Fori(0, NE) as e:
                nb = act.value_load(nbk[0:1, bass.ds(e, 1)], min_val=1, max_val=2)
                for n in (1, 2):
                    with act.If(nb == n):
                        expert(e, n)

        @block.vector
        def _(dve):
            v = nc.vector
            n_link = [0]

            def link(ins):
                n_link[0] += 1
                ins.then_inc(s_chain, 1)
                dve.wait_ge(s_chain, n_link[0])

            dve.wait_ge(s_tp, 1)
            v.tensor_copy(par[:, 0:88], psum[7][:, 0:88])
            v.tensor_copy(par[:, 136:141], psum[7][:, 88:93])
            link(v.tensor_copy(par[:, 88:136], psum[7][:, 128:176]))
            v.tensor_scalar(gq[:, 0:1], par[:, QG:QG + 1], 1.0, None, ALU.mult)
            v.tensor_scalar(gq[:, 1:2], par[:, QG + 1:QG + 2], math.sqrt(DH), None, ALU.mult)
            v.tensor_scalar(gq[:, 2:3], par[:, QG + 2:QG + 3], (1.0 - LAMBDA_INIT) * math.sqrt(P), None, ALU.mult)
            link(v.tensor_scalar(gq[:, 3:5], par[:, QG + 3:QG + 5], math.sqrt(DV), None, ALU.mult))
            v.memset(rt[:, 8, :], 0.0).then_inc(s_par, 1)
            for b in range(4):
                dve.wait_ge(s_xt, b + 1)
                v.tensor_copy(xT[:, 2 * b:2 * b + 2, :], psum[b][:, :]).then_inc(s_x, 2)
            dve.wait_ge(s_const, 1)
            v.tensor_copy(slot_no[:], slot_i)
            link(v.tensor_copy(dist[:], dist_i))
            link(v.tensor_scalar(tri[:], tri[:], 1.0 / GLA_TAU, None, ALU.mult))
            link(v.scalar_tensor_tensor(dist[:], dist[:], -1.0, dist[:], ALU.mult, ALU.min))
            link(v.memset(dist[0:64, 192:256], HIDDEN))
            dve.wait_ge(s_small, 16 * 14)
            v.tensor_tensor(lam_pr[:, 0, :], lam_in[:, 0, :], lam_in[:, 1, :], ALU.mult)
            link(v.tensor_tensor(lam_pr[:, 1, :], lam_in[:, 2, :], lam_in[:, 3, :], ALU.mult))
            v.tensor_reduce(lam[:, 0:2], lam_pr, AX_X, ALU.add).then_inc(s_lam, 1)
            dve.wait_ge(s_lam, 1)
            dve.sem_inc(s_constv, 1)
            dve.wait_ge(s_lame, 1)
            link(v.tensor_tensor(lam[:, 0:1], lam[:, 3:4], lam[:, 2:3], ALU.subtract))
            link(v.tensor_scalar(lam[:, 0:1], lam[:, 0:1], -LAMBDA_INIT, None, ALU.add))

            dve.wait_ge(s_cact, 1)

            ada_order = [key for key in order if key[0].startswith("ada")]
            ada_done = [0]

            def ada_steps(count):
                for _ in range(count):
                    chunk, k = divmod(ada_done[0], KT)
                    key = ada_order[chunk]
                    n = chunk // 2
                    w = slot_view(index[key], KT, FW)
                    acc = ada_acc[:, n % 2, (chunk % 2) * FW:(chunk % 2 + 1) * FW]
                    if k == 0:
                        wait_landed(dve, index[key])
                        if n >= 2:
                            dve.wait_ge(s_modp, n - 1)
                        v.tensor_scalar(acc, w[:, 0, :], c_act[:, 0:1], None, ALU.mult).then_inc(s_ada, 1)
                    else:
                        dve.wait_ge(s_ada, chunk * (KT - 1) + k)
                        step = v.scalar_tensor_tensor(acc, w[:, k, :], c_act[:, k:k + 1], acc, ALU.mult, ALU.add)
                        if k == KT - 1:
                            step.then_inc(ada_used, 1)
                        else:
                            step.then_inc(s_ada, 1)
                    ada_done[0] += 1

            def mod_third(l, third):
                dve.wait_ge(s_modp, 6 * l + third + 1)
                o = 256 + 48 * l + 8 * third
                v.tensor_tensor(mod[:, l, 8 * third:8 * third + 8], psum[7][:, o:o + 8],
                                par[:, AB + 48 * l + 8 * third:AB + 48 * l + 8 * third + 8], ALU.add).then_inc(s_mod, 1)

            def gains(n):
                l, second = divmod(n, 2)
                dve.wait_ge(s_mod, 6 * l + (5 if second else 2))
                c = 32 if second else 8
                g = (N2 if second else N1) + 8 * l
                link(v.scalar_tensor_tensor(cols[:, n, :], mod[:, l, c:c + 8], 1.0, par[:, g:g + 8], ALU.add, ALU.mult))
                link(v.tensor_scalar(cols[:, n, :], cols[:, n, :], math.sqrt(D), None, ALU.mult))

            def normalise(n):
                r = rstd[:, 0, :]
                dve.wait_ge(s_root, ROOT[f"norm{n}"] + 1)
                link(v.reciprocal(r, r))
                if n == 1 or n == 3:
                    dve.wait_ge(s_fill, 8 * (n + 1))
                if n == 2:
                    dve.wait_ge(w2f_used, NCH)
                for k in range(KT):
                    v.scalar_tensor_tensor(hT[:, k, :], xT[:, k, :], cols[:, n, k:k + 1], r, ALU.mult,
                                           ALU.mult).then_inc(s_hp, 1)

            ada_steps(4 * KT)
            mod_third(0, 0)
            mod_third(0, 1)
            gains(0)
            normalise(0)
            ada_steps(2 * KT)
            for f in range(8):
                dve.wait_ge(s_root, ROOT["qk"] + f + 1)
                dve.wait_ge(s_evac, f + 1)
                dst = (bufA if f < 4 else bufB)[:, 2 * (f % 4):2 * (f % 4) + 2, :]
                r = rstd[:, 2 * (f % 2) + 2:2 * (f % 2) + 4, :]
                link(v.reciprocal(r, r))
                v.scalar_tensor_tensor(dst, dst, gq[:, f // 4:f // 4 + 1], r, ALU.mult, ALU.mult).then_inc(s_qn, 1)
                if f == 3:
                    mod_third(0, 2)
                if f == 7:
                    mod_third(0, 3)
                if f % 2 == 1:
                    ada_steps(KT)

            def biased(h):
                a = att(h)
                slope = 2.0 ** (-8.0 * (h + 1) / H)
                nm = small[:, h % 2, :]
                dve.wait_ge(s_sc, h + 1)
                if h >= 2:
                    dve.wait_ge(s_pd, h - 1)
                for m in range(2):
                    v.scalar_tensor_tensor(a["t1"][:, m, :], dist[:, :], slope,
                                           psum[2 * (h % 2) + m][:, 0:S], ALU.mult, ALU.add)
                    last = v.scalar_tensor_tensor(a["t0"][:, m, :], dist[:, P:S], slope,
                                                  psum[2 * (h % 2) + m][:, S:S + P], ALU.mult, ALU.add)
                link(last)
                v.tensor_reduce(nm[:, 0:2], a["t1"], AX_X, ALU.max, negate=True)
                v.tensor_reduce(nm[:, 2:4], a["t0"], AX_X, ALU.max, negate=True).then_inc(s_mx, 1)

            def differ(h):
                a = att(h)
                nm = small[:, h % 2, :]
                dve.wait_ge(s_ex, h + 1)
                if h >= 2:
                    dve.wait_ge(s_pt, h - 1)
                link(v.reciprocal(nm[:, 8:12], nm[:, 4:8]))
                v.tensor_scalar(nm[:, 12:13], nm[:, 9:10], lam[:, 0:1], None, ALU.mult)
                v.tensor_scalar(nm[:, 13:14], nm[:, 11:12], lam[:, 0:1], None, ALU.mult)
                v.tensor_scalar(a["d1"], a["t1"][:, 0, :], nm[:, 8:9], None, ALU.mult)
                link(v.tensor_scalar(a["d0"], a["t0"][:, 0, :], nm[:, 10:11], None, ALU.mult))
                link(v.scalar_tensor_tensor(a["d1"], a["t1"][:, 1, :], nm[:, 12:13], a["d1"], ALU.mult, ALU.add))
                v.scalar_tensor_tensor(a["d0"], a["t0"][:, 1, :], nm[:, 13:14], a["d0"], ALU.mult,
                                       ALU.add).then_inc(s_pd, 1)

            def head_norm(g):
                dve.wait_ge(s_root, ROOT["sub"] + g + 1)
                r = rstd[:, 2 * g:2 * g + 2, :]
                link(v.reciprocal(r, r))
                v.scalar_tensor_tensor(oT[:, 2 * g:2 * g + 2, :], oT[:, 2 * g:2 * g + 2, :], gq[:, 2:3], r,
                                       ALU.mult, ALU.mult).then_inc(s_on, 2)

            biased(0)
            biased(1)
            for h in range(H):
                differ(h)
                if h + 2 < H:
                    biased(h + 2)
                if h == 0:
                    mod_third(0, 4)
                if h >= 4 and h % 2 == 0:
                    head_norm((h - 4) // 2)
            head_norm(2)
            head_norm(3)

            def residual(l, f0):
                dve.wait_ge(s_mod, 6 * l + 3)
                for g in range(4):
                    f = f0 + g
                    dve.wait_ge(s_fill, f + 1)
                    for j in range(2):
                        m = 2 * g + j
                        last = v.scalar_tensor_tensor(xT[:, m, :], psum[f % 4][:, j * S:(j + 1) * S],
                                                      mod[:, l, 16 + m:17 + m], xT[:, m, :], ALU.mult, ALU.add)
                        if j == 0:
                            last.then_inc(s_x, 1)
                    last.then_inc(s_evac, 1)
                    dve.wait_ge(s_evac, f + 1)
                    dve.sem_inc(s_x, 1)

            residual(0, 12)
            gains(1)
            normalise(1)
            for f in range(NCH):
                n = ffn_width(f) // P
                for j in range(n):
                    g = f * FPC + j
                    dve.wait_ge(s_silu, g + 1)
                    if f >= 2:
                        dve.wait_ge(w2f_used, f - 1)
                    v.tensor_tensor(hid[:, f % 2, j * S:(j + 1) * S], silu_f[:, g % 8, :],
                                    psum[4 + g % 2][:, S:2 * S], ALU.mult).then_inc(s_hid, 1)
                    ada_steps(2 * KT // n)
                if f:
                    mod_third(*((0, 5) if f == 1 else (1, f - 2)))
            for m in range(KT):
                if m < 6:
                    dve.wait_ge(s_y, m // 2 + 1)
                else:
                    dve.wait_ge(w2f_used, NCH)
                v.scalar_tensor_tensor(xT[:, m, :], psum[m // 2][:, (m % 2) * S:(m % 2 + 1) * S],
                                       mod[:, 0, 40 + m:41 + m], xT[:, m, :], ALU.mult, ALU.add).then_inc(s_x, 1)
            gains(2)
            normalise(2)
            mod_third(1, 4)
            ada_steps(KT)

            dve.wait_ge(s_late, 64)
            for tt in range(TT):
                dve.wait_ge(s_z, tt + 1)
                link(v.tensor_tensor(lz[:, tt, :], psum[4 + tt][:, :], ba_row[:, :], ALU.add))
                v.scalar_tensor_tensor(le[:, tt, :], lz[:, tt, :], -1.0, lz[:, tt, :], ALU.mult, ALU.max).then_inc(s_zb, 1)
            dve.wait_ge(s_ln, 1)
            v.scalar_tensor_tensor(la, lz, 0.0, le, ALU.min, ALU.subtract).then_inc(s_la, 1)
            ada_steps(KT)
            dve.wait_ge(s_be, 2)
            b16 = bT.rearrange("p g (c s) -> p (g c) s", c=NC)
            d16 = dd.rearrange("p g (c s) -> p (g c) s", c=NC)
            v.tensor_tensor(d16, b16[:, :, CHUNK - 1:CHUNK].to_broadcast([P, GH * NC, CHUNK]), b16,
                            ALU.subtract).then_inc(s_dd, 1)
            dve.wait_ge(s_evac, 20)
            v.scalar_tensor_tensor(qd, gq_t, float(P) ** -0.5, eb, ALU.mult, ALU.mult).then_inc(s_qd, 1)
            v.tensor_tensor(ki, gk_t, ei, ALU.mult).then_inc(s_qd, 1)
            dve.wait_ge(s_ed, 1)
            v.tensor_tensor(kd, gk_t, dd[:, :, :], ALU.mult).then_inc(s_qd, 1)
            mod_third(1, 5)
            dve.wait_ge(s_la, 1)
            link(v.memset(am[:, :, :], 0.0))
            dve.wait_ge(s_am, 1)
            for g in range(2):
                last = v.copy_predicated(am[:, 4 * g:4 * g + 4, :],
                                         tri[:, :].bitcast(I32).rearrange("p (o c) -> p o c", o=1).to_broadcast([P, 4, P]),
                                         psum[4 + g][:, :].rearrange("p (o c) -> p o c", o=4))
            last.then_inc(s_ame, 1)
            for c in range(NC - 1):
                dve.wait_ge(s_kv, c + 1)
                for g in range(GH):
                    kv = psum[4 + g // 2][:, (g % 2) * DV:(g % 2 + 1) * DV]
                    if c == 0:
                        last = v.tensor_copy(state[0][:, g, :], kv)
                    else:
                        last = v.scalar_tensor_tensor(state[c][:, g, :], state[c - 1][:, g, :],
                                                      eb[:, g, (c + 1) * CHUNK - 1:(c + 1) * CHUNK], kv,
                                                      ALU.mult, ALU.add)
                last.then_inc(s_st, 1)
                dve.wait_ge(s_st, c + 1)
            for g in range(GH):
                r = bufA[:, g, :]
                dve.wait_ge(s_root, ROOT["gla"] + g + 1)
                link(v.reciprocal(r, r))
                for w in range(2):
                    o = oT[:, 2 * g + w, :]
                    link(v.scalar_tensor_tensor(o, o, gq[:, 3 + w:4 + w], r, ALU.mult, ALU.mult))
                    dve.wait_ge(s_evac, 28)
                    v.tensor_tensor(o, o, bufB[:, 2 * g + w, :], ALU.mult).then_inc(s_gn, 1)
            residual(1, 28)
            gains(3)
            normalise(3)

            for k in range(KT):
                last = v.tensor_scalar(diag[:, k, :], ident[:], mod[:, 1, 40 + k:41 + k], None, ALU.mult)
            last.then_inc(s_dg, 1)
            r3 = [rt[:, j, :].rearrange("p (t e) -> p t e", t=TT) for j in range(9)]
            sel, tmp, ex, lg = r3[0], r3[3], r3[4], r3[5]
            link(v.memset(gate[:, :, :], 0.0))
            link(v.memset(posx[:, :, :], -1.0))
            mx = rt[:, 6, :]
            dve.wait_ge(s_lg, 1)
            link(v.tensor_copy(lg, psum[4][:, 0:TT * NE].rearrange("p (t e) -> p t e", t=TT)))
            for tt in range(TT):
                mine = rt[:, 5, tt * NE:(tt + 1) * NE].rearrange("p (e o) -> p e o", o=1).to_broadcast([P, NE, NE])
                other = rt[:, 5, tt * NE:(tt + 1) * NE].rearrange("p (o e) -> p o e", o=1).to_broadcast([P, NE, NE])
                link(v.tensor_tensor(cmp_a[:, tt], other, mine, ALU.is_gt))
                link(v.tensor_tensor(cmp_b[:, tt], other, mine, ALU.is_equal))
                link(v.tensor_tensor(cmp_b[:, tt], cmp_b[:, tt], lower_e[:, :, :], ALU.mult))
                link(v.tensor_tensor(cmp_a[:, tt], cmp_a[:, tt], cmp_b[:, tt], ALU.add))
                link(v.tensor_reduce(tmp[:, tt, :], cmp_a[:, tt], AX_X, ALU.add))
                link(v.tensor_reduce(mx[:, tt:tt + 1], lg[:, tt, :], AX_X, ALU.max, negate=True))
            link(v.tensor_scalar(sel, tmp, 1.5, None, ALU.is_lt))
            dve.sem_inc(s_sel, 1)
            for tt in range(TT):
                link(v.tensor_scalar(tmp[:, tt, :], lg[:, tt, :], mx[:, tt:tt + 1], None, ALU.add))
            dve.sem_inc(s_lgm, 1)
            dve.wait_ge(s_rexp, 1)
            link(v.tensor_tensor(ex, ex, sel, ALU.mult))
            link(v.tensor_reduce(mx[:, 2:4], ex, AX_X, ALU.add))
            link(v.reciprocal(mx[:, 4:6], mx[:, 2:4]))
            for tt in range(TT):
                link(v.tensor_scalar(gate[:, tt, 0:NE], ex[:, tt, :], mx[:, 4 + tt:5 + tt], None, ALU.mult))
            dve.wait_ge(s_pos, 1)
            pos = psum[7][:, 0:TT * NE].rearrange("p (t e) -> p t e", t=TT)
            link(v.scalar_tensor_tensor(tmp, pos, 1.0, sel, ALU.add, ALU.mult))
            link(v.tensor_scalar(posx[:, :, 0:NE], tmp, -1.0, None, ALU.add))
            link(v.tensor_scalar(rt[:, 7, 0:NE], psum[7][:, 2 * NE:3 * NE], P + 0.5, 1.0, ALU.is_gt, ALU.add))
            link(v.tensor_copy(nbk[:, :], rt[:, 7, 0:NE]))
            link(v.memset(rt[:, 7, 0:1], 1.0))
            link(v.tensor_copy(nbp[:, 0:1], rt[:, 7, 0:1]))
            link(v.tensor_copy(nbp[:, 1:NE], nbk[:, 0:NE - 1]))
            link(v.memset(PgT[:, 0, :], 0.0))
            v.memset(y_sb[:, 0, :], 0.0).then_inc(s_eye, 1)
            dve.wait_ge(s_g2, 1)
            dve.sem_inc(s_rt, 1)

            def dispatch(e):
                for tt in range(TT):
                    v.tensor_scalar(Pm[:, tt, :], slot_no[:], posx[:, tt, bass.ds(e, 1)], None, ALU.is_equal)
                    last = v.tensor_scalar(Pg[:, tt, :], slot_no[:], posx[:, tt, bass.ds(e, 1)],
                                           gate[:, tt, bass.ds(e, 1)], ALU.is_equal, ALU.mult)
                last.then_inc(s_P, 1)

            def expert(e, nb):
                done = [0]

                def split_up_to(q_end):
                    while done[0] <= min(q_end, EQ - 1):
                        q = done[0]
                        dve.wait_ge(hi_done, e * EQ + q + 1)
                        v.tensor_tensor(w_lo[:, q % PIECES, :], raw_piece(q), w_hi[:, q % PIECES, :].bitcast(F32),
                                        ALU.subtract).then_inc(lo_done, 1)
                        done[0] += 1

                for g, bank in enumerate((0, 1, 6, 7)):
                    split_up_to(g if g < AHEAD else AHEAD)
                    dve.wait_ge(s_gh, e * 4 + g + 1)
                    v.tensor_tensor(hg_lo[:, 2 * g:2 * g + 2, 0:nb * P],
                                    psum[bank][:, :].rearrange("p (k s) -> p k s", k=2)[:, :, 0:nb * P],
                                    hg_hi[:, 2 * g:2 * g + 2, 0:nb * P].bitcast(F32), ALU.subtract).then_inc(s_gl, 1)
                for q in range(EQ):
                    split_up_to(q + AHEAD)
                    i, p = divmod(q, PPC)
                    what, c = eorder[i]
                    if q < 4:
                        tt, half = divmod(q, 2)
                        dve.wait_ge(s_sct, e * 4 + q + 1)
                        dst = x_acc[:, tt, half * 512:(half + 1) * 512]
                        v.tensor_tensor(dst, dst, psum[2 + q][:, :], ALU.add).then_inc(s_add, 1)
                    if what == "w3" and p == PPC - 1:
                        dve.wait_ge(s_esl, e * ECH + c + 1)
                        dve.wait_ge(w_free, e * EQ + PIECES + q + 1)
                        if c:
                            dve.wait_ge(s_et, e * ECH + c)
                        for b in range(nb):
                            last = v.tensor_tensor(hid_e[:, b, :], silu_e[:, b, :], psum[6 + b][:, :], ALU.mult)
                        last.then_inc(s_ea, 1)
                    if q in turn_at:
                        c = turn_at[q]
                        dve.wait_ge(s_hdh, e * ECH + c + 1)
                        for b in range(nb):
                            last = v.tensor_tensor(hid_lo[:, c % 2, b, :], psum[6 + b][:, :],
                                                   hid_hi[:, c % 2, b, :].bitcast(F32), ALU.subtract)
                        last.then_inc(s_hdl, 1)
                    if q == EQ - 2:
                        dve.wait_ge(s_gge, e + 1)
                        dispatch(e + 1)
                dve.wait_ge(w_free, (e + 1) * EQ + PIECES)
                dve.wait_ge(s_add, e * 4 + 4)
                for b in range(nb):
                    for half in range(2):
                        last = v.tensor_tensor(y_sb[:, b, half * 512:(half + 1) * 512], psum[2 + 2 * b + half][:, :],
                                               g2bc[:, half * 512:(half + 1) * 512], ALU.mult)
                last.then_inc(s_eye, 1)

            dispatch(0)
            with dve.Fori(0, NE) as e:
                nb = dve.value_load(nbk[0:1, bass.ds(e, 1)], min_val=1, max_val=2)
                for n in (1, 2):
                    with dve.If(nb == n):
                        expert(e, n)
            for n in range(4):
                tt, half = divmod(n, 2)
                dve.wait_ge(s_sct, NE * 4 + n + 1)
                dst = x_acc[:, tt, half * 512:(half + 1) * 512]
                v.tensor_tensor(dst, dst, psum[2 + n][:, :], ALU.add).then_inc(s_add, 1)


INPUTS = ["x", "c", "ada_w", "ada_b", "norm1_g", "norm2_g", "da_w_in", "da_q_gain", "da_k_gain", "da_lam_q1",
          "da_lam_k1", "da_lam_q2", "da_lam_k2", "da_subln_g", "da_w_out", "gla_w_in", "gla_w_a1", "gla_w_a2",
          "gla_b_a", "gla_out_g", "gla_w_out", "ffn_w1", "ffn_w3", "ffn_w2", "moe_router", "moe_w1", "moe_w3",
          "moe_w2"]


def kernel(**inputs):
    import numpy as np
    import concourse.bacc as bacc
    from concourse.bass_utils import run_bass_kernel_spmd

    nc = bacc.Bacc("TRN2", target_bir_lowering=False, num_devices=1, dynamic_dma_scratch_size=1024)
    arrays, t = {}, {}
    for name in INPUTS:
        a = np.ascontiguousarray(inputs[name])
        if name in ("moe_w1", "moe_w3", "moe_w2"):
            a = a[0]
        arrays[f"in_{name}"] = a
        t[name] = nc.dram_tensor(f"in_{name}", a.shape, mybir.dt.from_np(a.dtype), kind="ExternalInput").ap()
    t["out"] = nc.dram_tensor("out_x", (1, S, D), F32, kind="ExternalOutput").ap()
    build(nc, t)
    r = run_bass_kernel_spmd(nc, [arrays], core_ids=[0])
    return r.results[0]["out_x"]
```

```python
import math
from contextlib import ExitStack

import concourse.bass as bass
from concourse import mybir

ALU = mybir.AluOpType
ACT = mybir.ActivationFunctionType
AX_X = mybir.AxisListType.X
F32 = mybir.dt.float32
F32R = mybir.dt.float32r
I32 = mybir.dt.int32

P = 128
D = 1024
S = 256
TT = S // P
KT = D // P
CHUNK = 64
EPS = 1e-6
H = 8
DH = 64
LAMBDA_INIT = 0.8 - 0.6 * math.exp(-0.3 * 0)
GH = 4
DV = D // GH
NC = S // CHUNK
GLA_RANK = 16
GLA_TAU = 16.0
FFN = 2816
FT = FFN // P
NE = 8
EF = 3584
FW = 512
FPC = FW // P
ECH = EF // FW
NCH = (FFN + FW - 1) // FW
HIDDEN = -1e30

SLOTS = 7
SLOT = KT * FW
SUB = 1024
PPC = SLOT // SUB
PIECES = 3
AHEAD = PIECES - 1


def stream_before_experts():
    ada = iter([("ada0", i) for i in range(12)] + [("ada1", i) for i in range(12)])
    order = [next(ada) for _ in range(4)]
    for i in range(6):
        order += [("in0", i), next(ada)]
    order += [("out0", i) for i in range(2)]
    for f in range(NCH):
        order += [("w1", f), next(ada), ("w3", f), next(ada)]
        if f:
            order += [("w2", f - 1)]
    order += [("w2", NCH - 1)]
    for i in range(6):
        order += [("in1", i)]
        if i < 2:
            order += [next(ada)]
    return order + [("out1", i) for i in range(2)]


def stream_of_expert():
    order = []
    for c in range(ECH):
        order += [("w1", c), ("w3", c)]
        if c:
            order += [("w2", c - 1)]
    return order + [("w2", ECH - 1)]


def build(nc, t):
    order = stream_before_experts()
    index = {key: i for i, key in enumerate(order)}
    PRE = len(order)
    eorder = stream_of_expert()
    PER = len(eorder)
    EQ = PER * PPC
    assert PER % SLOTS == 0 and EQ % PIECES == 0
    fpieces = []
    for f in range(NCH + 1):
        if f < NCH:
            for j in range(min(FPC, FT - f * FPC)):
                fpieces += [("w1", f, j), ("w3", f, j)]
        if f:
            fpieces += [("w2", f - 1, j) for j in range(min(FPC, FT - (f - 1) * FPC))]
    fpiece = {key: q for q, key in enumerate(fpieces)}
    FQ = len(fpieces)
    assert FQ % PIECES == 0
    last_piece = {key: PPC * i + PPC - 1 for i, key in enumerate(eorder)}
    turn_at = {last_piece["w3", c] + 2: c for c in range(ECH)}
    proj_rank = {k: i + 1 for i, k in enumerate([k for k in order if k[0][:-1] in ("in", "out")])}
    ada_rank = {k: i + 1 for i, k in enumerate([k for k in order if k[0].startswith("ada")])}

    ROOT = {"norm0": 0, "qk": 1, "sub": 9, "norm1": 13, "norm2": 14, "gla": 15, "norm3": 19}

    with ExitStack() as ctx:
        def sb(name, shape, dt=F32):
            return ctx.enter_context(nc.sbuf_tensor(name, shape, dt))

        def sem(name):
            return ctx.enter_context(nc.semaphore(name))

        with ExitStack() as of_mixers:
            def sb_mixer(name, shape):
                return of_mixers.enter_context(nc.sbuf_tensor(name, shape, F32))

            V = sb_mixer("V", [P, TT, D])
            hT = sb_mixer("hT", [P, KT, S])
            bufA = sb_mixer("bufA", [P, KT, S])
            bufB = sb_mixer("bufB", [P, KT, S])
            oT = sb_mixer("oT", [P, KT, S])
            halves = sb_mixer("halves", [P, P])
            dist = sb_mixer("dist", [P, S])
            bT = sb_mixer("bT", [P, GH, S])
            dd = sb_mixer("dd", [P, GH, S])
        w_hi = sb("w_hi", [P, PIECES, SUB], F32R)
        w_lo = sb("w_lo", [P, PIECES, SUB], F32R)
        hg_hi = sb("hg_hi", [P, KT, S], F32R)
        hg_lo = sb("hg_lo", [P, KT, S], F32R)
        hid_hi = sb("hid_hi", [P, 2, 2, FW], F32R)
        hid_lo = sb("hid_lo", [P, 2, 2, FW], F32R)
        ring = sb("ring", [P, SLOTS, SLOT])
        ident = sb("ident", [P, P])
        ones = sb("ones", [P, P])
        tri = sb("tri", [P, P])
        before = sb("before", [P, P])
        slot_no = sb("slot_no", [P, S])
        lower_e = sb("lower_e", [P, NE, NE])
        NPAR = 8 + 16 + 16 + 96 + 5
        par = sb("par", [P, NPAR])
        C0, N1, N2, AB, QG = 0, 8, 24, 40, 136
        c_act = sb("c_act", [P, KT])
        lam = sb("lam", [P, 4])
        router = sb("router", [P, KT, NE])
        mod = sb("mod", [P, 2, 48])
        ada_acc = sb("ada_acc", [P, 2, 1024])
        cols = sb("cols", [P, 4, KT])
        eps = sb("eps", [P, 4])
        gq = sb("gq", [P, 8])
        xT = sb("xT", [P, KT, S])
        sq = sb("sq", [P, KT, S])
        rstd = sb("rstd", [P, KT, S])
        work = sb("work", [P, 2, 2048])
        small = sb("small", [P, 2, 16])
        nbk = sb("nbk", [P, NE], I32)
        nbp = sb("nbp", [P, NE], I32)
        gate = sb("gate", [P, TT, NE + 1])
        posx = sb("posx", [P, TT, NE + 1])

        SUB_BANKS = (6, 0, 1, 2)

        psum = [ctx.enter_context(nc.psum_tensor(f"bank{i}", [P, 512], F32)) for i in range(8)]

        s_small = sem("s_small")
        s_late = sem("s_late")
        landed = [sem(f"landed{i}") for i in range(SLOTS)]
        s_ada = sem("s_ada")
        ada_used = sem("ada_used")
        s_const = sem("s_const")
        s_constv = sem("s_constv")
        s_tp = sem("s_tp")
        s_par = sem("s_par")
        s_cact = sem("s_cact")
        s_xt = sem("s_xt")
        s_x = sem("s_x")
        s_modp = sem("s_modp")
        s_mod = sem("s_mod")
        s_sq = sem("s_sq")
        s_ssq = sem("s_ssq")
        s_root = sem("s_root")
        s_hp = sem("s_hp")
        s_h = sem("s_h")
        s_fill = sem("s_fill")
        s_evac = sem("s_evac")
        s_qsq = sem("s_qsq")
        s_qss = sem("s_qss")
        s_qn = sem("s_qn")
        s_lam = sem("s_lam")
        s_lame = sem("s_lame")
        s_sc = sem("s_sc")
        s_mx = sem("s_mx")
        s_ex = sem("s_ex")
        s_pd = sem("s_pd")
        s_pt = sem("s_pt")
        s_pte = sem("s_pte")
        s_o = sem("s_o")
        s_oe = sem("s_oe")
        s_oss = sem("s_oss")
        s_on = sem("s_on")
        s_silu = sem("s_silu")
        s_prod = sem("s_prod")
        s_hidh = sem("s_hidh")
        s_hidl = sem("s_hidl")
        s_nr = sem("s_nr")
        s_a1 = sem("s_a1")
        s_a1e = sem("s_a1e")
        s_z = sem("s_z")
        s_zb = sem("s_zb")
        s_ln = sem("s_ln")
        s_la = sem("s_la")
        s_b = sem("s_b")
        s_be = sem("s_be")
        s_dd = sem("s_dd")
        s_ed = sem("s_ed")
        s_qd = sem("s_qd")
        s_kdt = sem("s_kdt")
        s_kde = sem("s_kde")
        s_am = sem("s_am")
        s_ame = sem("s_ame")
        s_kv = sem("s_kv")
        s_st = sem("s_st")
        s_go = sem("s_go")
        s_goe = sem("s_goe")
        s_gss = sem("s_gss")
        s_gn = sem("s_gn")
        s_lg = sem("s_lg")
        s_sel = sem("s_sel")
        s_pos = sem("s_pos")
        s_rt = sem("s_rt")
        s_ht = sem("s_ht")
        s_hte = sem("s_hte")
        s_dg = sem("s_dg")
        s_g2 = sem("s_g2")
        s_g2e = sem("s_g2e")
        s_y = sem("s_y")
        s_lgm = sem("s_lgm")
        s_rexp = sem("s_rexp")
        hi_done = sem("hi_done")
        lo_done = sem("lo_done")
        w_free = sem("w_free")
        s_P = sem("s_P")
        s_gt = sem("s_gt")
        s_gh = sem("s_gh")
        s_gl = sem("s_gl")
        s_gg = sem("s_gg")
        s_gge = sem("s_gge")
        s_esl = sem("s_esl")
        s_ea = sem("s_ea")
        s_et = sem("s_et")
        s_hdh = sem("s_hdh")
        s_hdl = sem("s_hdl")
        s_eye = sem("s_eye")
        s_sct = sem("s_sct")
        s_scb = sem("s_scb")
        s_add = sem("s_add")
        s_fin = sem("s_fin")
        s_out = sem("s_out")
        s_table = sem("s_table")
        s_chain = sem("s_chain")
        s_achain = sem("s_achain")
        s_gchain = sem("s_gchain")

        dist_i = sq[:, 0, :].bitcast(I32)
        slot_i = sq[:, 1, :].bitcast(I32)
        row_a, row_b = sq[:, 2, 0:P], sq[:, 3, 0:P]
        lam_in = sq[:, 4, :].rearrange("p (j d) -> p j d", j=4)
        lam_pr = sq[:, 5, 0:2 * DH].rearrange("p (j d) -> p j d", j=2)
        ba_row = work[:, 0, 1280:1792]
        wa1 = work[:, 0, 1792:1920].rearrange("p (k n) -> p k n", k=KT)
        wa2 = work[0:GLA_RANK, 1, 1536:2048]
        x_rows = work[:, :, 0:D]
        def att(h):
            w = work[:, h % 2, :]
            return {"t1": w[:, 0:512].rearrange("p (m s) -> p m s", m=2),
                    "t0": w[:, 512:768].rearrange("p (m s) -> p m s", m=2),
                    "d1": w[:, 768:1024], "d0": w[:, 1024:1152], "pt": w[:, 1152:1536]}
        silu_f, prod_f = rstd[:, 0:4, :], rstd[:, 4:8, :]
        la = work[:, 0, 0:1024].rearrange("p (t c) -> p t c", t=TT)
        lz = work[:, 1, 0:1024].rearrange("p (t c) -> p t c", t=TT)
        le = work[:, 1, 1024:2048].rearrange("p (t c) -> p t c", t=TT)
        a1T = work[0:GLA_RANK, 0, 1024:1280]
        gq_t, gk_t = bufA[:, 0:GH, :], bufA[:, GH:2 * GH, :]
        eb = rstd[:, 0:GH, :]
        ei = rstd[:, GH:2 * GH, :]
        qd = sq[:, 0:GH, :]
        ki = sq[:, GH:2 * GH, :]
        kd = oT[:, 0:GH, :]
        kdt = work[:, 0, 0:1024].rearrange("p (g c) -> p g c", g=8)
        am = work[:, 1, 0:1024].rearrange("p (g c) -> p g c", g=8)
        state = [w.rearrange("p (g v) -> p g v", g=GH)
                 for w in (ada_acc[:, 0, :], ada_acc[:, 1, :], work[:, 1, 1024:2048])]
        x_acc = rstd[:, :, :].rearrange("p (t k) s -> p t (k s)", t=TT)
        h_tok = sq[:, :, :].rearrange("p (t k) s -> p t (k s)", t=TT)
        y_sb = xT[:, :, :].rearrange("p (t k) s -> p t (k s)", t=TT)
        g2bc = work[:, 0, 0:1024]
        silu_e = work[:, 0, 1024:2048].rearrange("p (b n) -> p b n", b=2)
        hid_e = ada_acc[:, 0, :].rearrange("p (b n) -> p b n", b=2)
        scattered = ada_acc[:, 1, :].rearrange("p (b n) -> p b n", b=2)
        diag = work[:, 1, 512:1536].rearrange("p (k c) -> p k c", k=KT)
        Pm = work[:, 1, 512:1024].rearrange("p (t s) -> p t s", t=TT)
        Pg = work[:, 1, 1024:1536].rearrange("p (t s) -> p t s", t=TT)
        PgT = work[:, 1, 1536:2048].rearrange("p (b s) -> p b s", b=2)
        rt = sb("rt", [P, 9, TT * NE])
        cmp_a = ada_acc[:, 0, 0:128].rearrange("p (t e o) -> p t e o", t=TT, e=NE)
        cmp_b = ada_acc[:, 0, 128:256].rearrange("p (t e o) -> p t e o", t=TT, e=NE)

        def slot(i, n=SLOT):
            return ring[:, i % SLOTS, 0:n]

        def chunk_in(w, c0, n):
            return w[:, c0:c0 + n].rearrange("(k p) n -> p k n", p=P)

        def ffn_width(f):
            return min(FW, FFN - f * FW)

        def source(key):
            kind, i = key
            if kind.startswith("ada"):
                return chunk_in(t["ada_w"][int(kind[3])], i * FW, FW), KT, FW
            if kind == "in0":
                return chunk_in(t["da_w_in"][0], i * FW, FW), KT, FW
            if kind == "in1":
                return chunk_in(t["gla_w_in"][0], i * FW, FW), KT, FW
            if kind == "out0":
                return chunk_in(t["da_w_out"][0], i * FW, FW), KT, FW
            if kind == "out1":
                return chunk_in(t["gla_w_out"][0], i * FW, FW), KT, FW
            n = ffn_width(i)
            if kind == "w2":
                return t["ffn_w2"][0][i * FW:i * FW + n, :].rearrange("(k p) n -> p k n", p=P), n // P, D
            return chunk_in(t["ffn_" + kind][0], i * FW, n), KT, n

        def slot_view(i, k, n):
            return ring[:, i % SLOTS, 0:k * n].rearrange("p (k n) -> p k n", k=k)

        def expert_source(e, i):
            what, c = eorder[i]
            if what == "w2":
                w = t["moe_w2"].rearrange("e (c k p) n -> e c p k n", p=P, k=FPC)
                return w[bass.ds(e, 1), c, :, :, :].rearrange("o p k n -> p (o k) n"), FPC, D
            w = t["moe_" + what].rearrange("e (k p) n -> e p k n", p=P)
            return w[bass.ds(e, 1), :, :, c * FW:(c + 1) * FW].rearrange("o p k n -> p (o k) n"), KT, FW

        def raw_tile(q):
            kind, f, j = fpieces[q]
            if kind == "w2":
                return slot_view(index[kind, f], ffn_width(f) // P, D)[:, j:j + 1, :]
            return slot_view(index[kind, f], KT, ffn_width(f))[:, :, j * P:(j + 1) * P]

        def split_tile(w, q):
            k = 1 if fpieces[q][0] == "w2" else KT
            return w[:, q % PIECES, :].rearrange("p (k n) -> p k n", k=k)

        def raw_piece(q):
            i, p = divmod(q, PPC)
            return ring[:, (PRE + i) % SLOTS, p * SUB:(p + 1) * SUB]

        def wait_landed(eng, i, e=0):
            if isinstance(e, int):
                eng.wait_ge(landed[i % SLOTS], 16 * (i // SLOTS + 1 + e * (PER // SLOTS)))
            else:
                eng.wait_ge(landed[i % SLOTS], e * (16 * PER // SLOTS) + 16 * (i // SLOTS + 1))

        block = ctx.enter_context(nc.Block())

        @block.sync
        def _(sp):
            sp.dma_start(x_rows, t["x"][0].rearrange("(t p) d -> p t d", p=P)).then_inc(s_small, 16)
            for r, name in ((88, "da_q_gain"), (89, "da_k_gain")):
                sp.dma_start(row_a[r:r + 1, :], t[name].rearrange("o m d -> o (m d)")).then_inc(s_small, 16)
            sp.dma_start(row_a[90:91, :], t["da_subln_g"]).then_inc(s_small, 16)
            sp.dma_start(row_a[91:93, :], t["gla_out_g"].rearrange("o (k p) -> (o k) p", p=P)).then_inc(s_small, 16)
            for j, name in enumerate(("da_lam_q1", "da_lam_k1", "da_lam_q2", "da_lam_k2")):
                sp.dma_start(lam_in[:, j, :], t[name][0:1, :].to_broadcast([P, DH])).then_inc(s_small, 16)

            def wait_used(key):
                kind, f = key
                if kind.startswith("ada"):
                    sp.wait_ge(ada_used, ada_rank[key])
                elif kind in ("w1", "w3", "w2"):
                    sp.wait_ge(lo_done, fpiece[kind, f, ffn_width(f) // P - 1] + 1)
                else:
                    sp.wait_ge(s_fill, 2 * proj_rank[key])

            def load(i, key):
                if i >= SLOTS:
                    wait_used(order[i - SLOTS])
                src, k, n = source(key)
                sp.dma_start(slot_view(i, k, n), src).then_inc(landed[i % SLOTS], 16)

            for i, key in enumerate(order):
                load(i, key)
                if key == ("w1", 1):
                    sp.wait_ge(s_o, H)
                    sp.dma_start(ba_row[:, :], t["gla_b_a"][0:1, :].to_broadcast([P, 512])).then_inc(s_late, 16)
                    sp.dma_start(wa1[:, :, :], t["gla_w_a1"][0].rearrange("(k p) n -> p k n", p=P)).then_inc(s_late, 16)
                    sp.dma_start(wa2[:, :], t["gla_w_a2"][0]).then_inc(s_late, 16)
                    sp.dma_start(router[:, :, :], t["moe_router"][0].rearrange("(k p) n -> p k n", p=P)).then_inc(s_late, 16)

            def load_expert(e, i, first=False):
                j = i - SLOTS
                if first:
                    wait_used(order[PRE + j])
                else:
                    back, j = (0, j) if j >= 0 else (-1, j + PER)
                    sp.wait_ge(lo_done, (e + back) * EQ + FQ + (j + 1) * PPC)
                src, k, n = expert_source(e, i)
                sp.dma_start(slot_view(PRE + i, k, n), src).then_inc(landed[(PRE + i) % SLOTS], 16)

            for i in range(SLOTS):
                load_expert(0, i, first=True)
            with sp.Fori(0, NE - 1) as e:
                for i in range(SLOTS, PER):
                    load_expert(e, i)
                for i in range(SLOTS):
                    load_expert(e + 1, i)
            for i in range(SLOTS, PER):
                load_expert(NE - 1, i)
            for tt in range(TT):
                sp.wait_ge(s_fin, 2 * tt + 2)
                sp.dma_start(t["out"][0, tt * P:(tt + 1) * P, :], x_acc[:, tt, :]).then_inc(s_out, 16)
            sp.wait_ge(s_out, 16 * TT)

        @block.gpsimd
        def _(pool):
            n = [0]

            def link(ins):
                n[0] += 1
                ins.then_inc(s_gchain, 1)
                pool.wait_ge(s_gchain, n[0])

            nc.gpsimd.memset(ident[:], 0.0).then_inc(s_gchain, 1)
            nc.gpsimd.memset(ones[:], 1.0).then_inc(s_gchain, 1)
            nc.gpsimd.memset(halves[:], 0.0).then_inc(s_gchain, 1)
            nc.gpsimd.memset(lower_e[:], 1.0).then_inc(s_gchain, 1)
            n[0] = 4
            pool.wait_ge(s_gchain, 4)
            link(nc.gpsimd.affine_select(out=ident[:], in_=ident[:], compare_op=ALU.not_equal, fill=1.0, base=0,
                                         pattern=[[-1, P]], channel_multiplier=1))
            link(nc.gpsimd.memset(halves[0:64, 0:64], 1.0))
            link(nc.gpsimd.memset(halves[64:128, 64:128], 1.0))
            link(nc.gpsimd.affine_select(out=tri[:], in_=halves[:], compare_op=ALU.is_ge, fill=0.0, base=0,
                                         pattern=[[1, P]], channel_multiplier=-1))
            link(nc.gpsimd.affine_select(out=before[:], in_=ones[:], compare_op=ALU.is_gt, fill=0.0, base=0,
                                         pattern=[[1, P]], channel_multiplier=-1))
            link(nc.gpsimd.affine_select(out=lower_e[:], in_=lower_e[:], compare_op=ALU.is_gt, fill=0.0, base=0,
                                         pattern=[[1, NE], [-1, NE]], channel_multiplier=0))
            link(nc.gpsimd.iota(dist_i, pattern=[[-1, S]], base=P, channel_multiplier=1))
            link(nc.gpsimd.iota(slot_i, pattern=[[1, S]], base=0, channel_multiplier=0))
            for j, width in enumerate((D, DH, P, DV)):
                last = nc.gpsimd.memset(eps[:, j:j + 1], width * EPS)
            last.then_inc(s_const, 1)

            def add_expert(e):
                for n in range(4):
                    tt, half = divmod(n, 2)
                    dst = x_acc[:, tt, half * 512:(half + 1) * 512]
                    pool.wait_ge(s_scb, e * 4 + n + 1)
                    nc.gpsimd.tensor_tensor(dst, dst, scattered[:, n % 2, :], ALU.add).then_inc(s_add, 1)

            pool.wait_ge(s_hte, 8)
            pool.sem_inc(s_add, 2)
            with pool.Fori(0, NE) as e:
                add_expert(e)
                pool.wait_ge(s_add, e * 4 + 6)

        @block.tensor
        def _(pe):
            mm = nc.tensor.matmul
            fill = [0]
            pe.wait_ge(s_const, 1)

            pe.wait_ge(s_small, 16 * 14)
            nc.tensor.transpose(psum[7][:, 0:93], row_a[0:93, :], ident[0:93, 0:93])
            nc.tensor.transpose(psum[7][:, 128:176], row_b[0:48, :], ident[0:48, 0:48]).then_inc(s_tp, 1)
            for b in range(4):
                for j in range(2):
                    for i in range(TT):
                        last = nc.tensor.transpose(psum[b][:, j * S + i * P:j * S + (i + 1) * P],
                                                   x_rows[:, i, (2 * b + j) * P:(2 * b + j + 1) * P], ident[:])
                last.then_inc(s_xt, 1)

            def turn_third(l, third):
                n = 6 * l + third
                pe.wait_ge(ada_used, 2 * n + 2)
                if n:
                    pe.wait_ge(s_mod, n)
                for j in range(8):
                    last = nc.tensor.transpose(psum[6 + j // 4][:, (j % 4) * P:(j % 4 + 1) * P],
                                               ada_acc[:, n % 2, j * P:(j + 1) * P], ident[:])
                last.then_inc(s_modp, 1)

            def norm_sums(n, tiles=range(KT)):
                for k in tiles:
                    pe.wait_ge(s_sq, 8 * n + k + 1)
                    last = mm(psum[6][:, 0:S], ones[:], sq[:, k, :], start=(k == 0), stop=(k == KT - 1))
                if k == KT - 1:
                    last.then_inc(s_ssq, 1)

            def half_project(key, ready, token_major, g):
                i = index[key]
                w = slot_view(i, KT, FW)
                wait_landed(pe, i)
                src, signal, base = ready
                f = fill[0]
                if f >= 4:
                    pe.wait_ge(s_evac, f - 3)
                if token_major:
                    for k in range(KT):
                        pe.wait_ge(signal, base + k + 1)
                        last = mm(psum[f % 4][:, :], src[:, k, g * P:(g + 1) * P], w[:, k, :],
                                  start=(k == 0), stop=(k == KT - 1))
                else:
                    for j in range(2):
                        for k in range(KT):
                            pe.wait_ge(signal, base + k + 1)
                            m = 2 * g + j
                            last = mm(psum[f % 4][:, j * S:(j + 1) * S], w[:, k, m * P:(m + 1) * P], src[:, k, :],
                                      start=(k == 0), stop=(k == KT - 1))
                last.then_inc(s_fill, 1)
                fill[0] += 1

            def project(key, ready, token_major):
                for g in range(2):
                    half_project(key, ready, token_major, g)

            def qk_sums(f):
                pe.wait_ge(s_qsq, f + 1)
                if f >= 2:
                    pe.wait_ge(s_root, ROOT["qk"] + f - 1)
                mm(psum[4 + f % 2][:, :], halves[:], sq[:, 2 * (f % 4):2 * (f % 4) + 2, :],
                   start=True, stop=True).then_inc(s_qss, 1)

            norm_sums(0)
            pe.wait_ge(s_par, 1)
            pe.wait_ge(s_root, ROOT["norm0"] + 1)
            turn_third(0, 0)
            turn_third(0, 1)
            for i in range(6):
                project(("in0", i), (hT, s_h, 0), token_major=(i >= 4))
                if 1 <= i <= 4:
                    qk_sums(2 * (i - 1))
                    qk_sums(2 * (i - 1) + 1)
                if i in (2, 4):
                    turn_third(0, 1 + i // 2)
            turn_third(0, 4)

            def scores(h):
                if h >= 2:
                    pe.wait_ge(s_mx, h - 1)
                for m in range(2):
                    q = bufA[m * DH:(m + 1) * DH, h, :]
                    k = bufB[m * DH:(m + 1) * DH, h, :]
                    mm(psum[2 * (h % 2) + m][:, 0:S], q[:, P:S], k, start=True, stop=True)
                    last = mm(psum[2 * (h % 2) + m][:, S:S + P], q[:, 0:P], k[:, 0:P], start=True, stop=True)
                last.then_inc(s_sc, 1)

            def turn_map(h):
                a = att(h)
                pe.wait_ge(s_pd, h + 1)
                if h >= 1:
                    pe.wait_ge(s_pte, h)
                nc.tensor.transpose(psum[4][:, 0:P], a["d0"], ident[:])
                nc.tensor.transpose(psum[4][:, P:2 * P], a["d1"][:, 0:P], ident[:])
                nc.tensor.transpose(psum[4][:, 2 * P:3 * P], a["d1"][:, P:S], ident[:]).then_inc(s_pt, 1)

            def attend(h):
                a = att(h)
                pe.wait_ge(s_pte, h + 1)
                if h >= 1:
                    pe.wait_ge(s_oe, h)
                mm(psum[5][:, 0:S], V[:, 0, h * P:(h + 1) * P], a["pt"][:, 0:S], start=True, stop=False)
                mm(psum[5][:, P:S], V[:, 1, h * P:(h + 1) * P], a["pt"][:, S:S + P], start=False,
                   stop=True).then_inc(s_o, 1)

            def head_sums(g):
                pe.wait_ge(s_oe, 2 * g + 2)
                mm(psum[SUB_BANKS[g]][:, :], ones[:], sq[:, 2 * g:2 * g + 2, :], start=True, stop=True).then_inc(s_oss, 1)

            pe.wait_ge(s_qn, 8)
            pe.wait_ge(s_evac, 12)
            scores(0)
            scores(1)
            for h in range(H):
                if h + 2 < H:
                    scores(h + 2)
                turn_map(h)
                attend(h)
                if h == H - 2:
                    pe.wait_ge(s_mx, H)
                    for g in range(3):
                        head_sums(g)
            head_sums(3)
            pe.sem_inc(w_free, PIECES)
            project(("out0", 0), (oT, s_on, 0), False)
            half_project(("out0", 1), (oT, s_on, 0), False, 0)
            norm_sums(1, range(0, 2))
            half_project(("out0", 1), (oT, s_on, 0), False, 1)
            norm_sums(1, range(2, KT))

            pe.wait_ge(s_evac, 16)

            def hidden(what, f, j):
                q = fpiece[what, f, j]
                o = 0 if what == "w1" else S
                g = f * FPC + j
                if o == 0 and g >= 2:
                    pe.wait_ge(s_prod, g - 1)
                pe.wait_ge(lo_done, q + 1)
                whi, wlo = split_tile(w_hi, q), split_tile(w_lo, q)
                for k in range(KT):
                    if g == 0:
                        pe.wait_ge(s_h, 8 + k + 1)
                    out = psum[4 + g % 2][:, o:o + S]
                    mm(out, whi[:, k, :], hg_hi[:, k, :], start=(k == 0), stop=False)
                    mm(out, whi[:, k, :], hg_lo[:, k, :], start=False, stop=False)
                    last = mm(out, wlo[:, k, :], hg_hi[:, k, :], start=False, stop=(k == KT - 1))
                last.then_inc(w_free, 1)

            def ffn_out(f):
                n = ffn_width(f) // P
                for j in range(n):
                    q = fpiece["w2", f, j]
                    pe.wait_ge(s_hidl, f * FPC + j + 1)
                    pe.wait_ge(lo_done, q + 1)
                    whi, wlo = split_tile(w_hi, q), split_tile(w_lo, q)
                    buf, o = f % 2, j % 2 * S
                    xhi, xlo = hid_hi[:, buf, j // 2, o:o + S], hid_lo[:, buf, j // 2, o:o + S]
                    end = f == NCH - 1 and j == n - 1
                    for m in range(KT):
                        out = psum[m // 2][:, (m % 2) * S:(m % 2 + 1) * S]
                        ms = slice(m * P, (m + 1) * P)
                        mm(out, whi[:, 0, ms], xhi, start=(f == 0 and j == 0 and m % 2 == 0), stop=False,
                           skip_group_check=True)
                        mm(out, whi[:, 0, ms], xlo, start=False, stop=False, skip_group_check=True)
                        last = mm(out, wlo[:, 0, ms], xhi, start=False, stop=end, skip_group_check=True)
                        if end and m in (1, 3, 5):
                            last.then_inc(s_y, 1)
                    last.then_inc(w_free, 1)

            for f in range(NCH):
                for j in range(ffn_width(f) // P):
                    hidden("w1", f, j)
                    hidden("w3", f, j)
                if f:
                    ffn_out(f - 1)
                    turn_third(*((0, 5) if f == 1 else (1, f - 2)))
            ffn_out(NCH - 1)

            norm_sums(2)
            pe.wait_ge(s_late, 64)
            for k in range(KT):
                pe.wait_ge(s_h, 16 + k + 1)
                last = mm(psum[4][0:GLA_RANK, 0:S], wa1[:, k, :], hT[:, k, :], start=(k == 0), stop=(k == KT - 1))
            last.then_inc(s_a1, 1)
            h2 = (hT, s_h, 16)
            project(("in1", 0), h2, False)
            turn_third(1, 4)
            pe.wait_ge(s_a1e, 1)
            for tt in range(TT):
                mm(psum[4 + tt][:, :], a1T[:, tt * P:(tt + 1) * P], wa2[:, :], start=True,
                   stop=True).then_inc(s_z, 1)
            project(("in1", 1), h2, False)
            pe.wait_ge(s_la, 1)
            for g in range(GH):
                for tt in range(TT):
                    o = (g % 2) * S + tt * P
                    last = mm(psum[4 + g // 2][:, o:o + P], la[:, tt, g * P:(g + 1) * P], tri[:],
                              start=True, stop=True)
            last.then_inc(s_b, 1)
            project(("in1", 2), h2, True)
            turn_third(1, 5)
            pe.wait_ge(s_qd, 3)
            for g in range(GH):
                for tt in range(TT):
                    n = g * TT + tt
                    last = nc.tensor.transpose(psum[4 + n // 4][:, (n % 4) * P:(n % 4 + 1) * P],
                                               kd[:, g, tt * P:(tt + 1) * P], ident[:])
            last.then_inc(s_kdt, 1)
            project(("in1", 3), h2, True)
            pe.wait_ge(s_kde, 1)
            for g in range(GH):
                for tt in range(TT):
                    n = g * TT + tt
                    last = mm(psum[4 + n // 4][:, (n % 4) * P:(n % 4 + 1) * P], ki[:, g, tt * P:(tt + 1) * P],
                              qd[:, g, tt * P:(tt + 1) * P], start=True, stop=True)
            last.then_inc(s_am, 1)

            def chunk_state(c):
                r0, tt = (c % 2) * CHUNK, c // 2
                if c:
                    pe.wait_ge(s_st, c)
                else:
                    pe.wait_ge(s_ame, 1)
                for g in range(GH):
                    last = mm(psum[4 + g // 2][:, (g % 2) * DV:(g % 2 + 1) * DV], kdt[r0:r0 + CHUNK, g * TT + tt, :],
                              V[r0:r0 + CHUNK, tt, g * DV:(g + 1) * DV], start=True, stop=True)
                last.then_inc(s_kv, 1)

            project(("in1", 4), h2, False)
            pe.wait_ge(s_evac, 24)
            chunk_state(0)
            half_project(("in1", 5), h2, False, 0)
            chunk_state(1)
            half_project(("in1", 5), h2, False, 1)
            chunk_state(2)

            def head_out_sums(g):
                pe.wait_ge(s_goe, g + 1)
                if g == 2:
                    pe.wait_ge(s_mod, 12)
                for v in range(2):
                    last = mm(psum[4 + g][:, 0:S], ones[:], rstd[:, 2 * g + v, :],
                              start=(v == 0), stop=(v == 1))
                last.then_inc(s_gss, 1)

            for g in range(GH):
                pe.wait_ge(s_evac, 25 + g)
                for v in range(2):
                    for tt in range(TT):
                        o = v * S + tt * P
                        mm(psum[g][:, o:o + P], V[:, tt, g * DV + v * P:g * DV + (v + 1) * P], am[:, g * TT + tt, :],
                           start=(v == 0 and tt == 0), stop=False, skip_group_check=True)
                if g == 0:
                    pe.wait_ge(s_st, NC - 1)
                for v in range(2):
                    for c in range(1, NC):
                        o = v * S + c * CHUNK
                        last = mm(psum[g][:, o:o + CHUNK], state[c - 1][:, g, v * P:(v + 1) * P],
                                  qd[:, g, c * CHUNK:(c + 1) * CHUNK], start=False, stop=True, skip_group_check=True)
                last.then_inc(s_go, 1)
                if g:
                    head_out_sums(g - 1)
            head_out_sums(GH - 1)
            project(("out1", 0), (oT, s_gn, 0), False)
            half_project(("out1", 1), (oT, s_gn, 0), False, 0)
            norm_sums(3, range(0, 2))
            half_project(("out1", 1), (oT, s_gn, 0), False, 1)
            norm_sums(3, range(2, KT))

            for tt in range(TT):
                for k in range(KT):
                    pe.wait_ge(s_h, 24 + k + 1)
                    last = mm(psum[4][:, tt * NE:(tt + 1) * NE], hT[:, k, tt * P:(tt + 1) * P], router[:, k, :],
                              start=(k == 0), stop=(k == KT - 1))
            last.then_inc(s_lg, 1)
            pe.wait_ge(s_evac, 32)

            def tokens_first(n, src):
                b = n % 4
                tt, half = divmod(b, 2)
                for k in range(4):
                    last = nc.tensor.transpose(psum[b][:, k * P:(k + 1) * P],
                                               src[:, half * 4 + k, tt * P:(tt + 1) * P], ident[:])
                last.then_inc(s_ht, 1)

            for n in range(4):
                tokens_first(n, hT)
            pe.wait_ge(s_dg, 1)
            for k in range(KT):
                last = mm(psum[5 + k // 4][:, (k % 4) * P:(k % 4 + 1) * P], ones[:], diag[:, k, :], start=True, stop=True)
            last.then_inc(s_g2, 1)
            pe.wait_ge(s_sel, 1)
            selT = rt[:, 0, :].rearrange("p (t e) -> p t e", t=TT)
            mm(psum[7][:, 0:NE], before[:], selT[:, 0, :], start=True, stop=True)
            mm(psum[7][:, NE:2 * NE], before[:], selT[:, 1, :], start=True, stop=False)
            mm(psum[7][:, NE:2 * NE], ones[:], selT[:, 0, :], start=False, stop=True)
            mm(psum[7][:, 2 * NE:3 * NE], ones[:], selT[:, 0, :], start=True, stop=False)
            mm(psum[7][:, 2 * NE:3 * NE], ones[:], selT[:, 1, :], start=False, stop=True).then_inc(s_pos, 1)
            for n in range(4, 8):
                pe.wait_ge(s_hte, n - 3)
                tokens_first(n, xT)
            pe.wait_ge(s_rt, 1)
            pe.wait_ge(s_hte, 8)
            pe.wait_ge(s_g2e, 2)

            def gather(e, nb):
                for g, bank in enumerate((0, 1, 6, 7)):
                    for k in range(2):
                        kk = 2 * g + k
                        for tt in range(TT):
                            last = mm(psum[bank][:, k * S:k * S + nb * P], h_tok[:, tt, kk * P:(kk + 1) * P],
                                      Pm[:, tt, 0:nb * P], start=(tt == 0), stop=(tt == TT - 1))
                    last.then_inc(s_gt, 1)

            def scatter(e, nb):
                pe.wait_ge(s_eye, e + 1)
                for n in range(4):
                    tt, half = divmod(n, 2)
                    for b in range(nb):
                        last = mm(psum[2 + n][:, :], PgT[:, b, tt * P:(tt + 1) * P],
                                  y_sb[:, b, half * 512:(half + 1) * 512], start=(b == 0), stop=(b == nb - 1))
                    last.then_inc(s_sct, 1)

            def gates_turned(e, nb):
                pe.wait_ge(s_gl, e * 4 + 4)
                for b in range(nb):
                    for tt in range(TT):
                        last = nc.tensor.transpose(psum[7][:, b * S + tt * P:b * S + (tt + 1) * P],
                                                   Pg[:, tt, b * P:(b + 1) * P], ident[:])
                last.then_inc(s_gg, 1)

            def expert(e, nb):
                for q in range(EQ):
                    i, p = divmod(q, PPC)
                    what, c = eorder[i]
                    pe.wait_ge(lo_done, e * EQ + FQ + q + 1)
                    if what == "w1":
                        if c == 0:
                            pe.wait_ge(s_gl, e * 4 + 4)
                        elif p == 0:
                            pe.wait_ge(s_esl, e * ECH + c)
                    elif what == "w3" and p == 0:
                        if c == 0:
                            pe.wait_ge(s_gge, e + 1)
                        else:
                            pe.wait_ge(s_hdl, e * ECH + c)
                    elif what == "w2" and p == 0:
                        if c == 0:
                            pe.wait_ge(s_scb, e * 4 + 4)
                        pe.wait_ge(s_hdl, e * ECH + c + 1)
                    whi, wlo = w_hi[:, q % PIECES, :], w_lo[:, q % PIECES, :]
                    for b in range(nb):
                        for j in range(SUB // 512):
                            if what == "w2":
                                xs = slice(p * P, (p + 1) * P)
                                xhi, xlo = hid_hi[:, c % 2, b, xs], hid_lo[:, c % 2, b, xs]
                                out = psum[2 + 2 * b + j]
                                first, end = c == 0 and p == 0, c == ECH - 1 and p == PPC - 1
                            else:
                                k = 2 * p + j
                                xhi, xlo = hg_hi[:, k, b * P:(b + 1) * P], hg_lo[:, k, b * P:(b + 1) * P]
                                out = psum[(0 if what == "w1" else 6) + b]
                                first, end = k == 0, k == KT - 1
                            cs = slice(j * 512, (j + 1) * 512)
                            mm(out[:, :], xhi, whi[:, cs], start=first, stop=False)
                            mm(out[:, :], xhi, wlo[:, cs], start=False, stop=False)
                            last = mm(out[:, :], xlo, whi[:, cs], start=False, stop=end)
                    last.then_inc(w_free, 1)
                    if q in turn_at:
                        c = turn_at[q]
                        pe.wait_ge(s_ea, e * ECH + c + 1)
                        for b in range(nb):
                            for j in range(FPC):
                                last = nc.tensor.transpose(psum[6 + b][:, j * P:(j + 1) * P],
                                                           hid_e[:, b, j * P:(j + 1) * P], ident[:])
                        last.then_inc(s_et, 1)

            with pe.Fori(0, NE) as e:
                pe.wait_ge(s_P, e * 4 + 4)
                nb = pe.value_load(nbk[0:1, bass.ds(e, 1)], min_val=1, max_val=2)
                nb_before = pe.value_load(nbp[0:1, bass.ds(e, 1)], min_val=1, max_val=2)
                for n in (1, 2):
                    with pe.If(nb == n):
                        gather(e, n)
                for n in (1, 2):
                    with pe.If(nb_before == n):
                        scatter(e, n)
                for n in (1, 2):
                    with pe.If(nb == n):
                        gates_turned(e, n)
                        expert(e, n)
            nb_last = pe.value_load(nbk[0:1, NE - 1:NE], min_val=1, max_val=2)
            for n in (1, 2):
                with pe.If(nb_last == n):
                    scatter(NE, n)

        @block.scalar
        def _(act):
            A = nc.scalar.activation
            n_link = [0]

            def link(ins):
                n_link[0] += 1
                ins.then_inc(s_achain, 1)
                act.wait_ge(s_achain, n_link[0])

            def rows(dst, r0, src, n):
                act.dma_start(dst[r0:r0 + n, :], src).then_inc(s_small, 16)

            rows(row_a, 0, t["c"].rearrange("o (k p) -> (o k) p", p=P), 8)
            rows(row_a, 8, t["norm1_g"].rearrange("l (k p) -> (l k) p", p=P), 16)
            rows(row_a, 24, t["norm2_g"].rearrange("l (k p) -> (l k) p", p=P), 16)
            rows(row_a, 40, t["ada_b"][0:1].rearrange("l (k p) -> (l k) p", p=P), 48)
            rows(row_b, 0, t["ada_b"][1:2].rearrange("l (k p) -> (l k) p", p=P), 48)

            act.wait_ge(s_par, 1)
            A(c_act[:], par[:, C0:C0 + KT], ACT.Silu).then_inc(s_cact, 1)
            act.wait_ge(s_lam, 1)
            A(lam[:, 2:4], lam[:, 0:2], ACT.Exp).then_inc(s_lame, 1)

            def squares(n):
                if n == 0:
                    act.wait_ge(s_constv, 1)
                for k in range(KT):
                    act.wait_ge(s_x, 8 * n + k + 1)
                    A(sq[:, k, :], xT[:, k, :], ACT.Square).then_inc(s_sq, 1)

            tiles_done = [0]

            def split_up_to(q_end):
                while tiles_done[0] <= min(q_end, FQ - 1):
                    q = tiles_done[0]
                    kind, f, j = fpieces[q]
                    wait_landed(act, index[kind, f])
                    act.wait_ge(w_free, q + 1)
                    A(split_tile(w_hi, q), raw_tile(q), ACT.Copy).then_inc(hi_done, 1)
                    tiles_done[0] += 1

            def shift(n):
                l, second = divmod(n, 2)
                c = 24 if second else 0
                act.wait_ge(s_mod, 6 * l + (4 if second else 1))
                for k in range(KT):
                    act.wait_ge(s_hp, 8 * n + k + 1)
                    if n == 1:
                        A(hg_hi[:, k, :], sq[:, k, :], ACT.Identity, bias=mod[:, l, c + k:c + k + 1]).then_inc(s_nr, 1)
                    else:
                        A(hT[:, k, :], hT[:, k, :], ACT.Identity, bias=mod[:, l, c + k:c + k + 1]).then_inc(s_h, 1)

            def evac(f, dst, func=ACT.Copy):
                act.wait_ge(s_fill, f + 1)
                A(dst, psum[f % 4][:, :], func).then_inc(s_evac, 1)

            def root(dst, src, kind):
                A(dst, src, ACT.Sqrt, bias=eps[:, kind:kind + 1]).then_inc(s_root, 1)

            def load_sqrt_table():
                link(A(small[:, 0, 14:15], eps[:, 0:1], ACT.Sqrt))

            def norm_root(n):
                act.wait_ge(s_ssq, n + 1)
                root(rstd[:, 0, :], psum[6][:, 0:S], 0)

            def qk_root(f):
                act.wait_ge(s_qss, f + 1)
                if f >= 2:
                    act.wait_ge(s_qn, f - 1)
                root(rstd[:, 2 * (f % 2) + 2:2 * (f % 2) + 4, :], psum[4 + f % 2][:, :], 1)

            for b in range(4):
                act.wait_ge(s_xt, b + 1)
                A(xT[:, 2 * b:2 * b + 2, :], psum[b][:, :], ACT.Copy).then_inc(s_x, 2)
            act.wait_ge(s_const, 1)
            squares(0)
            norm_root(0)
            shift(0)
            for f in range(8):
                act.wait_ge(s_fill, f + 1)
                if f < 4:
                    act.wait_ge(s_ssq, 1)
                else:
                    act.wait_ge(s_qss, f - 3)
                A(sq[:, 2 * (f % 4):2 * (f % 4) + 2, :], psum[f % 4][:, :], ACT.Square).then_inc(s_qsq, 1)
                evac(f, (bufA if f < 4 else bufB)[:, 2 * (f % 4):2 * (f % 4) + 2, :])
                if f % 2 == 1 and f >= 3:
                    qk_root(f - 3)
                    qk_root(f - 2)
            for f in range(8, 12):
                evac(f, V[:, f % 2, ((f - 8) // 2) * 512:((f - 8) // 2 + 1) * 512])
                if f == 9:
                    qk_root(6)
                    qk_root(7)

            def exponentials(h):
                a = att(h)
                act.wait_ge(s_mx, h + 1)
                nm = small[:, h % 2, :]
                for m in range(2):
                    A(a["t1"][:, m, :], a["t1"][:, m, :], ACT.Exp, bias=nm[:, m:m + 1], accum_out=nm[:, 4 + m:5 + m])
                    last = A(a["t0"][:, m, :], a["t0"][:, m, :], ACT.Exp, bias=nm[:, 2 + m:3 + m],
                             accum_out=nm[:, 6 + m:7 + m])
                last.then_inc(s_ex, 1)

            def head_rstd():
                for g in range(4):
                    act.wait_ge(s_oss, g + 1)
                    A(rstd[:, 2 * g:2 * g + 2, :], psum[SUB_BANKS[g]][:, :], ACT.Ln, bias=eps[:, 2:3]).then_inc(s_achain, 1)
                n_link[0] += 4
                act.wait_ge(s_achain, n_link[0])
                for g in range(4):
                    A(rstd[:, 2 * g:2 * g + 2, :], rstd[:, 2 * g:2 * g + 2, :], ACT.Exp, scale=-0.5).then_inc(s_root, 1)

            def head_out(h):
                act.wait_ge(s_o, h + 1)
                if h == 0:
                    act.wait_ge(s_qss, 8)
                A(sq[:, h, :], psum[5][:, 0:S], ACT.Square)
                A(oT[:, h, :], psum[5][:, 0:S], ACT.Copy).then_inc(s_oe, 1)

            exponentials(0)
            for h in range(H):
                if h + 1 < H:
                    exponentials(h + 1)
                act.wait_ge(s_pt, h + 1)
                A(att(h)["pt"], psum[4][:, 0:3 * P], ACT.Copy).then_inc(s_pte, 1)
                head_out(h)
            head_rstd()
            split_up_to(AHEAD)
            load_sqrt_table()
            squares(1)
            norm_root(1)
            shift(1)
            for q, (what, f, j) in enumerate(fpieces):
                split_up_to(q + AHEAD)
                if what == "w3":
                    g = f * FPC + j
                    act.wait_ge(w_free, PIECES + q + 1)
                    if g >= 4:
                        act.wait_ge(s_prod, g - 3)
                    A(silu_f[:, g % 4, :], psum[4 + g % 2][:, 0:S], ACT.Silu).then_inc(s_silu, 1)
                    act.wait_ge(s_prod, g + 1)
                    o = j % 2 * S
                    A(hid_hi[:, f % 2, j // 2, o:o + S], prod_f[:, g % 4, :], ACT.Copy).then_inc(s_hidh, 1)
            load_sqrt_table()
            squares(2)
            norm_root(2)
            shift(2)
            act.wait_ge(s_a1, 1)
            A(a1T, psum[4][0:GLA_RANK, 0:S], ACT.Copy).then_inc(s_a1e, 1)
            for f in (16, 17):
                evac(f, bufA[:, 2 * (f - 16):2 * (f - 16) + 2, :])
            act.wait_ge(s_zb, 2)
            link(A(le, le, ACT.Exp, scale=-1.0))
            A(le, le, ACT.Ln, bias=ones[:, 0:1]).then_inc(s_ln, 1)
            for f in (18, 19):
                evac(f, bufA[:, 2 * (f - 16):2 * (f - 16) + 2, :])
            act.wait_ge(s_b, 1)
            for g in range(2):
                A(bT[:, 2 * g:2 * g + 2, :], psum[4 + g][:, :], ACT.Copy)
                A(eb[:, 2 * g:2 * g + 2, :], psum[4 + g][:, :], ACT.Exp)
                A(ei[:, 2 * g:2 * g + 2, :], psum[4 + g][:, :], ACT.Exp, scale=-1.0).then_inc(s_be, 1)
            act.wait_ge(s_dd, 1)
            A(dd[:, :, :], dd[:, :, :], ACT.Exp).then_inc(s_ed, 1)
            for f in (20, 21):
                evac(f, V[:, f % 2, 0:512])
            act.wait_ge(s_kdt, 1)
            A(kdt[:, 0:4, :], psum[4][:, :], ACT.Copy)
            A(kdt[:, 4:8, :], psum[5][:, :], ACT.Copy).then_inc(s_kde, 1)
            for f in (22, 23):
                evac(f, V[:, f % 2, 512:1024])
            for f in range(24, 28):
                evac(f, bufB[:, 2 * (f - 24):2 * (f - 24) + 2, :], ACT.Silu)
            act.wait_ge(s_qd, 3)
            act.wait_ge(s_st, NC - 1)

            def head_out_root(g):
                act.wait_ge(s_gss, g + 1)
                root(bufA[:, g, :], psum[4 + g][:, 0:S], 3)

            for g in range(GH):
                act.wait_ge(s_go, g + 1)
                A(rstd[:, 2 * g:2 * g + 2, :], psum[g][:, :], ACT.Square)
                A(oT[:, 2 * g:2 * g + 2, :], psum[g][:, :], ACT.Copy).then_inc(s_goe, 1)
                if g:
                    head_out_root(g - 1)
            head_out_root(GH - 1)
            act.wait_ge(s_gn, 8)
            squares(3)
            norm_root(3)
            shift(3)
            for n in range(8):
                if n == 4:
                    act.wait_ge(s_lgm, 1)
                    A(rt[:, 4, :], rt[:, 3, :], ACT.Exp).then_inc(s_rexp, 1)
                    act.wait_ge(s_g2, 1)
                    for g in range(2):
                        A(g2bc[:, g * 512:(g + 1) * 512], psum[5 + g][:, :], ACT.Copy).then_inc(s_g2e, 1)
                act.wait_ge(s_ht, n + 1)
                dst = h_tok if n < 4 else x_acc
                tt, half = divmod(n % 4, 2)
                A(dst[:, tt, half * 512:(half + 1) * 512], psum[n % 4][:, :], ACT.Copy).then_inc(s_hte, 1)
            act.wait_ge(s_rt, 1)

            def copy_scattered(e, n):
                act.wait_ge(s_sct, e * 4 + n + 1)
                act.wait_ge(s_add, e * 4 + n + 1)
                A(scattered[:, n % 2, :], psum[2 + n][:, :], ACT.Copy).then_inc(s_scb, 1)

            def expert(e, nb):
                done = [0]

                def split_up_to(q_end):
                    while done[0] <= min(q_end, EQ - 1):
                        q = done[0]
                        if q % PPC == 0:
                            wait_landed(act, PRE + q // PPC, e)
                        act.wait_ge(w_free, e * EQ + FQ + q + 1)
                        A(w_hi[:, q % PIECES, :], raw_piece(q), ACT.Copy).then_inc(hi_done, 1)
                        done[0] += 1

                for g, bank in enumerate((0, 1, 6, 7)):
                    split_up_to(g if g < AHEAD else AHEAD)
                    act.wait_ge(s_gt, e * 4 + g + 1)
                    A(hg_hi[:, 2 * g:2 * g + 2, 0:nb * P],
                      psum[bank][:, :].rearrange("p (k s) -> p k s", k=2)[:, :, 0:nb * P], ACT.Copy).then_inc(s_gh, 1)
                for q in range(EQ):
                    if q in (2, 5, 8, 11):
                        copy_scattered(e, (q - 2) // 3)
                    split_up_to(q + AHEAD)
                    i, p = divmod(q, PPC)
                    what, c = eorder[i]
                    if q == 0:
                        act.wait_ge(s_gg, e + 1)
                        A(PgT[:, 0:nb, :], psum[7][:, 0:nb * S].rearrange("p (b s) -> p b s", b=nb),
                          ACT.Copy).then_inc(s_gge, 1)
                    if what == "w3" and p == 0:
                        act.wait_ge(w_free, e * EQ + FQ + PIECES + q)
                        if c:
                            act.wait_ge(s_ea, e * ECH + c)
                        for b in range(nb):
                            last = A(silu_e[:, b, :], psum[b][:, :], ACT.Silu)
                        last.then_inc(s_esl, 1)
                    if q - 1 in turn_at:
                        c = turn_at[q - 1]
                        act.wait_ge(s_et, e * ECH + c + 1)
                        for b in range(nb):
                            last = A(hid_hi[:, c % 2, b, :], psum[6 + b][:, :], ACT.Copy)
                        last.then_inc(s_hdh, 1)

            with act.Fori(0, NE) as e:
                A(small[:, 1, 15:16], ones[:, 0:1], ACT.Silu).then_inc(s_table, 1)
                act.wait_ge(s_table, e + 1)
                nb = act.value_load(nbk[0:1, bass.ds(e, 1)], min_val=1, max_val=2)
                for n in (1, 2):
                    with act.If(nb == n):
                        expert(e, n)
        @block.vector
        def _(dve):
            v = nc.vector
            n_link = [0]

            def link(ins):
                n_link[0] += 1
                ins.then_inc(s_chain, 1)
                dve.wait_ge(s_chain, n_link[0])

            dve.wait_ge(s_tp, 1)
            v.tensor_copy(par[:, 0:88], psum[7][:, 0:88])
            v.tensor_copy(par[:, 136:141], psum[7][:, 88:93])
            link(v.tensor_copy(par[:, 88:136], psum[7][:, 128:176]))
            v.tensor_scalar(gq[:, 0:1], par[:, QG:QG + 1], 1.0, None, ALU.mult)
            v.tensor_scalar(gq[:, 1:2], par[:, QG + 1:QG + 2], math.sqrt(DH), None, ALU.mult)
            v.tensor_scalar(gq[:, 2:3], par[:, QG + 2:QG + 3], (1.0 - LAMBDA_INIT) * math.sqrt(P), None, ALU.mult)
            link(v.tensor_scalar(gq[:, 3:5], par[:, QG + 3:QG + 5], math.sqrt(DV), None, ALU.mult))
            v.memset(rt[:, 8, :], 0.0).then_inc(s_par, 1)
            dve.wait_ge(s_const, 1)
            v.tensor_copy(slot_no[:], slot_i)
            link(v.tensor_copy(dist[:], dist_i))
            link(v.tensor_scalar(tri[:], tri[:], 1.0 / GLA_TAU, None, ALU.mult))
            link(v.scalar_tensor_tensor(dist[:], dist[:], -1.0, dist[:], ALU.mult, ALU.min))
            link(v.memset(dist[0:64, 192:256], HIDDEN))
            dve.wait_ge(s_small, 16 * 14)
            v.tensor_tensor(lam_pr[:, 0, :], lam_in[:, 0, :], lam_in[:, 1, :], ALU.mult)
            link(v.tensor_tensor(lam_pr[:, 1, :], lam_in[:, 2, :], lam_in[:, 3, :], ALU.mult))
            v.tensor_reduce(lam[:, 0:2], lam_pr, AX_X, ALU.add).then_inc(s_lam, 1)
            dve.wait_ge(s_lam, 1)
            dve.sem_inc(s_constv, 1)
            dve.wait_ge(s_lame, 1)
            link(v.tensor_tensor(lam[:, 0:1], lam[:, 3:4], lam[:, 2:3], ALU.subtract))
            link(v.tensor_scalar(lam[:, 0:1], lam[:, 0:1], -LAMBDA_INIT, None, ALU.add))

            dve.wait_ge(s_cact, 1)

            ada_order = [key for key in order if key[0].startswith("ada")]
            ada_done = [0]

            def ada_steps(count):
                for _ in range(count):
                    chunk, k = divmod(ada_done[0], KT)
                    key = ada_order[chunk]
                    n = chunk // 2
                    w = slot_view(index[key], KT, FW)
                    acc = ada_acc[:, n % 2, (chunk % 2) * FW:(chunk % 2 + 1) * FW]
                    if k == 0:
                        wait_landed(dve, index[key])
                        if n >= 2:
                            dve.wait_ge(s_modp, n - 1)
                        v.tensor_scalar(acc, w[:, 0, :], c_act[:, 0:1], None, ALU.mult).then_inc(s_ada, 1)
                    else:
                        dve.wait_ge(s_ada, chunk * (KT - 1) + k)
                        step = v.scalar_tensor_tensor(acc, w[:, k, :], c_act[:, k:k + 1], acc, ALU.mult, ALU.add)
                        if k == KT - 1:
                            step.then_inc(ada_used, 1)
                        else:
                            step.then_inc(s_ada, 1)
                    ada_done[0] += 1

            def mod_third(l, third):
                dve.wait_ge(s_modp, 6 * l + third + 1)
                m = mod[:, l, 8 * third:8 * third + 8]
                for half in range(2):
                    last = v.tensor_reduce(m[:, 4 * half:4 * half + 4],
                                           psum[6 + half][:, :].rearrange("p (j c) -> p j c", j=4), AX_X, ALU.add)
                link(last)
                v.tensor_tensor(m, m, par[:, AB + 48 * l + 8 * third:AB + 48 * l + 8 * third + 8],
                                ALU.add).then_inc(s_mod, 1)

            def gains(n):
                l, second = divmod(n, 2)
                dve.wait_ge(s_mod, 6 * l + (5 if second else 2))
                c = 32 if second else 8
                g = (N2 if second else N1) + 8 * l
                link(v.scalar_tensor_tensor(cols[:, n, :], mod[:, l, c:c + 8], 1.0, par[:, g:g + 8], ALU.add, ALU.mult))
                link(v.tensor_scalar(cols[:, n, :], cols[:, n, :], math.sqrt(D), None, ALU.mult))

            def invert_root(n):
                dve.wait_ge(s_root, ROOT[f"norm{n}"] + 1)
                link(v.reciprocal(rstd[:, 0, :], rstd[:, 0, :]))

            def normalise(n):
                r = rstd[:, 0, :]
                if n == 3:
                    dve.wait_ge(s_fill, 8 * (n + 1))
                if n == 2:
                    dve.wait_ge(w_free, PIECES + FQ)
                for k in range(KT):
                    v.scalar_tensor_tensor((sq if n == 1 else hT)[:, k, :], xT[:, k, :], cols[:, n, k:k + 1], r, ALU.mult,
                                           ALU.mult).then_inc(s_hp, 1)

            ada_steps(2 * KT)
            invert_root(0)
            ada_steps(KT)
            mod_third(0, 0)
            ada_steps(KT)
            mod_third(0, 1)
            gains(0)
            normalise(0)
            ada_steps(2 * KT)
            for f in range(8):
                dve.wait_ge(s_root, ROOT["qk"] + f + 1)
                dve.wait_ge(s_evac, f + 1)
                dst = (bufA if f < 4 else bufB)[:, 2 * (f % 4):2 * (f % 4) + 2, :]
                r = rstd[:, 2 * (f % 2) + 2:2 * (f % 2) + 4, :]
                link(v.reciprocal(r, r))
                v.scalar_tensor_tensor(dst, dst, gq[:, f // 4:f // 4 + 1], r, ALU.mult, ALU.mult).then_inc(s_qn, 1)
                if f == 3:
                    mod_third(0, 2)
                if f == 7:
                    mod_third(0, 3)
                if f % 2 == 1:
                    ada_steps(KT)

            def biased(h):
                a = att(h)
                slope = 2.0 ** (-8.0 * (h + 1) / H)
                nm = small[:, h % 2, :]
                dve.wait_ge(s_sc, h + 1)
                if h >= 2:
                    dve.wait_ge(s_pd, h - 1)
                for m in range(2):
                    v.scalar_tensor_tensor(a["t1"][:, m, :], dist[:, :], slope,
                                           psum[2 * (h % 2) + m][:, 0:S], ALU.mult, ALU.add)
                    last = v.scalar_tensor_tensor(a["t0"][:, m, :], dist[:, P:S], slope,
                                                  psum[2 * (h % 2) + m][:, S:S + P], ALU.mult, ALU.add)
                link(last)
                v.tensor_reduce(nm[:, 0:2], a["t1"], AX_X, ALU.max, negate=True)
                v.tensor_reduce(nm[:, 2:4], a["t0"], AX_X, ALU.max, negate=True).then_inc(s_mx, 1)

            def differ(h):
                a = att(h)
                nm = small[:, h % 2, :]
                dve.wait_ge(s_ex, h + 1)
                if h >= 2:
                    dve.wait_ge(s_pt, h - 1)
                link(v.reciprocal(nm[:, 8:12], nm[:, 4:8]))
                v.tensor_scalar(nm[:, 12:13], nm[:, 9:10], lam[:, 0:1], None, ALU.mult)
                v.tensor_scalar(nm[:, 13:14], nm[:, 11:12], lam[:, 0:1], None, ALU.mult)
                v.tensor_scalar(a["d1"], a["t1"][:, 0, :], nm[:, 8:9], None, ALU.mult)
                link(v.tensor_scalar(a["d0"], a["t0"][:, 0, :], nm[:, 10:11], None, ALU.mult))
                link(v.scalar_tensor_tensor(a["d1"], a["t1"][:, 1, :], nm[:, 12:13], a["d1"], ALU.mult, ALU.add))
                v.scalar_tensor_tensor(a["d0"], a["t0"][:, 1, :], nm[:, 13:14], a["d0"], ALU.mult,
                                       ALU.add).then_inc(s_pd, 1)

            def head_norm(g):
                dve.wait_ge(s_root, ROOT["sub"] + g + 1)
                r = rstd[:, 2 * g:2 * g + 2, :]
                v.scalar_tensor_tensor(oT[:, 2 * g:2 * g + 2, :], oT[:, 2 * g:2 * g + 2, :], gq[:, 2:3], r,
                                       ALU.mult, ALU.mult).then_inc(s_on, 2)

            biased(0)
            biased(1)
            for h in range(H):
                differ(h)
                if h + 2 < H:
                    biased(h + 2)
                if h == 0:
                    mod_third(0, 4)
            for g in range(4):
                head_norm(g)

            tiles_done = [0]

            def split_up_to(q_end):
                while tiles_done[0] <= min(q_end, FQ - 1):
                    q = tiles_done[0]
                    dve.wait_ge(hi_done, q + 1)
                    v.tensor_tensor(split_tile(w_lo, q), raw_tile(q), split_tile(w_hi, q).bitcast(F32),
                                    ALU.subtract).then_inc(lo_done, 1)
                    tiles_done[0] += 1

            split_up_to(AHEAD)

            def residual(l, f0):
                dve.wait_ge(s_mod, 6 * l + 3)
                for g in range(4):
                    f = f0 + g
                    dve.wait_ge(s_fill, f + 1)
                    for j in range(2):
                        m = 2 * g + j
                        last = v.scalar_tensor_tensor(xT[:, m, :], psum[f % 4][:, j * S:(j + 1) * S],
                                                      mod[:, l, 16 + m:17 + m], xT[:, m, :], ALU.mult, ALU.add)
                        if j == 0:
                            last.then_inc(s_x, 1)
                    last.then_inc(s_evac, 1)
                    dve.wait_ge(s_evac, f + 1)
                    dve.sem_inc(s_x, 1)

            residual(0, 12)
            gains(1)
            invert_root(1)
            normalise(1)
            for k in range(KT):
                dve.wait_ge(s_nr, k + 1)
                v.scalar_tensor_tensor(hg_lo[:, k, :], sq[:, k, :], mod[:, 0, 24 + k:25 + k],
                                       hg_hi[:, k, :].bitcast(F32), ALU.add, ALU.subtract).then_inc(s_h, 1)
            for q, (what, f, j) in enumerate(fpieces):
                split_up_to(q + AHEAD)
                if what == "w3":
                    g = f * FPC + j
                    o = j % 2 * S
                    dve.wait_ge(s_silu, g + 1)
                    v.tensor_tensor(prod_f[:, g % 4, :], silu_f[:, g % 4, :], psum[4 + g % 2][:, S:2 * S],
                                    ALU.mult).then_inc(s_prod, 1)
                    ada_steps(4 if f == 0 else 2)
                    dve.wait_ge(s_hidh, g + 1)
                    v.tensor_tensor(hid_lo[:, f % 2, j // 2, o:o + S], prod_f[:, g % 4, :],
                                    hid_hi[:, f % 2, j // 2, o:o + S].bitcast(F32), ALU.subtract).then_inc(s_hidl, 1)
                if what == "w2" and f < NCH - 1:
                    ada_steps(3 if f == NCH - 2 else 2)
                if what == "w2" and (what, f, j + 1) not in fpiece and f < NCH - 1:
                    mod_third(*((0, 5) if f == 0 else (1, f - 1)))
            for m in range(KT):
                if m < 6:
                    dve.wait_ge(s_y, m // 2 + 1)
                else:
                    dve.wait_ge(w_free, PIECES + FQ)
                v.scalar_tensor_tensor(xT[:, m, :], psum[m // 2][:, (m % 2) * S:(m % 2 + 1) * S],
                                       mod[:, 0, 40 + m:41 + m], xT[:, m, :], ALU.mult, ALU.add).then_inc(s_x, 1)
            gains(2)
            invert_root(2)
            normalise(2)
            mod_third(1, 4)
            ada_steps(KT)

            dve.wait_ge(s_late, 64)
            for tt in range(TT):
                dve.wait_ge(s_z, tt + 1)
                link(v.tensor_tensor(lz[:, tt, :], psum[4 + tt][:, :], ba_row[:, :], ALU.add))
                v.scalar_tensor_tensor(le[:, tt, :], lz[:, tt, :], -1.0, lz[:, tt, :], ALU.mult, ALU.max).then_inc(s_zb, 1)
            dve.wait_ge(s_ln, 1)
            v.scalar_tensor_tensor(la, lz, 0.0, le, ALU.min, ALU.subtract).then_inc(s_la, 1)
            ada_steps(KT)
            dve.wait_ge(s_be, 2)
            b16 = bT.rearrange("p g (c s) -> p (g c) s", c=NC)
            d16 = dd.rearrange("p g (c s) -> p (g c) s", c=NC)
            v.tensor_tensor(d16, b16[:, :, CHUNK - 1:CHUNK].to_broadcast([P, GH * NC, CHUNK]), b16,
                            ALU.subtract).then_inc(s_dd, 1)
            dve.wait_ge(s_evac, 20)
            v.scalar_tensor_tensor(qd, gq_t, float(P) ** -0.5, eb, ALU.mult, ALU.mult).then_inc(s_qd, 1)
            v.tensor_tensor(ki, gk_t, ei, ALU.mult).then_inc(s_qd, 1)
            dve.wait_ge(s_ed, 1)
            v.tensor_tensor(kd, gk_t, dd[:, :, :], ALU.mult).then_inc(s_qd, 1)
            mod_third(1, 5)
            dve.wait_ge(s_la, 1)
            link(v.memset(am[:, :, :], 0.0))
            dve.wait_ge(s_am, 1)
            for g in range(2):
                last = v.copy_predicated(am[:, 4 * g:4 * g + 4, :],
                                         tri[:, :].bitcast(I32).rearrange("p (o c) -> p o c", o=1).to_broadcast([P, 4, P]),
                                         psum[4 + g][:, :].rearrange("p (o c) -> p o c", o=4))
            last.then_inc(s_ame, 1)
            for c in range(NC - 1):
                dve.wait_ge(s_kv, c + 1)
                for g in range(GH):
                    kv = psum[4 + g // 2][:, (g % 2) * DV:(g % 2 + 1) * DV]
                    if c == 0:
                        last = v.tensor_copy(state[0][:, g, :], kv)
                    else:
                        last = v.scalar_tensor_tensor(state[c][:, g, :], state[c - 1][:, g, :],
                                                      eb[:, g, (c + 1) * CHUNK - 1:(c + 1) * CHUNK], kv,
                                                      ALU.mult, ALU.add)
                last.then_inc(s_st, 1)
                dve.wait_ge(s_st, c + 1)
            dve.wait_ge(s_evac, 28)
            for g in range(GH):
                dve.wait_ge(s_goe, g + 1)
                for w in range(2):
                    o = oT[:, 2 * g + w, :]
                    last = v.scalar_tensor_tensor(o, o, gq[:, 3 + w:4 + w], bufB[:, 2 * g + w, :], ALU.mult, ALU.mult)
                r = bufA[:, g:g + 1, :]
                dve.wait_ge(s_root, ROOT["gla"] + g + 1)
                n_link[0] += 2
                last.then_inc(s_chain, 1)
                v.reciprocal(r, r).then_inc(s_chain, 1)
                dve.wait_ge(s_chain, n_link[0])
                o = oT[:, 2 * g:2 * g + 2, :]
                v.tensor_tensor(o, o, r.to_broadcast([P, 2, S]), ALU.mult).then_inc(s_gn, 2)
            residual(1, 28)
            gains(3)
            invert_root(3)
            normalise(3)

            for k in range(KT):
                last = v.tensor_scalar(diag[:, k, :], ident[:], mod[:, 1, 40 + k:41 + k], None, ALU.mult)
            last.then_inc(s_dg, 1)
            r3 = [rt[:, j, :].rearrange("p (t e) -> p t e", t=TT) for j in range(9)]
            sel, tmp, ex, lg = r3[0], r3[3], r3[4], r3[5]
            link(v.memset(gate[:, :, :], 0.0))
            link(v.memset(posx[:, :, :], -1.0))
            mx = rt[:, 6, :]
            dve.wait_ge(s_lg, 1)
            link(v.tensor_copy(lg, psum[4][:, 0:TT * NE].rearrange("p (t e) -> p t e", t=TT)))
            for tt in range(TT):
                mine = rt[:, 5, tt * NE:(tt + 1) * NE].rearrange("p (e o) -> p e o", o=1).to_broadcast([P, NE, NE])
                other = rt[:, 5, tt * NE:(tt + 1) * NE].rearrange("p (o e) -> p o e", o=1).to_broadcast([P, NE, NE])
                link(v.tensor_tensor(cmp_a[:, tt], other, mine, ALU.is_gt))
                link(v.tensor_tensor(cmp_b[:, tt], other, mine, ALU.is_equal))
                link(v.tensor_tensor(cmp_b[:, tt], cmp_b[:, tt], lower_e[:, :, :], ALU.mult))
                link(v.tensor_tensor(cmp_a[:, tt], cmp_a[:, tt], cmp_b[:, tt], ALU.add))
                link(v.tensor_reduce(tmp[:, tt, :], cmp_a[:, tt], AX_X, ALU.add))
                link(v.tensor_reduce(mx[:, tt:tt + 1], lg[:, tt, :], AX_X, ALU.max, negate=True))
            link(v.tensor_scalar(sel, tmp, 1.5, None, ALU.is_lt))
            dve.sem_inc(s_sel, 1)
            for tt in range(TT):
                link(v.tensor_scalar(tmp[:, tt, :], lg[:, tt, :], mx[:, tt:tt + 1], None, ALU.add))
            dve.sem_inc(s_lgm, 1)
            dve.wait_ge(s_rexp, 1)
            link(v.tensor_tensor(ex, ex, sel, ALU.mult))
            link(v.tensor_reduce(mx[:, 2:4], ex, AX_X, ALU.add))
            link(v.reciprocal(mx[:, 4:6], mx[:, 2:4]))
            for tt in range(TT):
                link(v.tensor_scalar(gate[:, tt, 0:NE], ex[:, tt, :], mx[:, 4 + tt:5 + tt], None, ALU.mult))
            dve.wait_ge(s_pos, 1)
            pos = psum[7][:, 0:TT * NE].rearrange("p (t e) -> p t e", t=TT)
            link(v.scalar_tensor_tensor(tmp, pos, 1.0, sel, ALU.add, ALU.mult))
            link(v.tensor_scalar(posx[:, :, 0:NE], tmp, -1.0, None, ALU.add))
            link(v.tensor_scalar(rt[:, 7, 0:NE], psum[7][:, 2 * NE:3 * NE], P + 0.5, 1.0, ALU.is_gt, ALU.add))
            link(v.tensor_copy(nbk[:, :], rt[:, 7, 0:NE]))
            link(v.memset(rt[:, 7, 0:1], 1.0))
            link(v.tensor_copy(nbp[:, 0:1], rt[:, 7, 0:1]))
            link(v.tensor_copy(nbp[:, 1:NE], nbk[:, 0:NE - 1]))
            dve.wait_ge(s_g2, 1)
            dve.sem_inc(s_rt, 1)

            def dispatch(e, n):
                tt = n // 2
                if n % 2 == 0:
                    v.tensor_scalar(Pm[:, tt, :], slot_no[:], posx[:, tt, bass.ds(e, 1)], None,
                                    ALU.is_equal).then_inc(s_P, 1)
                else:
                    v.tensor_scalar(Pg[:, tt, :], slot_no[:], posx[:, tt, bass.ds(e, 1)],
                                    gate[:, tt, bass.ds(e, 1)], ALU.is_equal, ALU.mult).then_inc(s_P, 1)

            def expert(e, nb):
                done = [0]

                def split_up_to(q_end):
                    while done[0] <= min(q_end, EQ - 1):
                        q = done[0]
                        dve.wait_ge(hi_done, e * EQ + FQ + q + 1)
                        v.tensor_tensor(w_lo[:, q % PIECES, :], raw_piece(q), w_hi[:, q % PIECES, :].bitcast(F32),
                                        ALU.subtract).then_inc(lo_done, 1)
                        done[0] += 1

                for g, bank in enumerate((0, 1, 6, 7)):
                    split_up_to(g if g < AHEAD else AHEAD)
                    dve.wait_ge(s_gh, e * 4 + g + 1)
                    v.tensor_tensor(hg_lo[:, 2 * g:2 * g + 2, 0:nb * P],
                                    psum[bank][:, :].rearrange("p (k s) -> p k s", k=2)[:, :, 0:nb * P],
                                    hg_hi[:, 2 * g:2 * g + 2, 0:nb * P].bitcast(F32), ALU.subtract).then_inc(s_gl, 1)
                for q in range(EQ):
                    split_up_to(q + AHEAD)
                    i, p = divmod(q, PPC)
                    what, c = eorder[i]
                    if what == "w3" and p == PPC - 1:
                        dve.wait_ge(s_esl, e * ECH + c + 1)
                        dve.wait_ge(w_free, e * EQ + FQ + PIECES + q + 1)
                        if c:
                            dve.wait_ge(s_et, e * ECH + c)
                        for b in range(nb):
                            last = v.tensor_tensor(hid_e[:, b, :], silu_e[:, b, :], psum[6 + b][:, :], ALU.mult)
                        last.then_inc(s_ea, 1)
                    if q - 1 in turn_at:
                        c = turn_at[q - 1]
                        dve.wait_ge(s_hdh, e * ECH + c + 1)
                        for b in range(nb):
                            last = v.tensor_tensor(hid_lo[:, c % 2, b, :], psum[6 + b][:, :],
                                                   hid_hi[:, c % 2, b, :].bitcast(F32), ALU.subtract)
                        last.then_inc(s_hdl, 1)
                    if q >= EQ - 4 * PPC and p == 0:
                        n = q // PPC - (PER - 4)
                        if n == 0:
                            dve.wait_ge(s_gge, e + 1)
                        dispatch(e + 1, n)
                dve.wait_ge(w_free, (e + 1) * EQ + FQ + PIECES)
                for b in range(nb):
                    for half in range(2):
                        last = v.tensor_tensor(y_sb[:, b, half * 512:(half + 1) * 512], psum[2 + 2 * b + half][:, :],
                                               g2bc[:, half * 512:(half + 1) * 512], ALU.mult)
                last.then_inc(s_eye, 1)

            for n in range(4):
                dispatch(0, n)
            link(v.memset(PgT[:, 0, :], 0.0))
            dve.wait_ge(s_ht, 8)
            v.memset(y_sb[:, 0, :], 0.0).then_inc(s_eye, 1)
            with dve.Fori(0, NE) as e:
                nb = dve.value_load(nbk[0:1, bass.ds(e, 1)], min_val=1, max_val=2)
                for n in (1, 2):
                    with dve.If(nb == n):
                        expert(e, n)
            dve.wait_ge(s_add, NE * 4 + 2)
            for n in range(4):
                tt, half = divmod(n, 2)
                dve.wait_ge(s_sct, NE * 4 + n + 1)
                dst = x_acc[:, tt, half * 512:(half + 1) * 512]
                v.tensor_tensor(dst, dst, psum[2 + n][:, :], ALU.add).then_inc(s_fin, 1)

INPUTS = ["x", "c", "ada_w", "ada_b", "norm1_g", "norm2_g", "da_w_in", "da_q_gain", "da_k_gain", "da_lam_q1",
          "da_lam_k1", "da_lam_q2", "da_lam_k2", "da_subln_g", "da_w_out", "gla_w_in", "gla_w_a1", "gla_w_a2",
          "gla_b_a", "gla_out_g", "gla_w_out", "ffn_w1", "ffn_w3", "ffn_w2", "moe_router", "moe_w1", "moe_w3",
          "moe_w2"]


def kernel(**inputs):
    import numpy as np
    import concourse.bacc as bacc
    from concourse.bass_utils import run_bass_kernel_spmd

    nc = bacc.Bacc("TRN2", target_bir_lowering=False, num_devices=1, dynamic_dma_scratch_size=1024)
    arrays, t = {}, {}
    for name in INPUTS:
        a = np.ascontiguousarray(inputs[name])
        if name in ("moe_w1", "moe_w3", "moe_w2"):
            a = a[0]
        arrays[f"in_{name}"] = a
        t[name] = nc.dram_tensor(f"in_{name}", a.shape, mybir.dt.from_np(a.dtype), kind="ExternalInput").ap()
    t["out"] = nc.dram_tensor("out_x", (1, S, D), F32, kind="ExternalOutput").ap()
    build(nc, t)
    r = run_bass_kernel_spmd(nc, [arrays], core_ids=[0])
    return r.results[0]["out_x"]
```
